# Optimizing a Trainium2 kernel written in Bass

```python
import jax, jax.numpy as jnp
from jax import lax
import numpy as np

D_MODEL = 1024
BATCH = 1
SEQ = 1024
DEPTH = 2

GRID_W = 64
CTX_LEN = 256
D_MIX = 1024
HEAD_DIM = 64
EPS = 1e-6
A_GROUPS = 4
A_WIDTH = A_GROUPS * HEAD_DIM
CHUNK = 128
B_HEADS = 8
B_KV_HEADS = 2
B_GROUP = B_HEADS // B_KV_HEADS
B_WIDTH = B_HEADS * HEAD_DIM
B_KV_WIDTH = B_KV_HEADS * HEAD_DIM
Q_BLOCK = 128
ATTN_SCALE = HEAD_DIM ** -0.5
ROPE_THETA = 10000.0
HALF_ROT = HEAD_DIM // 2
ROPE_FREQS = HALF_ROT // 2
C_HEADS = 4
C_WIDTH = C_HEADS * HEAD_DIM
M_CHUNK = 128
F_BIAS_LO = 3.0
F_BIAS_HI = 6.0
SPLIT_SIZES = (A_WIDTH, A_WIDTH, A_WIDTH,
               B_WIDTH, B_KV_WIDTH, B_KV_WIDTH, B_WIDTH,
               C_WIDTH, C_WIDTH, C_WIDTH, C_WIDTH, C_WIDTH, 4 * C_HEADS)
D_IN = 3 * A_WIDTH + 2 * B_WIDTH + 2 * B_KV_WIDTH + 5 * C_WIDTH + 4 * C_HEADS


def _rms_norm(x, g):
    xf = x.astype(jnp.float32)
    y = xf * lax.rsqrt(jnp.mean(xf * xf, axis=-1, keepdims=True) + EPS)
    return (y * g.astype(jnp.float32)).astype(x.dtype)

def _layer_norm(x):
    xf = x.astype(jnp.float32)
    mu = jnp.mean(xf, axis=-1, keepdims=True)
    var = jnp.mean(jnp.square(xf - mu), axis=-1, keepdims=True)
    return ((xf - mu) * lax.rsqrt(var + EPS)).astype(x.dtype)

def _split_proj(p):
    idx = [int(i) for i in np.cumsum(SPLIT_SIZES)[:-1]]
    return jnp.split(p, idx, axis=-1)

def _rope_tables(rows_n):
    row = jnp.repeat(jnp.arange(rows_n, dtype=jnp.int32), GRID_W)
    col = jnp.tile(jnp.arange(GRID_W, dtype=jnp.int32), rows_n)
    freqs = ROPE_THETA ** (-jnp.arange(ROPE_FREQS, dtype=jnp.float32) / ROPE_FREQS)
    ang_r = row.astype(jnp.float32)[:, None] * freqs
    ang_c = col.astype(jnp.float32)[:, None] * freqs
    return (jnp.cos(ang_r), jnp.sin(ang_r), jnp.cos(ang_c), jnp.sin(ang_c))

def _apply_rope(x, tabs):
    cos_r, sin_r, cos_c, sin_c = tabs
    shp = (1, x.shape[1]) + (1,) * (x.ndim - 3) + (ROPE_FREQS,)
    xf = x.astype(jnp.float32)

    def rot(xh, cos, sin):
        cos = cos.reshape(shp)
        sin = sin.reshape(shp)
        x1, x2 = xh[..., :ROPE_FREQS], xh[..., ROPE_FREQS:]
        return jnp.concatenate([x1 * cos - x2 * sin, x2 * cos + x1 * sin], axis=-1)

    out = jnp.concatenate([rot(xf[..., :HALF_ROT], cos_r, sin_r),
                           rot(xf[..., HALF_ROT:], cos_c, sin_c)], axis=-1)
    return out.astype(x.dtype)

def _attend(q, k, v):
    s = jnp.einsum('bqkgd,bskd->bkgqs', q, k).astype(jnp.float32) * ATTN_SCALE
    p = jax.nn.softmax(s, axis=-1).astype(v.dtype)
    return jnp.einsum('bkgqs,bskd->bqkgd', p, v)

def _gmlp_branch(u, v, z, w_s, b_s):
    B_, T, _ = u.shape
    shp = (B_, T // CHUNK, CHUNK, A_GROUPS, HEAD_DIM)
    vn = _layer_norm(jax.nn.gelu(v).reshape(shp))
    sv = jnp.einsum('gpq,bcqgd->bcpgd', w_s, vn) + b_s.T[:, :, None]
    return (jax.nn.gelu(u).reshape(shp) * sv).reshape(B_, T, A_WIDTH) * jax.nn.silu(z)

def _mlstm_scan(q, k, v, log_i, log_f, state, emit_h):
    B_, T, H, D = q.shape
    nc = T // M_CHUNK

    def chunks(a):
        return a.reshape((B_, nc, M_CHUNK) + a.shape[2:]).swapaxes(0, 1)

    xs = (chunks(q), chunks(k), chunks(v), chunks(log_i), chunks(log_f))
    lower = jnp.tril(jnp.ones((M_CHUNK, M_CHUNK), dtype=bool))[None, :, :, None]

    def step(carry, inp):
        C, n, m = carry
        qc, kc, vc, li, lf = inp
        qf = qc.astype(jnp.float32)
        kf = kc.astype(jnp.float32) * (D ** -0.5)
        vf = vc.astype(jnp.float32)
        b = jnp.cumsum(lf, axis=1)
        b_end = b[:, -1]
        w_end = b_end[:, None] - b + li
        m_new = jnp.maximum(b_end + m, jnp.max(w_end, axis=1))
        decay = jnp.exp(b_end + m - m_new)
        wk = jnp.exp(w_end - m_new[:, None])
        C_new = decay[..., None, None] * C + jnp.einsum('blh,blhd,blhe->bhde', wk, vf, kf)
        n_new = decay[..., None] * n + jnp.einsum('blh,blhe->bhe', wk, kf)
        h = None
        if emit_h:
            a = b + m[:, None]
            dmat = b[:, :, None] - b[:, None] + li[:, None]
            dmat = jnp.where(lower, dmat, -jnp.inf)
            m_t = jnp.maximum(a, jnp.max(dmat, axis=2))
            inter = jnp.exp(a - m_t)
            s = jnp.einsum('bthd,bshd->btsh', qf, kf) * jnp.exp(dmat - m_t[:, :, None])
            num = jnp.einsum('btsh,bshd->bthd', s, vf) + inter[..., None] * jnp.einsum('bhde,bthe->bthd', C, qf)
            den = jnp.sum(s, axis=2) + inter * jnp.einsum('bhe,bthe->bth', n, qf)
            h = num / jnp.maximum(jnp.abs(den), jnp.exp(-m_t))[..., None]
        return (C_new, n_new, m_new), h

    state, hs = lax.scan(step, state, xs)
    h = hs.swapaxes(0, 1).reshape(B_, T, H, D).astype(q.dtype) if emit_h else None
    return h, state

def _layer(x, ctx, mod_lat, mod_ctx, tabs, g_norm, w_in, w_s, b_s, g_q, g_k, b_gates, g_head, w_out,
           with_ctx_out):
    B_, S, _ = x.shape
    Lc = ctx.shape[1]
    sh, sc, gt = jnp.split(mod_lat, 3, axis=-1)
    sh_c, sc_c, gt_c = jnp.split(mod_ctx, 3, axis=-1)
    xn = _rms_norm(x, g_norm) * (1 + sc[:, None]) + sh[:, None]
    cn = _rms_norm(ctx, g_norm) * (1 + sc_c) + sh_c
    (au, av, az, bq, bk, bv, bz, cq, ck, cv, co, cz, cg) = _split_proj(xn @ w_in)
    (au_c, av_c, az_c, bq_c, bk_c, bv_c, bz_c, cq_c, ck_c, cv_c, co_c, cz_c, cg_c) = _split_proj(cn @ w_in)

    def heads_q(t):
        return _rms_norm(t.reshape(t.shape[:2] + (B_KV_HEADS, B_GROUP, HEAD_DIM)), g_q)

    def heads_k(t):
        return _rms_norm(t.reshape(t.shape[:2] + (B_KV_HEADS, HEAD_DIM)), g_k)

    q_lat = _apply_rope(heads_q(bq), tabs)
    k_lat = _apply_rope(heads_k(bk), tabs)
    v_lat = bv.reshape(B_, S, B_KV_HEADS, HEAD_DIM)
    k_ctx = heads_k(bk_c)
    v_ctx = bv_c.reshape(B_, Lc, B_KV_HEADS, HEAD_DIM)
    k_all = jnp.concatenate([k_ctx, k_lat], axis=1)
    v_all = jnp.concatenate([v_ctx, v_lat], axis=1)
    q_blocks = q_lat.reshape(B_, S // Q_BLOCK, Q_BLOCK, B_KV_HEADS, B_GROUP, HEAD_DIM).swapaxes(0, 1)
    o_lat = lax.map(lambda qb: _attend(qb, k_all, v_all), q_blocks)
    y_b = o_lat.swapaxes(0, 1).reshape(B_, S, B_WIDTH) * jax.nn.silu(bz)

    def mheads(t):
        return t.reshape(t.shape[:2] + (C_HEADS, HEAD_DIM))

    def gates(g):
        g = g.astype(jnp.float32) + b_gates.astype(jnp.float32)
        i_f, f_f, i_b, f_b = jnp.split(g, 4, axis=-1)
        return i_f, jax.nn.log_sigmoid(f_f), i_b, jax.nn.log_sigmoid(f_b)

    def flip(t):
        return jnp.flip(t, axis=1)

    ql, kl, vl = mheads(cq), mheads(ck), mheads(cv)
    qc_, kc_, vc_ = mheads(cq_c), mheads(ck_c), mheads(cv_c)
    li_f, lf_f, li_b, lf_b = gates(cg)
    ci_f, cf_f, ci_b, cf_b = gates(cg_c)
    st0 = (jnp.zeros((B_, C_HEADS, HEAD_DIM, HEAD_DIM), jnp.float32),
           jnp.zeros((B_, C_HEADS, HEAD_DIM), jnp.float32),
           jnp.zeros((B_, C_HEADS), jnp.float32))
    h_cf, st_f = _mlstm_scan(qc_, kc_, vc_, ci_f, cf_f, st0, with_ctx_out)
    h_cb, st_b = _mlstm_scan(flip(qc_), flip(kc_), flip(vc_), flip(ci_b), flip(cf_b), st0, with_ctx_out)
    h_lf, _ = _mlstm_scan(ql, kl, vl, li_f, lf_f, st_f, True)
    h_lb, _ = _mlstm_scan(flip(ql), flip(kl), flip(vl), flip(li_b), flip(lf_b), st_b, True)
    g_hd = g_head.reshape(C_HEADS, HEAD_DIM)
    h_lat = _rms_norm(h_lf + flip(h_lb), g_hd).reshape(B_, S, C_WIDTH)
    y_c = jax.nn.sigmoid(co) * h_lat * jax.nn.silu(cz)

    y_a = _gmlp_branch(au, av, az, w_s, b_s)

    x = x + gt[:, None] * (jnp.concatenate([y_a, y_b, y_c], axis=-1) @ w_out)

    if with_ctx_out:
        o_ctx = _attend(heads_q(bq_c), k_ctx, v_ctx).reshape(B_, Lc, B_WIDTH)
        y_b_c = o_ctx * jax.nn.silu(bz_c)
        h_ctx = _rms_norm(h_cf + flip(h_cb), g_hd).reshape(B_, Lc, C_WIDTH)
        y_c_c = jax.nn.sigmoid(co_c) * h_ctx * jax.nn.silu(cz_c)
        y_a_c = _gmlp_branch(au_c, av_c, az_c, w_s, b_s)
        ctx = ctx + gt_c * (jnp.concatenate([y_a_c, y_b_c, y_c_c], axis=-1) @ w_out)
    return x, ctx

def first_inputs(seed: int = 0) -> dict:
    key = jax.random.key(seed)
    ks = jax.random.split(key, 16)
    f32 = jnp.float32

    def nrm(k, shape, scale):
        return jax.random.normal(k, shape, f32) * scale

    f_bias = jnp.linspace(F_BIAS_LO, F_BIAS_HI, C_HEADS, dtype=f32)
    zeros_h = jnp.zeros((C_HEADS,), f32)
    gate_base = jnp.concatenate([zeros_h, f_bias, zeros_h, f_bias])
    return {
        'x': nrm(ks[0], (BATCH, SEQ, D_MODEL), 1.0),
        'c': nrm(ks[1], (BATCH, D_MODEL), 1.0),
        'ctx': nrm(ks[2], (BATCH, CTX_LEN, D_MODEL), 1.0),
        'c_ctx': nrm(ks[3], (D_MODEL,), 1.0),
        'w_ada': nrm(ks[4], (DEPTH, D_MODEL, 3 * D_MODEL), 0.5 * D_MODEL ** -0.5),
        'b_ada': nrm(ks[5], (DEPTH, 3 * D_MODEL), 0.01),
        'g_norm': 1.0 + nrm(ks[6], (DEPTH, D_MODEL), 0.02),
        'w_in': nrm(ks[7], (DEPTH, D_MODEL, D_IN), D_MODEL ** -0.5),
        'w_s': nrm(ks[8], (DEPTH, A_GROUPS, CHUNK, CHUNK), CHUNK ** -0.5),
        'b_s': 1.0 + nrm(ks[9], (DEPTH, A_GROUPS, CHUNK), 0.02),
        'g_q': 1.0 + nrm(ks[10], (DEPTH, HEAD_DIM), 0.02),
        'g_k': 1.0 + nrm(ks[11], (DEPTH, HEAD_DIM), 0.02),
        'b_gates': gate_base + nrm(ks[12], (DEPTH, 4 * C_HEADS), 0.1),
        'g_head': 1.0 + nrm(ks[13], (DEPTH, C_WIDTH), 0.02),
        'w_out': nrm(ks[14], (DEPTH, D_MIX, D_MODEL), D_MIX ** -0.5),
        'g_final': 1.0 + nrm(ks[15], (D_MODEL,), 0.02),
    }

def first_block(x, c, ctx, c_ctx, w_ada, b_ada, g_norm, w_in, w_s, b_s, g_q, g_k, b_gates, g_head, w_out,
              g_final):
    ROWS = x.shape[1] // GRID_W
    tabs = _rope_tables(ROWS)
    silu_c = jax.nn.silu(c)
    silu_cc = jax.nn.silu(c_ctx)
    for l in range(DEPTH):
        mod_lat = silu_c @ w_ada[l] + b_ada[l]
        mod_ctx = silu_cc @ w_ada[l] + b_ada[l]
        x, ctx = _layer(x, ctx, mod_lat, mod_ctx, tabs, g_norm[l], w_in[l], w_s[l], b_s[l], g_q[l], g_k[l],
                        b_gates[l], g_head[l], w_out[l], with_ctx_out=(l < DEPTH - 1))
    return _rms_norm(x, g_final)


DEPTH_2 = 1


GLA_HEADS = 4
GLA_DK = 128
GLA_DV = 256
GLA_RANK = 16
GLA_TAU = 16.0
GLA_CHUNK = 64
GLA_QK = GLA_HEADS * GLA_DK
GLA_V = GLA_HEADS * GLA_DV

RET_HEADS = 4
RET_DK = 128
RET_DV = 256
RET_CHUNK = 128
RET_QK = RET_HEADS * RET_DK
RET_V = RET_HEADS * RET_DV
ROPE_BASE = 10000.0

N_GROUPS = 4
EXPERTS_PER_GROUP = 8
N_EXPERTS = N_GROUPS * EXPERTS_PER_GROUP
TOP_K = 2
EXPERT_FF = 256
MOE_BLOCK = 128

NORM_EPS = 1e-6

IN_SPLITS = (GLA_QK, GLA_QK, GLA_V, GLA_V, GLA_RANK, GLA_RANK,
             RET_QK, RET_QK, RET_V, RET_V, D_MODEL, D_MODEL)
IN_WIDTH = sum(IN_SPLITS)


def rmsnorm(x, g):
    xf = x.astype(jnp.float32)
    y = xf * lax.rsqrt(jnp.mean(xf * xf, axis=-1, keepdims=True) + NORM_EPS)
    return (y * g.astype(jnp.float32)).astype(x.dtype)

def head_groupnorm(o):
    of = o.astype(jnp.float32)
    mu = jnp.mean(of, axis=-1, keepdims=True)
    var = jnp.mean(jnp.square(of - mu), axis=-1, keepdims=True)
    return ((of - mu) * lax.rsqrt(var + NORM_EPS)).astype(o.dtype)

def modulate(h, shift, scale):
    return h * (1.0 + scale) + shift

def split_columns(proj):
    out = []
    start = 0
    for w in IN_SPLITS:
        out.append(proj[..., start:start + w])
        start += w
    return out

def retention_log_decays():
    h = jnp.arange(RET_HEADS, dtype=jnp.float32)
    fwd = jnp.log1p(-jnp.exp2(-5.0 - h))
    bwd = jnp.log1p(-jnp.exp2(-5.5 - h))
    return fwd, bwd

def axial_rope(t, rows, cols):
    half = t.shape[-1] // 2
    n = half // 2
    inv = ROPE_BASE ** (-jnp.arange(n, dtype=jnp.float32) / n)

    def rot(u, p):
        ang = p[:, None] * inv[None, :]
        cos = jnp.cos(ang)[None, :, None, :].astype(u.dtype)
        sin = jnp.sin(ang)[None, :, None, :].astype(u.dtype)
        u1, u2 = u[..., :n], u[..., n:]
        return jnp.concatenate([u1 * cos - u2 * sin, u1 * sin + u2 * cos], axis=-1)

    return jnp.concatenate([rot(t[..., :half], rows), rot(t[..., half:], cols)], axis=-1)

def to_chunks(t, chunk):
    B, L, H, W = t.shape
    return jnp.moveaxis(t.reshape(B, L // chunk, chunk, H, W), 1, 0)

def from_chunks(o):
    N, B, C, H, W = o.shape
    return jnp.moveaxis(o, 0, 1).reshape(B, N * C, H, W)

def gla_scan(q, k, v, log_a, s0, strict):
    C = GLA_CHUNK
    ti = jnp.arange(C)
    mask = (ti[:, None] > ti[None, :]) if strict else (ti[:, None] >= ti[None, :])
    mask5 = mask[None, :, :, None, None]

    def step(S, inp):
        qc, kc, vc, lac = inp
        b = jnp.cumsum(lac.astype(jnp.float32), axis=1)
        inter = jnp.einsum('bthk,bhkv->bthv', qc * jnp.exp(b), S)
        decay = jnp.exp(jnp.where(mask5, b[:, :, None] - b[:, None, :], -jnp.inf))
        scores = jnp.einsum('bthk,btshk,bshk->btsh', qc, decay, kc)
        intra = jnp.einsum('btsh,bshv->bthv', scores, vc)
        b_last = b[:, -1]
        S_new = jnp.exp(b_last)[..., None] * S + jnp.einsum(
            'bshk,bshv->bhkv', kc * jnp.exp(b_last[:, None] - b), vc)
        return S_new, inter + intra

    S_fin, o = lax.scan(step, s0, (to_chunks(q, C), to_chunks(k, C), to_chunks(v, C), to_chunks(log_a, C)))
    return from_chunks(o).astype(v.dtype), S_fin

def retention_scan(q, k, v, log_gamma, s0, strict):
    C = RET_CHUNK
    pos = jnp.arange(C, dtype=jnp.float32)
    ti = jnp.arange(C)
    mask = (ti[:, None] > ti[None, :]) if strict else (ti[:, None] >= ti[None, :])
    rel = pos[:, None] - pos[None, :]
    dmat = jnp.exp(jnp.where(mask[None], rel[None] * log_gamma[:, None, None], -jnp.inf))
    q_decay = jnp.exp((pos + 1.0)[:, None] * log_gamma[None, :])
    k_decay = jnp.exp((C - 1.0 - pos)[:, None] * log_gamma[None, :])
    c_decay = jnp.exp(C * log_gamma)

    def step(S, inp):
        qc, kc, vc = inp
        inter = jnp.einsum('bthk,bhkv->bthv', qc, S) * q_decay[None, :, :, None]
        scores = jnp.einsum('bthk,bshk->bhts', qc, kc) * dmat[None]
        intra = jnp.einsum('bhts,bshv->bthv', scores, vc)
        S_new = c_decay[None, :, None, None] * S + jnp.einsum(
            'bshk,bshv->bhkv', kc * k_decay[None, :, :, None], vc)
        return S_new, inter + intra

    S_fin, o = lax.scan(step, s0, (to_chunks(q, C), to_chunks(k, C), to_chunks(v, C)))
    return from_chunks(o).astype(v.dtype), S_fin

def mixer_heads(h, w_in, gla_lr_w, gla_lr_b, gla_norm, states, rope):
    B, L, _ = h.shape
    (gq, gk, gv, gg, glr_f, glr_b, rq, rk, rv, rg, m_gla, m_ret) = split_columns(h @ w_in)

    def heads(t, n):
        return t.reshape(B, L, n, -1)

    def flip(t):
        return jnp.flip(t, axis=1)

    gq = heads(gq, GLA_HEADS) * GLA_DK ** -0.5
    gk = heads(gk, GLA_HEADS)
    gv = heads(gv, GLA_HEADS)

    def log_gate(lr, d):
        z = (lr @ gla_lr_w[d] + gla_lr_b[d]).astype(jnp.float32)
        return heads(jax.nn.log_sigmoid(z) / GLA_TAU, GLA_HEADS)

    o_f, s_gf = gla_scan(gq, gk, gv, log_gate(glr_f, 0), states[0], False)
    o_b, s_gb = gla_scan(flip(gq), flip(gk), flip(gv), flip(log_gate(glr_b, 1)), states[1], True)
    o_gla = rmsnorm(o_f + flip(o_b), gla_norm) * jax.nn.silu(heads(gg, GLA_HEADS))
    o_gla = o_gla.reshape(B, L, GLA_V)

    rq = heads(rq, RET_HEADS)
    rk = heads(rk, RET_HEADS) * RET_DK ** -0.5
    rv = heads(rv, RET_HEADS)
    if rope is not None:
        rq = axial_rope(rq, rope[0], rope[1])
        rk = axial_rope(rk, rope[0], rope[1])
    lg_f, lg_b = retention_log_decays()
    r_f, s_rf = retention_scan(rq, rk, rv, lg_f, states[2], False)
    r_b, s_rb = retention_scan(flip(rq), flip(rk), flip(rv), lg_b, states[3], True)
    o_ret = head_groupnorm(r_f + flip(r_b)) * jax.nn.silu(heads(rg, RET_HEADS))
    o_ret = o_ret.reshape(B, L, RET_V)
    return o_gla, o_ret, m_gla, m_ret, (s_gf, s_gb, s_rf, s_rb)

def merge_branches(o_gla, o_ret, m_gla, m_ret, w_branch_gla, w_branch_ret, w_out):
    y = jax.nn.sigmoid(m_gla) * (o_gla @ w_branch_gla) + jax.nn.sigmoid(m_ret) * (o_ret @ w_branch_ret)
    return y @ w_out

def hier_moe(h, w_rg, b_rg, w_re, b_re, w_gate, w_up, w_down):
    B, L, D = h.shape
    T = B * L
    xt = h.reshape(T, D)
    g_logits = (xt @ w_rg + b_rg).astype(jnp.float32)
    g_prob = jax.nn.softmax(g_logits, axis=-1)
    g_sel = jnp.argmax(g_logits, axis=-1).astype(jnp.int32)
    g_w = jnp.take_along_axis(g_prob, g_sel[:, None], axis=-1)[:, 0]
    e_logits = (xt @ w_re + b_re).astype(jnp.float32).reshape(T, N_GROUPS, EXPERTS_PER_GROUP)
    e_logits = jnp.take_along_axis(e_logits, g_sel[:, None, None], axis=1)[:, 0]
    top_v, top_i = lax.top_k(e_logits, TOP_K)
    e_w = jax.nn.softmax(top_v, axis=-1) * g_w[:, None]
    expert_id = g_sel[:, None] * EXPERTS_PER_GROUP + top_i.astype(jnp.int32)

    A = T * TOP_K
    flat_e = expert_id.reshape(A)
    flat_tok = jnp.repeat(jnp.arange(T, dtype=jnp.int32), TOP_K)
    flat_w = e_w.reshape(A)
    order = jnp.argsort(flat_e)
    se, stok, sw = flat_e[order], flat_tok[order], flat_w[order]
    counts = jax.ops.segment_sum(jnp.ones((A,), jnp.int32), flat_e, num_segments=N_EXPERTS)
    starts = jnp.cumsum(counts) - counts
    padded = (counts + MOE_BLOCK - 1) // MOE_BLOCK * MOE_BLOCK
    pends = jnp.cumsum(padded)
    pstarts = pends - padded
    dest = pstarts[se] + jnp.arange(A, dtype=jnp.int32) - starts[se]
    P = A + N_EXPERTS * MOE_BLOCK
    NB = P // MOE_BLOCK
    x_pad = jnp.zeros((P, D), h.dtype).at[dest].set(xt[stok])
    tok_pad = jnp.zeros((P,), jnp.int32).at[dest].set(stok)
    w_pad = jnp.zeros((P,), jnp.float32).at[dest].set(sw)
    block_start = jnp.arange(NB, dtype=jnp.int32) * MOE_BLOCK
    block_e = jnp.minimum(jnp.searchsorted(pends, block_start, side='right'), N_EXPERTS - 1)

    def expert_block(args):
        xb, e = args
        hid = jax.nn.silu(xb @ w_gate[e]) * (xb @ w_up[e])
        return hid @ w_down[e]

    y = lax.map(expert_block, (x_pad.reshape(NB, MOE_BLOCK, D), block_e)).reshape(P, D)
    out = jnp.zeros((T, D), jnp.float32).at[tok_pad].add(y.astype(jnp.float32) * w_pad[:, None])
    return out.astype(h.dtype).reshape(B, L, D)

def second_inputs(seed: int = 0) -> dict:
    key = jax.random.key(seed)
    ks = jax.random.split(key, 24)

    def nrm(k, shape, scale):
        return jax.random.normal(k, shape, jnp.float32) * scale

    D = D_MODEL
    return {
        'x': nrm(ks[0], (BATCH, SEQ, D), 1.0),
        'c': nrm(ks[1], (BATCH, D), 1.0),
        'ctx': nrm(ks[2], (BATCH, CTX_LEN, D), 1.0),
        'c_ctx': nrm(ks[3], (D,), 1.0),
        'w_ada': nrm(ks[4], (DEPTH_2, D, 6 * D), D ** -0.5),
        'b_ada': nrm(ks[5], (DEPTH_2, 6 * D), 0.02),
        'norm_mix': 1.0 + nrm(ks[6], (DEPTH_2, D), 0.05),
        'norm_ffn': 1.0 + nrm(ks[7], (DEPTH_2, D), 0.05),
        'w_in': nrm(ks[8], (DEPTH_2, D, IN_WIDTH), D ** -0.5),
        'gla_lr_w': nrm(ks[9], (DEPTH_2, 2, GLA_RANK, GLA_QK), GLA_RANK ** -0.5),
        'gla_lr_b': nrm(ks[10], (DEPTH_2, 2, GLA_QK), 0.1),
        'gla_norm': 1.0 + nrm(ks[11], (DEPTH_2, GLA_DV), 0.05),
        'w_branch_gla': nrm(ks[12], (DEPTH_2, GLA_V, D), GLA_V ** -0.5),
        'w_branch_ret': nrm(ks[13], (DEPTH_2, RET_V, D), RET_V ** -0.5),
        'w_out': nrm(ks[14], (DEPTH_2, D, D), D ** -0.5),
        'w_router_group': nrm(ks[15], (DEPTH_2, D, N_GROUPS), D ** -0.5),
        'b_router_group': nrm(ks[16], (DEPTH_2, N_GROUPS), 0.01),
        'w_router_expert': nrm(ks[17], (DEPTH_2, D, N_EXPERTS), D ** -0.5),
        'b_router_expert': nrm(ks[18], (DEPTH_2, N_EXPERTS), 0.01),
        'w_expert_gate': nrm(ks[19], (DEPTH_2, N_EXPERTS, D, EXPERT_FF), D ** -0.5),
        'w_expert_up': nrm(ks[20], (DEPTH_2, N_EXPERTS, D, EXPERT_FF), D ** -0.5),
        'w_expert_down': nrm(ks[21], (DEPTH_2, N_EXPERTS, EXPERT_FF, D), EXPERT_FF ** -0.5),
        'norm_final': 1.0 + nrm(ks[22], (D,), 0.05),
    }

def second_block(x, c, ctx, c_ctx, w_ada, b_ada, norm_mix, norm_ffn, w_in, gla_lr_w, gla_lr_b, gla_norm,
              w_branch_gla, w_branch_ret, w_out, w_router_group, b_router_group, w_router_expert,
              b_router_expert, w_expert_gate, w_expert_up, w_expert_down, norm_final):
    B, L, _ = x.shape
    ROWS = L // GRID_W
    rows = jnp.repeat(jnp.arange(ROWS, dtype=jnp.float32), GRID_W)
    cols = jnp.tile(jnp.arange(GRID_W, dtype=jnp.float32), ROWS)
    zero_states = (
        jnp.zeros((B, GLA_HEADS, GLA_DK, GLA_DV), jnp.float32),
        jnp.zeros((B, GLA_HEADS, GLA_DK, GLA_DV), jnp.float32),
        jnp.zeros((B, RET_HEADS, RET_DK, RET_DV), jnp.float32),
        jnp.zeros((B, RET_HEADS, RET_DK, RET_DV), jnp.float32),
    )
    h_lat = x
    h_ctx = ctx
    for layer in range(DEPTH_2):
        sh1, sc1, g1, sh2, sc2, g2 = jnp.split(
            (jax.nn.silu(c) @ w_ada[layer] + b_ada[layer])[:, None, :], 6, axis=-1)
        csh1, csc1, cg1, csh2, csc2, cg2 = jnp.split(
            (jax.nn.silu(c_ctx) @ w_ada[layer] + b_ada[layer])[None, None, :], 6, axis=-1)
        mix_args = (w_in[layer], gla_lr_w[layer], gla_lr_b[layer], gla_norm[layer])
        merge_args = (w_branch_gla[layer], w_branch_ret[layer], w_out[layer])
        moe_args = (w_router_group[layer], b_router_group[layer], w_router_expert[layer],
                    b_router_expert[layer], w_expert_gate[layer], w_expert_up[layer], w_expert_down[layer])

        hc = modulate(rmsnorm(h_ctx, norm_mix[layer]), csh1, csc1)
        c_gla, c_ret, c_mg, c_mr, ctx_states = mixer_heads(hc, *mix_args, zero_states, None)

        hl = modulate(rmsnorm(h_lat, norm_mix[layer]), sh1, sc1)
        l_gla, l_ret, l_mg, l_mr, _ = mixer_heads(hl, *mix_args, ctx_states, (rows, cols))
        h_lat = h_lat + g1 * merge_branches(l_gla, l_ret, l_mg, l_mr, *merge_args)
        h_lat = h_lat + g2 * hier_moe(modulate(rmsnorm(h_lat, norm_ffn[layer]), sh2, sc2), *moe_args)

        if layer < DEPTH_2 - 1:
            h_ctx = h_ctx + cg1 * merge_branches(c_gla, c_ret, c_mg, c_mr, *merge_args)
            h_ctx = h_ctx + cg2 * hier_moe(modulate(rmsnorm(h_ctx, norm_ffn[layer]), csh2, csc2), *moe_args)
    return rmsnorm(h_lat, norm_final)


def setup_inputs(seed=0):
    out = dict(first_inputs(seed))
    for name, value in second_inputs(seed + 1).items():
        if name != "x":
            out[name + "_2"] = value
    return out


def reference(
    x, c, ctx, c_ctx, w_ada, b_ada, g_norm, w_in, w_s, b_s, g_q, g_k, b_gates, g_head, w_out,
    g_final, c_2, ctx_2, c_ctx_2, w_ada_2, b_ada_2, norm_mix_2, norm_ffn_2, w_in_2, gla_lr_w_2,
    gla_lr_b_2, gla_norm_2, w_branch_gla_2, w_branch_ret_2, w_out_2, w_router_group_2,
    b_router_group_2, w_router_expert_2, b_router_expert_2, w_expert_gate_2, w_expert_up_2,
    w_expert_down_2, norm_final_2,
):
    x = first_block(
        x, c, ctx, c_ctx, w_ada, b_ada, g_norm, w_in, w_s, b_s, g_q, g_k, b_gates, g_head,
        w_out, g_final,
    )
    return second_block(
        x, c_2, ctx_2, c_ctx_2, w_ada_2, b_ada_2, norm_mix_2, norm_ffn_2, w_in_2, gla_lr_w_2,
        gla_lr_b_2, gla_norm_2, w_branch_gla_2, w_branch_ret_2, w_out_2, w_router_group_2,
        b_router_group_2, w_router_expert_2, b_router_expert_2, w_expert_gate_2, w_expert_up_2,
        w_expert_down_2, norm_final_2,
    )


_drawn_inputs = setup_inputs


def setup_inputs(seed=0):
    import zlib

    import numpy as np

    out = dict(_drawn_inputs(seed))
    spreads = {}
    factors = {'b_s': 8.0,
     'g_q': 8.0,
     'g_k': 8.0,
     'g_head': 5.52,
     'b_router_group_2': 3.547,
     'b_router_expert_2': 3.763}
    for name, (base, spread) in spreads.items():
        noise = np.random.default_rng([zlib.crc32(name.encode()), seed]).standard_normal(out[name].shape)
        drawn = base * np.exp(spread * noise) if base else spread * noise
        out[name] = __import__('jax').numpy.asarray(drawn.astype(out[name].dtype))
    for name, factor in factors.items():
        out[name] = (out[name] * factor).astype(out[name].dtype)
    return out
```

```python
from contextlib import ExitStack

import numpy as np

import concourse.bass as bass
from concourse import mybir

F32 = mybir.dt.float32
ALU = mybir.AluOpType
ACT = mybir.ActivationFunctionType
AX = mybir.AxisListType.X

NC_T = 2
NL_T = 8
NT = NC_T + NL_T
T = NT * 128
ARENA = 53200
GELU_C = -2.0 * 0.7978845608028654
W1 = [512, 512, 512, 512, 512, 512, 272]
LEVELS = [64, 32, 16, 8, 4, 2, 1]


def flat(tokens):
    for a in tokens:
        if isinstance(a, (list, tuple)):
            yield from flat(a)
        elif a is not None:
            yield a


class Op:

    def __init__(self, queue, index, sem, value):
        self.queue, self.index, self.sem, self.value = queue, index, sem, value


class Queue:

    def __init__(self, sem, awaited, eng):
        self.sem, self.awaited, self.eng = sem, awaited, eng
        self.n = self.count = 0
        self.seen = {}
        self.tail = None

    def _wait(self, after):
        for a in flat(after):
            if a.index is not None:
                a.queue.awaited.add(a.index)
            if self.eng is not None and self.seen.get(id(a.sem), 0) < a.value:
                self.eng.wait_ge(a.sem, a.value)
                self.seen[id(a.sem)] = a.value

    def __call__(self, fn, *after):
        self._wait(after)
        if fn is None:
            return None
        self.n += 1
        hit = self.n in self.awaited
        self.count += hit
        if self.eng is not None:
            ins = fn(self.eng)
            if hit:
                ins.then_inc(self.sem, 1)
        self.tail = Op(self, self.n, self.sem, self.count)
        return self.tail

    def dma(self, chan, fn, *after):
        self._wait(after)
        chan.count += 16
        if self.eng is not None:
            fn(self.eng).then_inc(chan.sem, 16)
        return Op(self, None, chan.sem, chan.count)

    def last(self):
        return self.tail


class Chan:
    def __init__(self, sem):
        self.sem, self.count = sem, 0


class Slot:

    def __init__(self, ap, chan=None):
        self.ap, self.free, self.chan = ap, [], chan


class Ring:
    def __init__(self, slots):
        self.slots, self.n = slots, 0

    def take(self):
        s = self.slots[self.n % len(self.slots)]
        self.n += 1
        return s


ENGINES = ("pe", "v", "a", "g", "sp")
CHANNELS = [f"d_m{i}" for i in range(24)] + [f"d_w{i}" for i in range(3)] + [f"d_x{i}" for i in range(NT)] + \
           [f"d_o{i}" for i in range(4)] + [f"d_rope{i}" for i in range(2)] + [f"d_n{i}" for i in range(4)] + \
           [f"d_g{i}" for i in range(3)] + [f"d_y{i}" for i in range(3)] + \
           [f"d_z{i}" for i in range(8)]
NOV = 15
NB = 32 + NOV


def program(nc, I, out):
    with ExitStack() as ctx:
        arena = ctx.enter_context(nc.sbuf_tensor("arena", [128, ARENA], F32))
        psum = ctx.enter_context(nc.psum_tensor("psum", [128, 8, 512], F32))
        sems = {n: ctx.enter_context(nc.semaphore("s_" + n)) for n in list(ENGINES) + CHANNELS}
        X1 = nc.dram_tensor("x1_scratch", [T, 1024], F32, kind="Internal").ap()
        X2 = nc.dram_tensor("x2_scratch", [1024, 1024], F32, kind="Internal").ap()
        HN = nc.dram_tensor("hn_scratch", [1024, 1024], F32, kind="Internal").ap()
        YB = nc.dram_tensor("yb_scratch", [NB * 128, 1024], F32, kind="Internal").ap()
        awaited = {n: set() for n in ENGINES}
        block = ctx.enter_context(nc.Block())

        def run(name, eng):
            describe(I, out, arena, psum, X1, X2, HN, YB, sems,
                     [Queue(sems[n], awaited[n], eng if n == name else None) for n in ENGINES])
        run(None, None)
        block.tensor(lambda e: run("pe", e))
        block.vector(lambda e: run("v", e))
        block.scalar(lambda e: run("a", e))
        block.gpsimd(lambda e: run("g", e))
        block.sync(lambda e: run("sp", e))


def describe(I, out, arena, psum, X1, X2, HN, YB, sems, queues):
    PE, V, A, G, SP = queues

    def chan(name):
        return Chan(sems[name])

    at = [0]

    def alloc(*shape):
        n = int(np.prod(shape))
        a = arena[:, at[0]:at[0] + n]
        at[0] += n
        assert at[0] <= ARENA, at[0]
        if len(shape) > 1:
            names = "abcd"[:len(shape)]
            kw = {names[i]: shape[i] for i in range(len(shape))}
            a = a.rearrange("p (" + " ".join(names) + ") -> p " + " ".join(names), **kw)
        return a

    def bc(ap, n):
        return ap.unsqueeze(len(ap.shape)).broadcast_to(list(ap.shape) + [n])

    def mid(ap, n):
        p, m = ap.shape
        return ap.unsqueeze(1).broadcast_to([p, n, m])

    banks = [Slot(psum[:, i, :]) for i in range(8)]
    rb = Ring(banks)

    def barrier():
        tails = [q.last() for q in (PE, V, A, G)]
        for q in (PE, V, A, G):
            q(None, tails)
        return tails

    ch_misc = [chan(f"d_m{i}") for i in range(24)]
    misc_last = [None] * 24
    misc_n = [0]

    def load(dst, src, *after):
        i = misc_n[0] % 24
        misc_n[0] += 1
        misc_last[i] = SP.dma(ch_misc[i], lambda e: e.dma_start(dst, src), misc_last[i], *after)
        return misc_last[i]

    ident = alloc(128)
    ones = alloc(128)
    sel4 = alloc(4, 128)
    bsel = alloc(128)
    small = alloc(64)
    t_id = load(ident, I["k_ident"])
    t_sel = load(sel4[0:4], I["k_sel4"])
    t_bsel = load(bsel[0:4], I["k_bsel"])
    t_ones = V(lambda e: e.memset(ones, 1.0))
    wring = Ring([Slot(alloc(4096), chan(f"d_w{i}")) for i in range(3)])

    def wload(src, cols, *after):
        s = wring.take()
        dst = s.ap[:, 0:8 * cols].rearrange("p (k n) -> p k n", k=8)
        tok = SP.dma(s.chan, lambda e: e.dma_start(dst, src), s.free, *after)
        return dst, tok, s

    def rstd_of(ss, dst, scale, *after):
        a = V(lambda e: e.tensor_scalar(dst, ss, scale, 1e-6, ALU.mult, ALU.add), *after)
        a = A(lambda e: e.activation(dst, dst, ACT.Ln), a)
        return A(lambda e: e.activation(dst, dst, ACT.Exp, scale=-0.5), a)

    def mm_group(out_ap, pairs):
        def fn(e):
            n = len(pairs)
            for i, (l, r) in enumerate(pairs):
                ins = e.matmul(out_ap, l, r, start=(i == 0), stop=(i == n - 1))
            return ins
        return fn

    def transposes(outs_ins, idn):
        def fn(e):
            for o, i in outs_ins:
                ins = e.transpose(o, i, idn)
            return ins
        return fn

    def to_feature(src, dst, t, scale, bias, *after):
        toks = []
        for half in range(2):
            b = rb.take()
            tr = PE(transposes([(b.ap[:, j * 128:(j + 1) * 128],
                                 src[:, (half * 4 + j) * 128:(half * 4 + j + 1) * 128]) for j in range(4)],
                               ident), b.free, t_id, *after)
            q = A if half == 0 else V
            for j in range(4):
                k = half * 4 + j
                d = dst[:, k, t * 128:(t + 1) * 128]
                s_ = b.ap[:, j * 128:(j + 1) * 128]
                if scale is None:
                    if q is A:
                        o = A(lambda e, d=d, s_=s_: e.activation(d, s_, ACT.Copy), tr)
                    else:
                        o = V(lambda e, d=d, s_=s_: e.tensor_copy(d, s_), tr)
                elif q is A:
                    o = A(lambda e, d=d, s_=s_, k=k: e.activation(
                        d, s_, ACT.Identity, bias=bias[:, k:k + 1], scale=scale[:, k:k + 1]), tr)
                else:
                    o = V(lambda e, d=d, s_=s_, k=k: e.tensor_scalar(
                        d, s_, scale[:, k:k + 1], bias[:, k:k + 1], ALU.mult, ALU.add), tr)
            b.free = [o]
            toks.append(o)
        return toks

    def sig_den(dst, src, *after):
        a = A(lambda e: e.activation(dst, src, ACT.Exp, scale=-1.0), *after)
        return G(lambda e: e.tensor_scalar(dst, dst, 1.0, None, ALU.add), a)

    def modulation(name_w, ngroups, cvec, t_c, MOD, badd):
        last = None
        for g in range(ngroups):
            w, tw, s = wload(name_w[g], 512)
            b = rb.take()

            def fn(e, w=w, b=b):
                for j in range(4):
                    for k in range(8):
                        ins = e.matmul(b.ap[:, 2 * j:2 * j + 2], w[:, k, j * 128:(j + 1) * 128],
                                       cvec[:, k, :], start=(k == 0), stop=(k == 7))
                return ins
            mm = PE(fn, tw, t_c, b.free)
            s.free = [mm]
            last = V(lambda e, g=g, b=b: e.tensor_tensor(
                MOD[:, 4 * g:4 * g + 4, :], b.ap[:, 0:8].rearrange("p (j v) -> p j v", v=2),
                bc(badd[:, 4 * g:4 * g + 4], 2), ALU.add), mm)
            b.free = [last]
        return last

    def silu_c(cvec, tmp, src, *after):
        l = load(cvec, src, *after)
        a = A(lambda e: e.activation(tmp, cvec, ACT.Exp, scale=-1.0), l)
        a = V(lambda e: e.tensor_scalar(tmp, tmp, 1.0, None, ALU.add), a)
        a = V(lambda e: e.reciprocal(tmp, tmp), a)
        return V(lambda e: e.tensor_tensor(cvec, cvec, tmp, ALU.mult), a)

    def row_broadcast(dst, cols, n, *after):
        dg = alloc(2, 128)
        free = [None, None]
        last = None
        for j in range(n):
            b = rb.take()
            d = V(lambda e, j=j: e.tensor_scalar(dg[:, j % 2, :], ident, cols[:, j:j + 1], None, ALU.mult),
                  t_id, free[j % 2], *after)
            m = PE(lambda e, j=j, b=b: e.matmul(b.ap[:, 0:128], ones, dg[:, j % 2, :], start=True, stop=True),
                   d, t_ones, b.free)
            free[j % 2] = m
            last = A(lambda e, j=j, b=b: e.activation(dst[:, j * 128:(j + 1) * 128], b.ap[:, 0:128], ACT.Copy), m)
            b.free = [last]
        return last

    def normalise_in(X, xT, src_rows, scale, bias, t_mod, *after):
        ss = alloc(NT)
        sq = alloc(1024)
        lo = []
        for t in range(NT):
            s_ = src_rows[t]
            c = ch_x[t]
            lo.append(SP.dma(c, lambda e, t=t, s_=s_: e.dma_start(X[:, t, :], s_), *after))
        a = None
        for t in range(NT):
            a = A(lambda e, t=t: e.activation(sq, X[:, t, :], ACT.Square, accum_out=ss[:, t:t + 1]), lo[t], after, a)
        r = rstd_of(ss, ss, 1.0 / 1024, a)
        toks = []
        for t in range(NT):
            q = V if t % 2 else G
            m = q(lambda e, t=t: e.tensor_scalar(X[:, t, :], X[:, t, :], ss[:, t:t + 1], None, ALU.mult), r)
            v = 1 if t < NC_T else 0
            toks += to_feature(X[:, t, :], xT, t, scale[:, :, v], bias[:, :, v], m, t_mod)
        return toks

    ch_x = [chan(f"d_x{i}") for i in range(NT)]
    ch_o = [chan(f"d_o{i}") for i in range(4)]

    x1_store = [None] * NT
    x2_store = [None] * NL_T
    top = at[0]
    rows0 = [I["ctx"][t * 128:(t + 1) * 128, :] for t in range(NC_T)] + \
            [I["x"][t * 128:(t + 1) * 128, :] for t in range(NL_T)]
    DEPTH = 2
    phase = []
    for l in range(DEPTH):
        emit_ctx = l < DEPTH - 1
        t0 = 0 if emit_ctx else NC_T
        at[0] = top
        xnT = alloc(8, T)
        Y = alloc(NT, 1024)
        cvec = alloc(8, 2)
        ctmp = alloc(8, 2)
        MOD = alloc(24, 2)
        AM = alloc(8, 2)
        bada = alloc(24)
        gn = alloc(8)
        gates_b = alloc(16)
        keep = at[0]
        tb = load(bada, I["b_ada"][l], phase)
        tg = load(gn, I["g_norm"][l], phase)
        tc = silu_c(cvec, ctmp, I["c"], phase)
        tm = modulation(I["w_ada"][l], 6, cvec, [tc, tb], MOD, bada)
        tm = V(lambda e: e.tensor_scalar(AM, MOD[:, 8:16, :], 1.0, None, ALU.add), tm)
        tm = V(lambda e: e.tensor_tensor(AM, AM, bc(gn, 2), ALU.mult), tm, tg)
        rows = rows0 if l == 0 else [X1[t * 128:(t + 1) * 128, :] for t in range(NT)]
        tx = normalise_in(Y, xnT, rows, AM, MOD[:, 0:8, :], tm, phase, x1_store)
        xnT_ready = tx
        barrier()
        at[0] = keep
        KV = alloc(NT, 256)
        wsT = alloc(4, 128)
        bsT = alloc(4)
        vu = alloc(2, 512)
        zb = alloc(2, 256)
        t1 = alloc(512)
        t2 = alloc(512)
        t3 = alloc(256)
        t4 = alloc(256)
        st = alloc(16)
        bar = [q.last() for q in (PE, V, A, G)]
        dw = load(wsT, I["w_s"][l], bar)
        db = load(bsT, I["b_s"][l], bar)
        w0, tw0, s0 = wload(I["w_in"][0][l], 512)
        w1, tw1, s1 = wload(I["w_in"][1][l], 512)
        prev_vu = [None, None]
        last_y = [None] * NT
        kv_t = [None] * NT
        for t in range(NT):
            cols = slice(t * 128, (t + 1) * 128)
            full = t >= t0
            b1 = rb.take()
            c0 = 0 if full else 256
            m1 = PE(mm_group(b1.ap[:, c0:512], [(xnT[:, k, cols], w1[:, k, c0:512]) for k in range(8)]),
                    tw1, xnT_ready, b1.free)
            kv_t[t] = A(lambda e, t=t, b1=b1: e.activation(KV[:, t, :], b1.ap[:, 256:512], ACT.Copy), m1)
            b1.free = [kv_t[t]]
            if not full:
                s1.free = [m1]
                continue
            b0 = rb.take()
            m0 = PE(mm_group(b0.ap, [(xnT[:, k, cols], w0[:, k, :]) for k in range(8)]),
                    tw0, xnT_ready, b0.free)
            s0.free, s1.free = [m0], [m0]
            x_ = vu[:, t % 2, :]
            z_ = zb[:, t % 2, :]
            zc = A(lambda e, z_=z_, b1=b1: e.activation(z_, b1.ap[:, 0:256], ACT.Copy), m1, prev_vu[t % 2])
            b1.free = [zc]
            xc = A(lambda e, x_=x_, b0=b0: e.activation(x_, b0.ap, ACT.Copy), m0, prev_vu[t % 2])
            b0.free = [xc]
            a = V(lambda e, x_=x_: e.tensor_tensor(t1, x_, x_, ALU.mult), xc)
            a = V(lambda e: e.tensor_scalar(t1, t1, 0.044715, 1.0, ALU.mult, ALU.add), a)
            a = V(lambda e, x_=x_: e.tensor_tensor(t1, t1, x_, ALU.mult), a)
            a = A(lambda e: e.activation(t2, t1, ACT.Exp, scale=GELU_C), a)
            a = V(lambda e: e.tensor_scalar(t2, t2, 1.0, None, ALU.add), a)
            a = V(lambda e: e.reciprocal(t2, t2), a)
            g_ = V(lambda e, x_=x_: e.tensor_tensor(x_, t2, x_, ALU.mult), a)
            v4 = x_[:, 0:256].rearrange("p (g d) -> p g d", g=4)
            q4 = t3.rearrange("p (g d) -> p g d", g=4)
            a = V(lambda e, v4=v4: e.tensor_reduce(st[:, 0:4], v4, AX, ALU.add), g_)
            a = V(lambda e: e.tensor_scalar(st[:, 0:4], st[:, 0:4], 1.0 / 64, None, ALU.mult), a)
            vc = V(lambda e, v4=v4: e.tensor_tensor(v4, v4, bc(st[:, 0:4], 64), ALU.subtract), a)
            a = V(lambda e, v4=v4: e.tensor_tensor(q4, v4, v4, ALU.mult), vc)
            a = V(lambda e: e.tensor_reduce(st[:, 4:8], q4, AX, ALU.add), a)
            a = rstd_of(st[:, 4:8], st[:, 4:8], 1.0 / 64, a)
            a = V(lambda e, v4=v4: e.tensor_tensor(v4, v4, bc(st[:, 4:8], 64), ALU.mult), a)
            b2 = rb.take()

            def fn(e, b2=b2, x_=x_):
                for g in range(4):
                    ins = e.matmul(b2.ap[:, g * 64:(g + 1) * 64], wsT[:, g, :], x_[:, g * 64:(g + 1) * 64],
                                   start=True, stop=True)
                return ins
            ms = PE(fn, a, dw, b2.free)
            zd = sig_den(t4, z_, zc, last_y[t - 1] if t else None)
            a = V(lambda e: e.reciprocal(t4, t4), zd)
            a = V(lambda e, z_=z_: e.tensor_tensor(t4, t4, z_, ALU.mult), a)
            a1 = V(lambda e, x_=x_: e.tensor_tensor(t4, t4, x_[:, 256:512], ALU.mult), a, g_)
            a = V(lambda e, b2=b2: e.tensor_tensor(q4, b2.ap[:, 0:256].rearrange("p (g d) -> p g d", g=4),
                                                   bc(bsT, 64), ALU.add), ms, db)
            b2.free = [a]
            last_y[t] = V(lambda e, t=t: e.tensor_tensor(Y[:, t, 0:256], t3, t4, ALU.mult), a, a1)
            prev_vu[t % 2] = [last_y[t], ms]
        barrier()
        at[0] = keep
        KV = alloc(NT, 256)
        kT = alloc(2, T)
        qT = alloc(4, T)
        mark = at[0]
        rope = alloc(NL_T, 128)
        gqk = alloc(2, 64)
        qs = alloc(2, 512)
        t1 = alloc(512)
        t2 = alloc(512)
        kd = alloc(2, 128)
        st = alloc(16)
        bar = [q.last() for q in (PE, V, A, G)]
        dr = load(rope, I["k_rope1"], bar)
        dg = [load(gqk[:, 0, :], I["g_q"][l].partition_broadcast(128), bar),
              load(gqk[:, 1, :], I["g_k"][l].partition_broadcast(128), bar)]

        def headnorm_rope(x_, n, gi, t, *after):
            x3 = x_.rearrange("p (h d) -> p h d", h=n)
            y_ = t1[:, 0:64 * n]
            y3 = y_.rearrange("p (h d) -> p h d", h=n)
            a = G(lambda e: e.tensor_tensor(y_, x_, x_, ALU.mult), hn[0], *after)
            a = V(lambda e: e.tensor_reduce(st[:, 0:n], y3, AX, ALU.add), a)
            a = rstd_of(st[:, 0:n], st[:, 0:n], 1.0 / 64, a)
            a = V(lambda e: e.tensor_tensor(x3, x3, bc(st[:, 0:n], 64), ALU.mult), a)
            a = V(lambda e: e.tensor_tensor(x3, x3, mid(gqk[:, gi, :], n), ALU.mult), a, dg)
            if t < NC_T:
                hn[0] = a
                return a
            tab = rope[:, t - NC_T, :]
            z_ = t2[:, 0:64 * n]
            z3 = z_.rearrange("p (h d) -> p h d", h=n)
            b_ = V(lambda e: e.tensor_tensor(y3, x3, mid(tab[:, 0:64], n), ALU.mult), a, dr)
            last = []
            x5 = x_.rearrange("p (h r s f) -> p h r s f", h=n, r=2, s=2)
            z5 = z_.rearrange("p (h r s f) -> p h r s f", h=n, r=2, s=2)
            s5 = tab[:, 64:128].rearrange("p (r s f) -> p r s f", r=2, s=2)
            for r in range(2):
                for s in range(2):
                    last.append(G(lambda e, r=r, s=s: e.tensor_tensor(
                        z5[:, :, r, s, :], x5[:, :, r, 1 - s, :], mid(s5[:, r, s, :], n), ALU.mult), a, dr))
            hn[0] = V(lambda e: e.tensor_tensor(x_, y_, z_, ALU.add), b_, last)
            return hn[0]

        hn = [None]

        w, tw, s_ = wload(I["w_in"][2][l], 512)
        prev = [None, None]
        pk = [None, None]
        for t in range(NT):
            cols = slice(t * 128, (t + 1) * 128)
            a = headnorm_rope(KV[:, t, 0:128], 2, 1, t)
            k3 = KV[:, t, 0:128].rearrange("p (g d) -> p g d", g=2)
            kd4 = kd.rearrange("p g (r d) -> p g r d", r=2)
            a = [V(lambda e, k3=k3, r=r: e.tensor_copy(kd4[:, :, r, :], k3), a, pk[t % 2]) for r in range(2)]
            b = rb.take()
            tr = PE(transposes([(b.ap[:, g * 128:(g + 1) * 128], kd[:, g, :]) for g in range(2)], ident), a, b.free)
            pk = [tr, tr]
            o = A(lambda e, b=b, cols=cols: e.activation(
                kT[:, :, cols], b.ap[:, 0:256].rearrange("p (g t) -> p g t", g=2), ACT.Copy), tr)
            b.free = [o]
            if t < t0:
                continue
            b = rb.take()
            m = PE(mm_group(b.ap, [(xnT[:, k, cols], w[:, k, :]) for k in range(8)]), tw, b.free)
            s_.free = [m]
            q_ = qs[:, t % 2, :]
            c = A(lambda e, q_=q_, b=b: e.activation(q_, b.ap, ACT.Copy), m, prev[t % 2])
            b.free = [c]
            a = headnorm_rope(q_, 8, 0, t, c)
            b = rb.take()
            tr = PE(transposes([(b.ap[:, j * 128:(j + 1) * 128], q_[:, j * 128:(j + 1) * 128]) for j in range(4)],
                               ident), a, b.free)
            prev[t % 2] = tr
            o = A(lambda e, b=b, cols=cols: e.activation(
                qT[:, :, cols], b.ap.rearrange("p (g t) -> p g t", g=4), ACT.Copy), tr)
            b.free = [o]
        w3, tw3, s3 = wload(I["w_in"][3][l], 512)
        w5, tw5, s5_ = wload(I["w_in"][5][l], 512)
        barrier()
        pt = None
        for t in range(t0, NT):
            cols = slice(t * 128, (t + 1) * 128)
            b = rb.take()
            m = PE(mm_group(b.ap, [(xnT[:, k, cols], w3[:, k, :]) for k in range(8)]), tw3, b.free)
            s3.free = [m]
            a = A(lambda e, b=b: e.activation(t1, b.ap, ACT.Exp, scale=-1.0), m, pt)
            a = V(lambda e: e.tensor_scalar(t1, t1, 1.0, None, ALU.add), a)
            a = V(lambda e: e.reciprocal(t1, t1), a)
            a = V(lambda e, b=b, t=t: e.tensor_tensor(Y[:, t, 256:768], b.ap, t1, ALU.mult), a)
            b.free = [a]
            b = rb.take()
            m = PE(mm_group(b.ap, [(xnT[:, k, cols], w5[:, k, :]) for k in range(8)]), tw5, b.free)
            s5_.free = [m]
            a2 = A(lambda e, b=b: e.activation(t2, b.ap, ACT.Exp, scale=-1.0), m, pt)
            a2 = V(lambda e: e.tensor_scalar(t2, t2, 1.0, None, ALU.add), a2)
            a2 = V(lambda e: e.tensor_tensor(t2[:, 0:256], t2[:, 0:256], t2[:, 256:512], ALU.mult), a2)
            a2 = V(lambda e: e.reciprocal(t2[:, 0:256], t2[:, 0:256]), a2)
            a2 = V(lambda e, b=b, t=t: e.tensor_tensor(Y[:, t, 768:1024], b.ap[:, 256:512], t2[:, 0:256],
                                                       ALU.mult), a2)
            b.free = [a2]
            pt = [a, a2]
        barrier()
        at[0] = mark
        Pm = alloc(2, T)
        PT = alloc(2, T)
        st = alloc(4, 4)
        sets = [psum[:, 0:3, :].rearrange("p b n -> p (b n)"), psum[:, 3:6, :].rearrange("p b n -> p (b n)")]
        set_free = [[b for s in banks[0:3] for b in s.free], [b for s in banks[3:6] for b in s.free]]
        pv_free = [banks[6].free, banks[7].free]
        P_free = [None, None]
        PT_free = [None, None]
        units = [(t, h) for t in range(t0, NT) for h in range(8)]
        state = {}

        def att_scores(u):
            t, h = units[u]
            n = (NC_T if t < NC_T else NT) * 128
            i = u % 2
            base = 64 * (h % 2)
            g = h // 4
            S = sets[i]

            def fn(e):
                for c in range(0, n, 512):
                    w_ = min(512, n - c)
                    ins = e.matmul(S[:, c:c + w_], qT[base:base + 64, h // 2, t * 128:(t + 1) * 128],
                                   kT[base:base + 64, g, c:c + w_], start=True, stop=True)
                return ins
            m = PE(fn, set_free[i])
            mx = st[:, i, 0:1]
            a = V(lambda e: e.tensor_reduce(mx, S[:, 0:n], AX, ALU.max), m, state.get(u - 2))
            a = V(lambda e: e.tensor_scalar(mx, mx, -0.125, None, ALU.mult), a)
            state["e", u] = A(lambda e: e.activation(Pm[:, i, 0:n], S[:, 0:n], ACT.Exp, bias=mx, scale=0.125,
                                                     accum_out=st[:, i, 1:2]), a, P_free[i])

        def att_values(u):
            t, h = units[u]
            nt = NC_T if t < NC_T else NT
            i = u % 2
            g = h // 4
            S = sets[i]
            outs = []
            for c in range(0, nt, 4):
                n = min(4, nt - c)
                tr = PE(transposes([(S[:, (c + j) * 128:(c + j + 1) * 128], Pm[:, i, (c + j) * 128:(c + j + 1) * 128])
                                    for j in range(n)], ident), state["e", u])
                d = PT[:, i, c * 128:(c + n) * 128]
                s_ = S[:, c * 128:(c + n) * 128]
                if c == 0:
                    o = V(lambda e, d=d, s_=s_: e.tensor_copy(d, s_), tr, PT_free[i])
                else:
                    o = A(lambda e, d=d, s_=s_: e.activation(d, s_, ACT.Copy), tr, PT_free[i])
                outs.append(o)
            P_free[i] = [tr]
            set_free[i] = outs
            O = psum[:, 6 + i, 0:64]

            def fn(e):
                for c in range(nt):
                    ins = e.matmul(O, PT[:, i, c * 128:(c + 1) * 128], KV[:, c, 128 + 64 * g:192 + 64 * g],
                                   start=(c == 0), stop=(c == nt - 1))
                return ins
            m = PE(fn, outs, pv_free[i])
            PT_free[i] = [m]
            a = V(lambda e: e.reciprocal(st[:, i, 2:3], st[:, i, 1:2]), state["e", u])
            yv = Y[:, t, 256 + 64 * h:320 + 64 * h]
            a = V(lambda e: e.scalar_tensor_tensor(yv, O, st[:, i, 2:3], yv, ALU.mult, ALU.mult), a, m)
            pv_free[i] = [a]
            state[u] = a

        for u in range(len(units)):
            att_scores(u)
            if u:
                att_values(u - 1)
        att_values(len(units) - 1)
        barrier()
        for b in banks:
            b.free = []
        at[0] = keep
        kc = alloc(NT, 256)
        va = alloc(NT, 4, 65)
        qkT = alloc(4, T)
        graw = alloc(2, 288)
        LIF = alloc(4, T)
        bar = [q.last() for q in (PE, V, A, G)]
        gb4 = gates_b[0:4, 0:4]
        dgb = load(gb4, I["b_gates"][l], bar)
        w4, tw4, s4 = wload(I["w_in"][4][l], 512)
        w6, tw6, s6 = wload(I["w_in"][6][l], 272)
        on = V(lambda e: e.memset(va[:, :, :, 64:65], 1.0))
        prev = [None, None]
        for t in range(NT):
            cols = slice(t * 128, (t + 1) * 128)
            b = rb.take()
            m = PE(mm_group(b.ap, [(xnT[:, k, cols], w4[:, k, :]) for k in range(8)]), tw4, b.free)
            s4.free = [m]
            a1 = A(lambda e, b=b, t=t: e.activation(kc[:, t, :], b.ap[:, 0:256], ACT.Copy, scale=0.125), m)
            a2 = V(lambda e, b=b, t=t: e.tensor_copy(
                va[:, t, :, 0:64], b.ap[:, 256:512].rearrange("p (h d) -> p h d", h=4)), m, a1)
            b.free = [a2]
            b = rb.take()
            m = PE(mm_group(b.ap[:, 0:272], [(xnT[:, k, cols], w6[:, k, :]) for k in range(8)]), tw6, b.free)
            s6.free = [m]
            a3 = A(lambda e, b=b, t=t: e.activation(graw[:, t % 2, 0:272], b.ap[:, 0:272], ACT.Copy), m, prev[t % 2])
            b.free = [a3]
            b = rb.take()
            tr = PE(transposes(
                [(b.ap[:, j * 128:(j + 1) * 128], graw[:, t % 2, j * 128:(j + 1) * 128]) for j in range(2)] +
                [(b.ap[:, (2 + j) * 128:(3 + j) * 128], kc[:, t, j * 128:(j + 1) * 128]) for j in range(2)],
                ident), a1, a3, b.free)
            o = V(lambda e, b=b, cols=cols: e.tensor_copy(qkT[:, :, cols], b.ap.rearrange("p (g t) -> p g t", g=4)), tr)
            b.free = [o]
            b = rb.take()
            tr = PE(transposes([(b.ap[0:4, j * 128:(j + 1) * 128], graw[:, t % 2, 256 + 4 * j:260 + 4 * j])
                                for j in range(4)], ident), b.free)
            prev[t % 2] = tr
            o = A(lambda e, b=b, cols=cols: e.activation(
                LIF[0:4, :, cols], b.ap[0:4, :].rearrange("p (g t) -> p g t", g=4), ACT.Copy), tr)
            b.free = [o]
        barrier()
        at[0] = top
        B_ = alloc(T)
        M_ = alloc(T)
        Wd = alloc(T)
        NM = alloc(T)
        stack = alloc(T)
        rst = alloc(T)
        HF = alloc(NT, 256)
        assert at[0] <= top + 8 * T
        at[0] = keep + NT * 256 + NT * 260 + 4 * T + 2 * 288 + 4 * T
        colq1 = alloc(NT, 128)
        colq = colq1.unsqueeze(1).broadcast_to([128, 2, NT, 128])
        mneg = alloc(2, 512)
        gh = alloc(256)
        C0 = alloc(2, 130)
        kw = alloc(2, 256)
        NMx = B_[:, 0:1024].rearrange("p (a b) -> p a b", a=2)
        dec1 = B_[:, 1024:1024 + 2 * NT].rearrange("p (c j) -> p c j", j=2)
        dec = dec1.unsqueeze(1).broadcast_to([128, 2, NT, 2])
        st = B_[:, 1100:1132].rearrange("p (a b) -> p a b", a=2)
        Dm = stack[:, 0:1024].rearrange("p (a b) -> p a b", a=2)
        nd = graw.rearrange("p a b -> p (a b)")[:, 0:520].rearrange("p (a b) -> p a b", a=2)
        bar = [q.last() for q in (PE, V, A, G)]
        t_m = [load(mneg[:, 0, :], I["k_mneg"][0], bar), load(mneg[:, 1, :], I["k_mneg"][1], bar)]
        t_gh = load(gh, I["g_head"][l].partition_broadcast(128), bar)
        t_rst = load(rst[0:4, :], I["k_rst"][0:4, :], bar)
        a = None
        for j in range(4):
            a = V(lambda e, j=j: e.tensor_scalar(LIF[0:4, j, :], LIF[0:4, j, :], gb4[:, j:j + 1], None, ALU.add), dgb)
            if j >= 2:
                x_ = LIF[0:4, j, :]
                a1 = A(lambda e, x_=x_: e.activation(B_[0:4, :], x_, ACT.Abs), a)
                a1 = A(lambda e: e.activation(B_[0:4, :], B_[0:4, :], ACT.Exp, scale=-1.0), a1)
                a1 = A(lambda e: e.activation(B_[0:4, :], B_[0:4, :], ACT.Ln, bias=1.0), a1)
                a = V(lambda e, x_=x_: e.tensor_scalar(x_, x_, 0.0, None, ALU.min), a1)
                a = V(lambda e, x_=x_: e.tensor_tensor(x_, x_, B_[0:4, :], ALU.subtract), a, a1)
                barrier()
        barrier()
        zs = V(lambda e: e.memset(stack, 0.0))
        hprev = [None] * NT
        for d in range(2):
            LI, LF = LIF[0:4, d, :], LIF[0:4, 2 + d, :]
            seg = [(0, NC_T * 128), (NC_T * 128, T)]

            def view(ap, a_, b_, d=d):
                v = ap[:, a_:b_]
                return v[:, ::-1] if d else v
            init = 0.0
            tok = [t_rst]
            for a_, b_ in seg:
                tok.append(V(lambda e, a_=a_, b_=b_: e.tensor_tensor_scan(
                    view(B_[0:4, :], a_, b_), rst[0:4, a_:b_], view(LF, a_, b_), 0.0, ALU.mult, ALU.add), t_rst))
                tok.append(V(lambda e, a_=a_, b_=b_, init=init: e.tensor_tensor_scan(
                    view(M_[0:4, :], a_, b_), view(LF, a_, b_), view(LI, a_, b_), init, ALU.add, ALU.max), tok))
                init = M_[0:4, a_:a_ + 1] if d else M_[0:4, b_ - 1:b_]
            a = V(lambda e: e.tensor_tensor(Wd[0:4, :], LI, B_[0:4, :], ALU.subtract), tok)
            a1 = V(lambda e: e.tensor_tensor(NM[0:4, :], B_[0:4, :], M_[0:4, :], ALU.subtract), a)
            order = list(range(NT)) if d == 0 else list(range(NC_T))[::-1] + list(range(NC_T, NT))[::-1]
            pr = None
            a1 = [a1, zs]
            for c in order:
                cs = slice(c * 128, (c + 1) * 128)
                end = c * 128 if d else c * 128 + 127
                if pr is None:
                    a1.append(V(lambda e, cs=cs: e.tensor_copy(stack[0:4, cs], NM[0:4, cs]), a1))
                else:
                    pe_ = pr * 128 if d else pr * 128 + 127
                    a1.append(V(lambda e, cs=cs, pe_=pe_: e.tensor_scalar(
                        stack[0:4, cs], NM[0:4, cs], M_[0:4, pe_:pe_ + 1], None, ALU.add), a1))
                a1.append(V(lambda e, cs=cs, end=end: e.tensor_scalar(
                    stack[64:68, cs], Wd[0:4, cs], NM[0:4, end:end + 1], None, ALU.add), a1))
                pr = c
            a1.append(V(lambda e: e.tensor_scalar(stack[32:36, :], M_[0:4, :], -1.0, None, ALU.mult), a1))
            ends = stack[0:4, :].rearrange("p (c t) -> p c t", c=NT)[:, :, 0 if d else 127]
            dx = NMx[0:4, 0, 0:NT * 4].rearrange("p (c h) -> p c h", c=NT)
            a = V(lambda e: e.tensor_tensor(dx, bc(ends, 4), mid(ident[0:4, 0:4], NT), ALU.mult), a1)
            b = rb.take()

            def fn(e, b=b):
                bb = b.ap[:, 0:2 * NT].rearrange("p (c j) -> p c j", j=2)
                x4 = dx.rearrange("p c (j i) -> p c j i", i=2)
                e.matmul(bb, bsel[0:4, :], x4[:, :, :, 0], start=True, stop=False)
                return e.matmul(bb, bsel[0:4, :], x4[:, :, :, 1], start=False, stop=True)
            m = PE(fn, a, t_bsel, b.free)
            t_dec = A(lambda e, b=b, d=d: e.activation(dec[:, d, :, :], b.ap[:, 0:2 * NT].rearrange(
                "p (c j) -> p c j", j=2), ACT.Exp), m)
            b.free = [t_dec]
            cq = []
            for c0 in range(0, NT, 4):
                n = min(4, NT - c0)
                b = rb.take()
                tr = PE(transposes([(b.ap[:, j * 128:(j + 1) * 128], stack[:, (c0 + j) * 128:(c0 + j + 1) * 128])
                                    for j in range(n)], ident), a1, b.free)
                o = A(lambda e, b=b, c0=c0, n=n, d=d: e.activation(
                    colq[:, d, c0:c0 + n, :], b.ap[:, 0:n * 128].rearrange("p (c t) -> p c t", c=n), ACT.Exp), tr)
                b.free = [o]
                cq.append(o)
            zc = V(lambda e: e.memset(C0, 0.0))
            cst = [zc]
            fD = [cq, cq]
            fkw = [None, None]
            fnd = [None, None]
            fx = [a, a]
            fst = [None, None]
            for n_, c in enumerate(order):
                i = n_ % 2
                cs = slice(c * 128, (c + 1) * 128)
                C3 = C0[:, i, :].rearrange("p (j n) -> p j n", j=2)
                Cn = C0[:, 1 - i, :].rearrange("p (j n) -> p j n", j=2)
                cur = list(cst)
                reads = []
                if emit_ctx or c >= NC_T:
                    nx = NMx[0:4, i, :].rearrange("p (h t) -> p h t", h=4)
                    a = V(lambda e, nx=nx, cs=cs: e.tensor_tensor(nx, mid(NM[0:4, cs], 4), sel4[0:4], ALU.mult),
                          fx[i], t_sel, m)
                    b = rb.take()

                    def fn(e, b=b, cs=cs, i=i):
                        e.matmul(b.ap, Wd[0:4, cs], sel4[0:4].rearrange("p h t -> p (h t)"), start=True, stop=False)
                        return e.matmul(b.ap, ones[0:4, 0:128], NMx[0:4, i, :], start=False, stop=True)
                    mA = PE(fn, a, b.free)
                    fx[i] = mA
                    a = V(lambda e, b=b, i=i, d=d: e.tensor_tensor(Dm[:, i, :], b.ap, mneg[:, d, :], ALU.min),
                          mA, t_m, fD[i])
                    b.free = [a]
                    a = A(lambda e, i=i: e.activation(Dm[:, i, :], Dm[:, i, :], ACT.Exp), a)
                    bs = [rb.take(), rb.take()]
                    prods = []
                    for r in range(2):
                        p, b = 64 * r, bs[r]

                        def fn(e):
                            for j in range(2):
                                ins = e.matmul(b.ap[:, j * 128:(j + 1) * 128], qkT[p:p + 64, 2 + j, cs],
                                               qkT[p:p + 64, j, cs], start=True, stop=True)
                            return ins
                        mS = PE(fn, b.free)
                        D4 = Dm[:, i, :].rearrange("p (j r t) -> p j r t", j=2, r=2)[:, :, r, :]
                        prods.append(V(lambda e: e.tensor_tensor(
                            D4, b.ap[:, 0:256].rearrange("p (j t) -> p j t", j=2), D4, ALU.mult), mS, a))
                        b.free = [prods[-1]]
                    a = prods
                    b = rb.take()

                    def fn(e, b=b, i=i, c=c):
                        for h in range(4):
                            ins = e.matmul(b.ap[:, h * 65:h * 65 + 65], Dm[:, i, h * 128:(h + 1) * 128],
                                           va[:, c, h, :], start=True, stop=True)
                        return ins
                    mO = PE(fn, a, on, b.free)
                    fD[i] = mO
                    n3 = nd[:, i, :].rearrange("p (h n) -> p h n", h=4)
                    n4 = nd[:, i, :].rearrange("p (j r n) -> p j r n", j=2, r=2)
                    s_ = st[:, i, :]
                    prods = []
                    for r in range(2):
                        p, b2 = 64 * r, rb.take()

                        def fn(e):
                            for j in range(2):
                                ins = e.matmul(b2.ap[:, j * 65:j * 65 + 65], qkT[p:p + 64, j, cs],
                                               C3[p:p + 64, j, :], start=True, stop=True)
                            return ins
                        mI = PE(fn, cur, b2.free)
                        reads.append(mI)
                        g2 = colq[:, d, c, 0:4].rearrange("p (j r) -> p j r", r=2)[:, :, r]
                        prods.append(V(lambda e: e.tensor_tensor(
                            n4[:, :, r, :], b2.ap[:, 0:130].rearrange("p (j n) -> p j n", j=2), bc(g2, 65),
                            ALU.mult), mI, cq, fnd[i]))
                        b2.free = [prods[-1]]
                    a = prods
                    a = V(lambda e, b=b, i=i: e.tensor_tensor(nd[:, i, :], b.ap[:, 0:260], nd[:, i, :], ALU.add), a, mO)
                    b.free = [a]
                    a = V(lambda e, n3=n3, s_=s_: e.tensor_scalar(s_[:, 0:4], n3[:, :, 64], -1.0, None, ALU.mult), a)
                    a = V(lambda e, n3=n3, s_=s_: e.tensor_tensor(s_[:, 0:4], s_[:, 0:4], n3[:, :, 64], ALU.max), a)
                    a = V(lambda e, s_=s_, d=d, c=c: e.tensor_tensor(s_[:, 0:4], s_[:, 0:4], colq[:, d, c, 32:36], ALU.max), a)
                    a = V(lambda e, s_=s_: e.reciprocal(s_[:, 0:4], s_[:, 0:4]), a)
                    H3 = HF[:, c, :].rearrange("p (h n) -> p h n", h=4)
                    if d == 0:
                        a = V(lambda e, H3=H3, n3=n3, s_=s_: e.tensor_tensor(H3, n3[:, :, 0:64], bc(s_[:, 0:4], 64), ALU.mult), a)
                        hprev[c] = a
                    else:
                        a = V(lambda e, n3=n3, s_=s_: e.tensor_tensor(n3[:, :, 0:64], n3[:, :, 0:64], bc(s_[:, 0:4], 64), ALU.mult), a)
                        a = V(lambda e, H3=H3, n3=n3: e.tensor_tensor(H3, n3[:, :, 0:64], H3, ALU.add), a, hprev[c])
                        a = V(lambda e, H3=H3, n3=n3: e.tensor_tensor(n3[:, :, 0:64], H3, H3, ALU.mult), a)
                        a = V(lambda e, n3=n3, s_=s_: e.tensor_reduce(s_[:, 4:8], n3[:, :, 0:64], AX, ALU.add), a)
                        a = rstd_of(s_[:, 4:8], s_[:, 4:8], 1.0 / 64, a)
                        a = V(lambda e, H3=H3, s_=s_: e.tensor_tensor(H3, H3, bc(s_[:, 4:8], 64), ALU.mult), a)
                        a = G(lambda e, c=c: e.tensor_tensor(HF[:, c, :], HF[:, c, :], gh, ALU.mult), a, t_gh)
                        a = G(lambda e, c=c: e.tensor_tensor(Y[:, c, 768:1024], HF[:, c, :], Y[:, c, 768:1024], ALU.mult), a)
                    fnd[i] = a
                if n_ == len(order) - 1:
                    continue
                k3 = kc[:, c, :].rearrange("p (h n) -> p h n", h=4)
                kw3 = kw[:, i, :].rearrange("p (h n) -> p h n", h=4)
                a = G(lambda e, k3=k3, kw3=kw3, d=d, c=c: e.tensor_tensor(kw3, k3, bc(colq[:, d, c, 64:68], 64), ALU.mult),
                      cq, fkw[i])
                b = rb.take()

                def fn(e, b=b, kw3=kw3, c=c):
                    for h in range(4):
                        p = 64 * (h % 2)
                        j = h // 2
                        ins = e.matmul(b.ap[p:p + 64, j * 65:j * 65 + 65], kw3[:, h, :], va[:, c, h, :],
                                       start=True, stop=True)
                    return ins
                mC = PE(fn, a, on, b.free)
                fkw[i] = mC
                dd = dec[:, d, c, :]
                a = V(lambda e, Cn=Cn, C3=C3, dd=dd: e.tensor_tensor(Cn, C3, bc(dd, 65), ALU.mult), cur, t_dec, fst[i])
                a = V(lambda e, Cn=Cn, b=b: e.tensor_tensor(
                    Cn, b.ap[:, 0:130].rearrange("p (j n) -> p j n", j=2), Cn, ALU.add), a, mC)
                b.free = [a]
                fst[1 - i] = reads
                cst = [a]
            barrier()
        at[0] = top
        yT = alloc(8, T)
        at[0] = keep
        gtr = alloc(2, 1024)
        xr = alloc(2, 1024)
        xo = alloc(2, 1024)
        sq = alloc(1024)
        ss = alloc(4)
        gf = alloc(1024)
        bar = [q.last() for q in (PE, V, A, G)]
        last_layer = l == DEPTH - 1
        t_gf = load(gf, I["g_final"].partition_broadcast(128), bar) if last_layer else None
        tg_ = [row_broadcast(gtr[:, v, :], MOD[:, 16:24, v], 8) for v in range(2)]
        for t in range(t0, NT):
            tt = to_feature(Y[:, t, :], yT, t, None, None)
        wo = [wload(I["w_out"][l][g], 512) for g in range(2)]
        fr = [None, None]
        fo = [None, None]
        new_store = []
        for t in range(t0, NT):
            i = t % 2
            cols = slice(t * 128, (t + 1) * 128)
            lx = SP.dma(ch_x[i], lambda e, t=t, i=i: e.dma_start(xr[:, i, :], rows[t]), bar, fr[i])
            v = 1 if t < NC_T else 0
            toks = []
            for g in range(2):
                w, tw, s_ = wo[g]
                b = rb.take()
                m = PE(mm_group(b.ap, [(yT[:, k, cols], w[:, k, :]) for k in range(8)]), tw, b.free, tt)
                s_.free = [m]
                gs = slice(g * 512, (g + 1) * 512)
                a = V(lambda e, b=b, i=i, gs=gs, v=v: e.tensor_tensor(xo[:, i, gs], b.ap, gtr[:, v, gs], ALU.mult),
                      m, tg_, fo[i])
                b.free = [a]
                toks.append(V(lambda e, i=i, gs=gs: e.tensor_tensor(xo[:, i, gs], xo[:, i, gs], xr[:, i, gs], ALU.add),
                              a, lx))
            fr[i] = toks
            if not last_layer:
                st_ = SP.dma(ch_o[i], lambda e, t=t, i=i: e.dma_start(X1[t * 128:(t + 1) * 128, :], xo[:, i, :]), toks)
                x1_store[t] = st_
            else:
                a = A(lambda e, i=i: e.activation(sq, xo[:, i, :], ACT.Square, accum_out=ss[:, i:i + 1]), toks)
                a = rstd_of(ss[:, i:i + 1], ss[:, i:i + 1], 1.0 / 1024, a)
                a = V(lambda e, i=i: e.scalar_tensor_tensor(xo[:, i, :], xo[:, i, :], ss[:, i:i + 1], gf,
                                                            ALU.mult, ALU.mult), a, t_gf)
                st_ = SP.dma(ch_o[i], lambda e, t=t, i=i: e.dma_start(
                    X2[(t - NC_T) * 128:(t - NC_T + 1) * 128, :], xo[:, i, :]), a)
                x2_store[t - NC_T] = st_
            fo[i] = st_
            new_store.append(st_)
        phase = barrier() + [x for x in fo if x is not None]


    def recip_sig(dst, src, *after):
        a = A(lambda e: e.activation(dst, src, ACT.Exp, scale=-1.0), *after)
        a = V(lambda e: e.tensor_scalar(dst, dst, 1.0, None, ALU.add), a)
        return V(lambda e: e.reciprocal(dst, dst), a)

    at[0] = top
    MOD = alloc(48, 2)
    AM = alloc(8, 2)
    AF = alloc(8)
    lmask = alloc(8, 128)
    xnT = alloc(8, T)
    OT = alloc(8, 1024)
    work = at[0]
    Yc = alloc(8, 1024)
    ret_work = at[0]
    at[0] = work
    X = alloc(NT, 1024)
    cvec = alloc(8, 2)
    ctmp = alloc(8, 2)
    bada = alloc(48)
    gn = alloc(8)
    nf = alloc(8)
    tb = load(bada, I["b_ada2"], phase)
    tg = load(gn, I["norm_mix"], phase)
    tn = load(nf, I["norm_ffn"], phase)
    tlm = load(lmask, I["k_lmask"], phase)
    tc = silu_c(cvec, ctmp, I["c2"], phase)
    tm = modulation(I["w_ada2"], 12, cvec, [tc, tb], MOD, bada)
    tm = V(lambda e: e.tensor_scalar(AM, MOD[:, 8:16, :], 1.0, None, ALU.add), tm)
    tm = V(lambda e: e.tensor_tensor(AM, AM, bc(gn, 2), ALU.mult), tm, tg)
    ta = V(lambda e: e.tensor_scalar(AF, MOD[:, 32:40, 0], 1.0, None, ALU.add), tm)
    ta = V(lambda e: e.tensor_tensor(AF, AF, nf, ALU.mult), ta, tn)
    rows = [I["ctx2"][t * 128:(t + 1) * 128, :] for t in range(NC_T)] + \
           [X2[t * 128:(t + 1) * 128, :] for t in range(NL_T)]
    normalise_in(X, xnT, rows, AM, MOD[:, 0:8, :], tm, phase, x2_store)
    barrier()

    at[0] = work
    Vt = alloc(NT, 256)
    LRT = alloc(T)
    WLR = alloc(2, 128)
    qT = alloc(NL_T * 128)
    kT = alloc(T)
    bf = alloc(T)
    bb = alloc(T)
    E = alloc(T)
    KDT = alloc(NT, 128)
    Sb = alloc(NT, 256)
    Sf = alloc(2, 256)
    QF = alloc(2, 512)
    QK = alloc(2, 2, 512)
    acc = alloc(2, 512)
    tm_ = alloc(2, 256)
    gg = alloc(2, 256)
    gnr = alloc(256)
    bz = alloc(8)
    dec = alloc(2, NT)
    one = alloc(128)
    st = alloc(8)
    bar = [q.last() for q in (PE, V, A, G)]
    wl, twl, sl = wload(I["w_lr"], 32)
    t_bz = load(bz, I["lr_b"], bar)
    t_gn = load(gnr, I["gla_norm"].partition_broadcast(128), bar)
    t_one = V(lambda e: e.memset(one, 1.0))
    for t in range(NT):
        cols = slice(t * 128, (t + 1) * 128)
        i = t % 2
        b = rb.take()
        m = PE(mm_group(b.ap[:, 0:32], [(xnT[:, k, cols], wl[:, k, :]) for k in range(8)]), twl, b.free)
        sl.free = [m]
        c = A(lambda e: e.activation(tm_[:, i, 0:32], b.ap[:, 0:32], ACT.Copy), m, A.last(), PE.last())
        b.free = [c]
        b = rb.take()
        tr = PE(transposes([(b.ap[0:32, 0:128], tm_[:, i, 0:32])], ident), c, b.free)
        o = A(lambda e: e.activation(LRT[0:32, cols], b.ap[0:32, 0:128], ACT.Copy), tr)
        b.free = [o]
    for h in range(4):
        barrier()
        t_wl = load(WLR[0:32], I["gla_lr"][h], [q.last() for q in (PE, V, A, G)])
        w, tw, s_ = wload(I["w_gla"][h], 512)
        wg, twg, sg_ = wload(I["w_gg"][h], 256)
        tg = None
        for d, b_ in ((0, bf), (1, bb)):
            zs = []
            for c0 in range(0, T, 512):
                n = min(512, T - c0)
                b = rb.take()
                m = PE(lambda e: e.matmul(b.ap[:, 0:n], WLR[0:32, d, :], LRT[0:32, c0:c0 + n],
                                          start=True, stop=True), t_wl, b.free)
                o = A(lambda e: e.activation(b_[:, c0:c0 + n], b.ap[:, 0:n], ACT.Identity,
                                             bias=bz[:, 4 * d + h:4 * d + h + 1]), m, t_bz)
                b.free = [o]
                zs.append(o)
            a = A(lambda e: e.activation(E, b_, ACT.Abs), zs, tg)
            a = A(lambda e: e.activation(E, E, ACT.Exp, scale=-1.0), a)
            a = A(lambda e: e.activation(E, E, ACT.Ln, bias=1.0), a)
            a1 = V(lambda e: e.tensor_scalar(b_, b_, 0.0, 0.0625, ALU.min, ALU.mult), a)
            tg = V(lambda e: e.scalar_tensor_tensor(E, E, -0.0625, b_, ALU.mult, ALU.add), a1)
            sc = []
            for c in range(NT):
                v_ = b_[:, c * 128:(c + 1) * 128]
                e_ = E[:, c * 128:(c + 1) * 128]
                if d:
                    v_, e_ = v_[:, ::-1], e_[:, ::-1]
                sc.append(V(lambda e: e.tensor_tensor_scan(v_, one, e_, 0.0, ALU.mult, ALU.add), tg, t_one))
            tg = sc
        tgate = tg
        qk_t = []
        prev = [None, None]
        for t in range(NT):
            cols = slice(t * 128, (t + 1) * 128)
            i = t % 2
            lat = t >= NC_T
            c0 = 0 if lat else 128
            b = rb.take()
            m = PE(mm_group(b.ap[:, c0:512], [(xnT[:, k, cols], w[:, k, c0:512]) for k in range(8)]), tw, b.free)
            s_.free = [m]
            a1 = A(lambda e: e.activation(Vt[:, t, :], b.ap[:, 256:512], ACT.Copy), m)
            a2 = [A(lambda e: e.activation(tm_[:, i, 128:256], b.ap[:, 128:256], ACT.Copy), m, prev[i])]
            if lat:
                a2.append(A(lambda e: e.activation(tm_[:, i, 0:128], b.ap[:, 0:128], ACT.Copy,
                                                   scale=float(128 ** -0.5)), m, prev[i]))
            b.free = [a1, a2]
            b = rb.take()
            tr = PE(transposes([(b.ap[:, c0:c0 + 128], tm_[:, i, c0:c0 + 128])] +
                               ([(b.ap[:, 128:256], tm_[:, i, 128:256])] if lat else []), ident), a2, b.free)
            prev[i] = tr
            o = [V(lambda e: e.tensor_copy(kT[:, cols], b.ap[:, 128:256]), tr)]
            if lat:
                qc = slice((t - NC_T) * 128, (t - NC_T + 1) * 128)
                o.append(V(lambda e: e.tensor_copy(qT[:, qc], b.ap[:, 0:128]), tr))
            b.free = o
            qk_t += o
        def decayed_keys(d, b_, *after):
            e3 = E.rearrange("p (c t) -> p c t", c=NT)
            b3 = b_.rearrange("p (c t) -> p c t", c=NT)
            end = b3[:, :, 0] if d else b3[:, :, 127]
            a0 = A(lambda e: e.activation(dec[:, d, :], end, ACT.Exp), *after)
            a = V(lambda e: e.tensor_tensor(e3, bc(end, 128), b3, ALU.subtract), *after)
            a = A(lambda e: e.activation(E, E, ACT.Exp), a)
            a = V(lambda e: e.tensor_tensor(E, E, kT, ALU.mult), a)
            outs = [a0]
            for c0 in range(0, NT, 4):
                n = min(4, NT - c0)
                b = rb.take()
                tr = PE(transposes([(b.ap[:, j * 128:(j + 1) * 128], e3[:, c0 + j, :]) for j in range(n)], ident),
                        a, b.free)
                o = A(lambda e: e.activation(KDT[:, c0:c0 + n, :], b.ap[:, 0:n * 128].rearrange(
                    "p (c t) -> p c t", c=n), ACT.Copy), tr, *after)
                b.free = [o]
                outs.append(o)
            return outs

        def next_state(dst, src, d, c, *after):
            b = rb.take()
            m = PE(lambda e: e.matmul(b.ap[:, 0:256], KDT[:, c, :], Vt[:, c, :], start=True, stop=True), b.free, *after)
            a = V(lambda e: e.scalar_tensor_tensor(dst, src, dec[:, d, c:c + 1], b.ap[:, 0:256],
                                                   ALU.mult, ALU.add), m, *after)
            b.free = [a]
            return a
        barrier()
        kd = decayed_keys(1, bb)
        order = list(range(NC_T))[::-1] + list(range(NC_T, NT))[::-1]
        a = V(lambda e: e.memset(Sb[:, order[0], :], 0.0))
        for n_ in range(NT - 1):
            a = next_state(Sb[:, order[n_ + 1], :], Sb[:, order[n_], :], 1, order[n_], kd, a)
        barrier()
        kd = decayed_keys(0, bf)
        a = V(lambda e: e.memset(Sf[:, 0, :], 0.0))
        for c in range(NC_T):
            a = next_state(Sf[:, (c + 1) % 2, :], Sf[:, c % 2, :], 0, c, kd, a)
        barrier()
        sft = a
        for half in range(2):
            ls = NC_T * 128 + half * 512
            qs_ = half * 512
            bfh, bbh = bf[:, ls:ls + 512], bb[:, ls:ls + 512]
            qh, kh = qT[:, qs_:qs_ + 512], kT[:, ls:ls + 512]
            ac = acc[:, half, :]
            ac3 = ac.rearrange("p (c t) -> p c t", c=4)

            def scores(qq, kk, *after):
                b = rb.take()

                def fn(e):
                    for c in range(4):
                        ins = e.matmul(b.ap[:, c * 128:(c + 1) * 128], kk[:, c * 128:(c + 1) * 128],
                                       qq[:, c * 128:(c + 1) * 128], start=True, stop=True)
                    return ins
                return b, PE(fn, b.free, *after)
            b, m = scores(qh, kh)
            a = V(lambda e: e.tensor_tensor(ac3, b.ap.rearrange("p (c t) -> p c t", c=4),
                                            lmask[:, 7, :].unsqueeze(1).broadcast_to([128, 4, 128]), ALU.mult), m, tlm)
            b.free = [a]
            last_acc = a
            fq = [None, None]
            for n_, L in enumerate(LEVELS):
                nb = 512 // (2 * L)
                i = n_ % 2
                f4 = bfh.rearrange("p (n s l) -> p n s l", s=2, l=L)
                b4 = bbh.rearrange("p (n s l) -> p n s l", s=2, l=L)
                aq = QK[:, i, 0, :]
                ak = QK[:, i, 1, :]
                q4 = aq.rearrange("p (n s l) -> p n s l", s=2, l=L)
                k4 = ak.rearrange("p (n s l) -> p n s l", s=2, l=L)
                rf = f4[:, :, 0, L - 1:L].broadcast_to([128, nb, L])
                rb_ = b4[:, :, 1, 0:1].broadcast_to([128, nb, L])
                o1 = V(lambda e: e.tensor_tensor(q4[:, :, 1, :], f4[:, :, 1, :], rf, ALU.subtract), fq[i])
                o2 = G(lambda e: e.tensor_tensor(q4[:, :, 0, :], b4[:, :, 0, :], rb_, ALU.subtract), fq[i])
                o3 = V(lambda e: e.tensor_tensor(k4[:, :, 0, :], rf, f4[:, :, 0, :], ALU.subtract), fq[i])
                o4 = G(lambda e: e.tensor_tensor(k4[:, :, 1, :], rb_, b4[:, :, 1, :], ALU.subtract), fq[i])
                a = A(lambda e: e.activation(QK[:, i, :, :], QK[:, i, :, :], ACT.Exp), o1, o2, o3, o4)
                o1 = G(lambda e: e.tensor_tensor(aq, aq, qh, ALU.mult), a)
                o2 = V(lambda e: e.tensor_tensor(ak, ak, kh, ALU.mult), a)
                b, m = scores(aq, ak, o1, o2)
                fq[i] = m
                a = V(lambda e: e.copy_predicated(
                    ac3, lmask[:, n_, :].bitcast(mybir.dt.int32).unsqueeze(1).broadcast_to([128, 4, 128]),
                    b.ap.rearrange("p (c t) -> p c t", c=4)), m, last_acc)
                b.free = [a]
                last_acc = a
            a1 = A(lambda e: e.activation(QF[:, 0, :], bfh, ACT.Exp), PE.last())
            a1 = G(lambda e: e.tensor_tensor(QF[:, 0, :], QF[:, 0, :], qh, ALU.mult), a1)
            a2 = A(lambda e: e.activation(QF[:, 1, :], bbh, ACT.Exp), PE.last())
            a2 = G(lambda e: e.tensor_tensor(QF[:, 1, :], QF[:, 1, :], qh, ALU.mult), a2)
            prev = [None, None]
            for cc in range(4):
                c = NC_T + half * 4 + cc
                i = c % 2
                cs = slice(cc * 128, (cc + 1) * 128)
                ts = slice((c - NC_T) * 128, (c - NC_T + 1) * 128)
                xs = slice(c * 128, (c + 1) * 128)
                cur = Sf[:, c % 2, :]
                b = rb.take()

                def fn(e):
                    e.matmul(b.ap[:, 0:256], ac[:, cs], Vt[:, c, :], start=True, stop=False)
                    e.matmul(b.ap[:, 0:256], QF[:, 0, cs], cur, start=False, stop=False)
                    return e.matmul(b.ap[:, 0:256], QF[:, 1, cs], Sb[:, c, :], start=False, stop=True)
                mo = PE(fn, last_acc, a1, a2, sft, b.free)
                if c < NT - 1:
                    sft = next_state(Sf[:, (c + 1) % 2, :], cur, 0, c, kd, sft, mo)
                b2 = rb.take()
                m = PE(mm_group(b2.ap[:, 0:256], [(xnT[:, k, xs], wg[:, k, :]) for k in range(8)]), twg, b2.free)
                sg_.free = [m]
                g_ = gg[:, i, :]
                a = recip_sig(g_, b2.ap[:, 0:256], m, prev[i])
                ag = V(lambda e: e.tensor_tensor(g_, b2.ap[:, 0:256], g_, ALU.mult), a)
                b2.free = [ag]
                ag = G(lambda e: e.tensor_tensor(g_, g_, gnr, ALU.mult), ag, t_gn)
                s1 = st[:, i:i + 1]
                a = A(lambda e: e.activation(tm_[:, i, :], b.ap[:, 0:256], ACT.Square, accum_out=s1), mo, prev[i])
                a = rstd_of(s1, s1, 1.0 / 256, a)
                a = V(lambda e: e.scalar_tensor_tensor(tm_[:, i, :], b.ap[:, 0:256], s1, g_, ALU.mult, ALU.mult), a, ag)
                b.free = [a]
                b = rb.take()
                tr = PE(transposes([(b.ap[:, j * 128:(j + 1) * 128], tm_[:, i, j * 128:(j + 1) * 128])
                                    for j in range(2)], ident), a, b.free)
                o = A(lambda e: e.activation(OT[:, 2 * h:2 * h + 2, ts], b.ap[:, 0:256].rearrange(
                    "p (j t) -> p j t", j=2), ACT.Copy), tr)
                b.free = [o]
                prev[i] = [tr, o]

    def merge(name, first):
        barrier()
        at[0] = ret_work
        sg2 = alloc(2, 512)
        fr = [None, None]
        for g in range(2):
            wb, twb, sb_ = wload(I[name][g], 512)
            wm, twm, sm_ = wload(I[name + "_m"][g], 512)
            for t in range(NL_T):
                i = t % 2
                b1, b2 = rb.take(), rb.take()
                m2 = PE(mm_group(b2.ap, [(xnT[:, k, (NC_T + t) * 128:(NC_T + t + 1) * 128], wm[:, k, :])
                                         for k in range(8)]), twm, b2.free)
                m1 = PE(mm_group(b1.ap, [(OT[:, k, t * 128:(t + 1) * 128], wb[:, k, :]) for k in range(8)]),
                        twb, b1.free)
                sb_.free, sm_.free = [m1], [m2]
                a = recip_sig(sg2[:, i, :], b2.ap, m2, fr[i])
                b2.free = [a]
                y_ = Yc[:, t, g * 512:(g + 1) * 512]
                if first:
                    a = V(lambda e: e.tensor_tensor(y_, b1.ap, sg2[:, i, :], ALU.mult), a, m1)
                    b1.free = [a]
                else:
                    a = V(lambda e: e.tensor_tensor(sg2[:, i, :], b1.ap, sg2[:, i, :], ALU.mult), a, m1)
                    b1.free = [a]
                    a = G(lambda e: e.tensor_tensor(y_, y_, sg2[:, i, :], ALU.add), a)
                fr[i] = a
        barrier()

    merge("w_bg", True)

    at[0] = ret_work
    Vt = alloc(NT, 256)
    KD = alloc(NT, 2, 128)
    qT = alloc(NL_T * 128)
    kT = alloc(T)
    rope = alloc(2, 256)
    rdm = alloc(128)
    rqd = alloc(2, 128)
    rkd = small[:, 0:16]
    Sb = alloc(NL_T, 256)
    Sf = alloc(2, 256)
    lm = lmask.rearrange("p a b -> p (a b)")
    tm_ = lm[:, 0:512].rearrange("p (a b) -> p a b", a=2)
    tz, ty = lm[:, 512:768], lm[:, 768:1024]
    gg = alloc(2, 256)
    acc = alloc(2, 128)
    QF = alloc(2, 256)
    st = small[:, 16:32]
    bar = [q.last() for q in (PE, V, A, G)]
    t_rk = load(rkd, I["k_rkd"], bar)
    rope_ch = [chan(f"d_rope{i}") for i in range(2)]
    for h in range(4):
        barrier()
        bar = [q.last() for q in (PE, V, A, G)]
        t_dm = load(rdm, I["k_rdm"][:, h, :], bar)
        t_qd = load(rqd, I["k_rqd"][:, :, h, :], bar)
        w, tw, s_ = wload(I["w_ret"][h], 512)
        wg, twg, sg_ = wload(I["w_rg"][h], 256)
        prev = [None, None]
        hz = None
        for t in range(NT):
            cols = slice(t * 128, (t + 1) * 128)
            i = t % 2
            lat = t >= NC_T
            c0 = 0 if lat else 128
            if lat:
                lr = SP.dma(rope_ch[i], lambda e: e.dma_start(rope[:, i, :], I["k_rope2"][:, t - NC_T, :]), bar, prev[i])
            b = rb.take()
            m = PE(mm_group(b.ap[:, c0:512], [(xnT[:, k, cols], w[:, k, c0:512]) for k in range(8)]), tw, b.free)
            s_.free = [m]
            a2 = [A(lambda e: e.activation(tm_[:, i, 128:256], b.ap[:, 128:256], ACT.Copy,
                                           scale=float(128 ** -0.5)), m, prev[i])]
            if lat:
                a2.append(A(lambda e: e.activation(tm_[:, i, 0:128], b.ap[:, 0:128], ACT.Copy), m, prev[i]))
            a1 = V(lambda e: e.tensor_copy(Vt[:, t, :], b.ap[:, 256:512]), a2)
            b.free = [a1]
            if lat:
                x3 = tm_[:, i, :].rearrange("p (a d) -> p a d", a=2)
                y3 = ty.rearrange("p (a d) -> p a d", a=2)
                x5 = tm_[:, i, :].rearrange("p (a r s f) -> p a r s f", a=2, r=2, s=2)
                z5 = tz.rearrange("p (a r s f) -> p a r s f", a=2, r=2, s=2)
                s4 = rope[:, i, 128:256].rearrange("p (r s f) -> p r s f", r=2, s=2)
                o = [V(lambda e: e.tensor_tensor(y3, x3, mid(rope[:, i, 0:128], 2), ALU.mult), a2, lr, hz)]
                for s in range(2):
                    tb_ = s4[:, :, s, :].unsqueeze(1).broadcast_to([128, 2, 2, 32])
                    o.append(G(lambda e: e.tensor_tensor(z5[:, :, :, s, :], x5[:, :, :, 1 - s, :], tb_, ALU.mult),
                               a2, lr, hz))
                hz = V(lambda e: e.tensor_tensor(tm_[:, i, :], ty, tz, ALU.add), o)
                a2 = [hz]
            kk = [G(lambda e: e.tensor_scalar(KD[:, t, d, :], tm_[:, i, 128:256], rkd[:, 4 * d + h:4 * d + h + 1],
                                              None, ALU.mult), a2, t_rk) for d in range(2)]
            b = rb.take()
            tr = PE(transposes([(b.ap[:, 128:256], tm_[:, i, 128:256])] +
                               ([(b.ap[:, 0:128], tm_[:, i, 0:128])] if lat else []), ident), a2, b.free)
            prev[i] = [tr, kk]
            o = [A(lambda e: e.activation(kT[:, cols], b.ap[:, 128:256], ACT.Copy), tr)]
            if lat:
                qc = slice((t - NC_T) * 128, (t - NC_T + 1) * 128)
                o.append(A(lambda e: e.activation(qT[:, qc], b.ap[:, 0:128], ACT.Copy), tr))
            b.free = o

        def next_ret(dst, src, d, c, *after):
            b = rb.take()
            m = PE(lambda e: e.matmul(b.ap[:, 0:256], KD[:, c, d, :], Vt[:, c, :], start=True, stop=True), b.free, *after)
            a = V(lambda e: e.scalar_tensor_tensor(dst, src, rkd[:, 8 + 4 * d + h:9 + 4 * d + h], b.ap[:, 0:256],
                                                   ALU.mult, ALU.add), m, *after)
            b.free = [a]
            return a
        barrier()
        order = list(range(NC_T))[::-1] + list(range(NC_T, NT))[::-1]
        back = [Sf[:, 1 - c, :] if c < NC_T else Sb[:, c - NC_T, :] for c in range(NT)]
        a = V(lambda e: e.memset(back[order[0]], 0.0))
        for n_ in range(NT - 1):
            a = next_ret(back[order[n_ + 1]], back[order[n_]], 1, order[n_], a)
        a = V(lambda e: e.memset(Sf[:, 0, :], 0.0), a)
        for c in range(NC_T):
            a = next_ret(Sf[:, (c + 1) % 2, :], Sf[:, c % 2, :], 0, c, a)
        sft = a
        prev = [None, None]
        for c in range(NC_T, NT):
            i = c % 2
            ts = slice((c - NC_T) * 128, (c - NC_T + 1) * 128)
            xs = slice(c * 128, (c + 1) * 128)
            cur = Sf[:, c % 2, :]
            b = rb.take()
            m = PE(lambda e: e.matmul(b.ap[:, 0:128], kT[:, xs], qT[:, ts], start=True, stop=True), b.free)
            a1 = V(lambda e: e.tensor_tensor(acc[:, i, :], b.ap[:, 0:128], rdm, ALU.mult), m, t_dm, prev[i])
            b.free = [a1]
            q3 = QF[:, i, :].rearrange("p (d t) -> p d t", d=2)
            a2 = G(lambda e: e.tensor_tensor(q3, mid(qT[:, ts], 2), rqd, ALU.mult), t_qd, prev[i])
            b = rb.take()

            def fn(e):
                e.matmul(b.ap[:, 0:256], acc[:, i, :], Vt[:, c, :], start=True, stop=False)
                e.matmul(b.ap[:, 0:256], QF[:, i, 0:128], cur, start=False, stop=False)
                return e.matmul(b.ap[:, 0:256], QF[:, i, 128:256], Sb[:, c - NC_T, :], start=False, stop=True)
            mo = PE(fn, a1, a2, sft, b.free)
            if c < NT - 1:
                sft = next_ret(Sf[:, (c + 1) % 2, :], cur, 0, c, sft, mo)
            b2 = rb.take()
            m = PE(mm_group(b2.ap[:, 0:256], [(xnT[:, k, xs], wg[:, k, :]) for k in range(8)]), twg, b2.free)
            sg_.free = [m]
            g_ = gg[:, i, :]
            a = recip_sig(g_, b2.ap[:, 0:256], m, prev[i])
            ag = V(lambda e: e.tensor_tensor(g_, b2.ap[:, 0:256], g_, ALU.mult), a)
            b2.free = [ag]
            s1, s2 = st[:, 4 * i:4 * i + 1], st[:, 4 * i + 1:4 * i + 2]
            o_ = tm_[:, i, :]
            a = A(lambda e: e.activation(o_, b.ap[:, 0:256], ACT.Copy, accum_out=s1), mo, prev[i])
            b.free = [a]
            a = V(lambda e: e.tensor_scalar(s1, s1, -1.0 / 256, None, ALU.mult), a)
            a = V(lambda e: e.tensor_scalar(o_, o_, s1, None, ALU.add), a)
            a = A(lambda e: e.activation(ty, o_, ACT.Square, accum_out=s2), a, hz)
            hz = a
            a = rstd_of(s2, s2, 1.0 / 256, a)
            a = V(lambda e: e.scalar_tensor_tensor(o_, o_, s2, g_, ALU.mult, ALU.mult), a, ag)
            b = rb.take()
            tr = PE(transposes([(b.ap[:, j * 128:(j + 1) * 128], tm_[:, i, j * 128:(j + 1) * 128])
                                for j in range(2)], ident), a, b.free)
            o = A(lambda e: e.activation(OT[:, 2 * h:2 * h + 2, ts], b.ap[:, 0:256].rearrange(
                "p (j t) -> p j t", j=2), ACT.Copy), tr)
            b.free = [o]
            prev[i] = [tr, o, mo]

    merge("w_br", False)

    at[0] = ret_work
    gtr = alloc(1024)
    xr = alloc(2, 1024)
    sq = alloc(1024)
    ss = alloc(NL_T)
    XO = xnT.rearrange("p k t -> p (k t)")[:, 0:8192].rearrange("p (t n) -> p t n", t=8)
    bar = [q.last() for q in (PE, V, A, G)]
    tgr = row_broadcast(gtr, MOD[:, 16:24, 0], 8)
    for t in range(NL_T):
        tt = to_feature(Yc[:, t, :], OT, t, None, None)
    wo = [wload(I["w_out2"][g], 512) for g in range(2)]
    fr = [None, None]
    ssl = []
    for t in range(NL_T):
        i = t % 2
        lx = SP.dma(ch_x[i], lambda e: e.dma_start(xr[:, i, :], X2[t * 128:(t + 1) * 128, :]), bar, fr[i])
        toks = []
        for g in range(2):
            w, tw, s_ = wo[g]
            b = rb.take()
            m = PE(mm_group(b.ap, [(OT[:, k, t * 128:(t + 1) * 128], w[:, k, :]) for k in range(8)]), tw, b.free, tt)
            s_.free = [m]
            gs = slice(g * 512, (g + 1) * 512)
            a = V(lambda e: e.tensor_tensor(XO[:, t, gs], b.ap, gtr[:, gs], ALU.mult), m, tgr)
            b.free = [a]
            toks.append(V(lambda e: e.tensor_tensor(XO[:, t, gs], XO[:, t, gs], xr[:, i, gs], ALU.add), a, lx))
        fr[i] = toks
        ssl = [A(lambda e: e.activation(sq, XO[:, t, :], ACT.Square, accum_out=ss[:, t:t + 1]), toks, ssl)]
    r = rstd_of(ss, ss, 1.0 / 1024, ssl)
    barrier()
    tt = []
    hn_store = []
    for t in range(NL_T):
        q = V if t % 2 else G
        m = q(lambda e: e.tensor_scalar(Yc[:, t, :], XO[:, t, :], ss[:, t:t + 1], None, ALU.mult), r)
        hn_store.append(SP.dma(ch_x[2 + t], lambda e: e.dma_start(HN[t * 128:(t + 1) * 128, :], Yc[:, t, :]), m))
        tt += to_feature(Yc[:, t, :], OT, t, AF, MOD[:, 24:32, 0], m)

    barrier()
    at[0] = ret_work
    wr = alloc(8, 36)
    br = alloc(36)
    LG = alloc(8, 36)
    rev = alloc(36)
    Wt = alloc(8, 32)
    em = alloc(8, 32)
    em2 = alloc(8, 32)
    oh1 = alloc(8, 32)
    oh2 = alloc(8, 32)
    s8 = alloc(12, 8)
    go = alloc(8, 4)
    gx = alloc(8, 4)
    bar = [q.last() for q in (PE, V, A, G)]
    t_r = [load(wr, I["w_router"], bar), load(br, I["b_router"].partition_broadcast(128), bar),
           load(rev, I["k_rev"], bar)]
    lg = []
    for t in range(NL_T):
        b = rb.take()
        m = PE(mm_group(b.ap[:, 0:36], [(OT[:, k, t * 128:(t + 1) * 128], wr[:, k, :]) for k in range(8)]), t_r, b.free)
        a = V(lambda e: e.tensor_tensor(LG[:, t, :], b.ap[:, 0:36], br, ALU.add), m)
        b.free = [a]
        lg.append(a)
    gl = LG[:, :, 0:4]
    el = LG[:, :, 4:36]

    def red(dst, src, op, *after):
        return V(lambda e: e.tensor_reduce(dst, src, AX, op), *after)

    def tt_(dst, x_, y_, op, *after):
        return V(lambda e: e.tensor_tensor(dst, x_, y_, op), *after)

    def pick_first(oh, val, vmax, n, r_, tmp, a):
        a = tt_(oh, val, bc(vmax, n), ALU.is_equal, a)
        a = tt_(oh, oh, mid(r_, 8), ALU.mult, a)
        a = red(tmp, oh, ALU.max, a)
        return tt_(oh, oh, bc(tmp, n), ALU.is_equal, a)
    a = red(s8[:, 0, :], gl, ALU.max, lg)
    g1_ = pick_first(go, gl, s8[:, 0, :], 4, rev[:, 0:4], s8[:, 1, :], a)
    a = tt_(gx, gl, bc(s8[:, 0, :], 4), ALU.subtract, g1_)
    a = A(lambda e: e.activation(gx, gx, ACT.Exp), a)
    a = red(s8[:, 2, :], gx, ALU.add, a)
    gw = V(lambda e: e.reciprocal(s8[:, 3, :], s8[:, 2, :]), a)
    a = V(lambda e: e.tensor_scalar(go, go, -1.0, 1e30, ALU.add, ALU.mult), gw)
    em4 = em.rearrange("p t (g x) -> p (t g) x", g=4)
    el4 = em2.rearrange("p t (g x) -> p (t g) x", g=4)
    a = V(lambda e: e.tensor_copy(em2, el), a)
    a = tt_(em4, el4, bc(go.rearrange("p t g -> p (t g)"), 8), ALU.add, a)
    a = red(s8[:, 4, :], em, ALU.max, a)
    a = pick_first(oh1, em, s8[:, 4, :], 32, rev[:, 4:36], s8[:, 5, :], a)
    a = V(lambda e: e.scalar_tensor_tensor(em2, oh1, -3e30, em, ALU.mult, ALU.add), a)
    a = red(s8[:, 6, :], em2, ALU.max, a)
    a = pick_first(oh2, em2, s8[:, 6, :], 32, rev[:, 4:36], s8[:, 7, :], a)
    a = tt_(s8[:, 8, :], s8[:, 6, :], s8[:, 4, :], ALU.subtract, a)
    a = A(lambda e: e.activation(s8[:, 8, :], s8[:, 8, :], ACT.Exp), a)
    a = V(lambda e: e.tensor_scalar(s8[:, 9, :], s8[:, 8, :], 1.0, None, ALU.add), a)
    a = V(lambda e: e.reciprocal(s8[:, 9, :], s8[:, 9, :]), a)
    a = tt_(s8[:, 9, :], s8[:, 9, :], s8[:, 3, :], ALU.mult, a)
    a = tt_(s8[:, 10, :], s8[:, 9, :], s8[:, 8, :], ALU.mult, a)
    M = alloc(8, 32)
    R = alloc(8, 32)
    C = alloc(32)
    nov = alloc(32)
    ovend = alloc(32)
    ovst = alloc(32)
    zero = alloc(32)
    tri = alloc(128)
    iota = alloc(128)
    tokid = alloc(8)
    tmp = alloc(8, 32)
    pj = alloc(2, 8, 8)
    eo = alloc(NOV, 32)
    eor = alloc(2, 16)
    SL = alloc(2, 128)
    BL = alloc(2, NB)
    ints = alloc(NB + 48).bitcast(mybir.dt.int32)
    idx = ints[:, 0:NB]
    desti = ints[:, NB:NB + 16].rearrange("p (j t) -> p j t", j=2)
    eoi = ints[:, NB + 16:NB + 48]
    t_c = [load(tri, I["k_tri"], bar), load(iota, I["k_iota"], bar), load(tokid, I["k_tokid"], bar)]
    w12 = s8[:, 9:11, :]
    a = tt_(M, oh1, oh2, ALU.add, a)
    b = rb.take()

    def fn(e):
        for t in range(8):
            for u in range(t + 1):
                e.matmul(b.ap[:, t * 32:(t + 1) * 32], tri if u == t else ones, M[:, u, :],
                         start=(u == 0), stop=(u == t))
        for t in range(8):
            ins = e.matmul(b.ap[:, 256:288], ones, M[:, t, :], start=(t == 0), stop=(t == 7))
        return ins
    m = PE(fn, a, t_c, t_ones, b.free)
    a = V(lambda e: e.tensor_copy(R, b.ap[:, 0:256].rearrange("p (t x) -> p t x", t=8)), m)
    a = V(lambda e: e.tensor_copy(C, b.ap[:, 256:288]), a)
    b.free = [a]
    a = V(lambda e: e.memset(zero, 0.0), a)
    a = V(lambda e: e.memset(nov, 0.0), a)
    for k in range(1, 8):
        a = V(lambda e: e.scalar_tensor_tensor(nov, C, 128.0 * k, nov, ALU.is_gt, ALU.add), a)
    a = V(lambda e: e.tensor_tensor_scan(ovend, nov, zero, 0.0, ALU.add, ALU.add), a)
    a = tt_(ovst, ovend, nov, ALU.subtract, a)
    a = tt_(eo[0:1], ovend[0:1, :].unsqueeze(1).broadcast_to([1, NOV, 32]), bc(iota[0:1, 0:NOV], 32), ALU.is_le, a)
    a = red(eor[0:1, 0, 0:NOV], eo[0:1], ALU.add, a)
    a = V(lambda e: e.tensor_scalar(eor[0:1, 1, 0:NOV], eor[0:1, 0, 0:NOV], 31.5, None, ALU.is_lt), a)
    a = V(lambda e: e.tensor_scalar(eor[0:1, 0, 0:NOV], eor[0:1, 0, 0:NOV], 31.0, None, ALU.min), a)
    t_eo = V(lambda e: e.tensor_copy(eoi[0:1, 0:32].rearrange("p (a b) -> p a b", a=2)[:, :, 0:NOV],
                                     eor[0:1, :, 0:NOV]), a)
    a = t_eo
    dst_t = []
    for j, oh in enumerate((oh1, oh2)):
        r_, e_, o_, f_, g_, blk, slot, dest = [pj[:, j, n, :] for n in range(8)]
        for dst, by in ((r_, R), (e_, mid(iota[:, 0:32], 8)), (o_, mid(ovst, 8))):
            a = tt_(tmp, oh, by, ALU.mult, a)
            a = red(dst, tmp, ALU.add, a)
        a = V(lambda e: e.tensor_scalar(g_, r_, 128.0, None, ALU.is_ge), a)
        a = V(lambda e: e.tensor_copy(f_, g_), a)
        for k in range(2, 8):
            a = V(lambda e: e.scalar_tensor_tensor(f_, r_, 128.0 * k, f_, ALU.is_ge, ALU.add), a)
        a = tt_(blk, o_, e_, ALU.subtract, a)
        a = V(lambda e: e.scalar_tensor_tensor(blk, blk, 31.0, g_, ALU.add, ALU.mult), a)
        a = tt_(blk, blk, e_, ALU.add, a)
        a = tt_(blk, blk, f_, ALU.add, a)
        a = V(lambda e: e.scalar_tensor_tensor(slot, f_, -128.0, r_, ALU.mult, ALU.add), a)
        a = V(lambda e: e.scalar_tensor_tensor(dest, blk, 128.0, slot, ALU.mult, ALU.add), a)
        a = V(lambda e: e.tensor_copy(desti[:, j, :], dest), a)
        dst_t.append(a)
    b = rb.take()
    fr = [None, None]
    n_ = 0
    for t in range(8):
        for j in range(2):
            i = n_ % 2
            slot, blk = pj[:, j, 6, t:t + 1], pj[:, j, 5, t:t + 1]
            a1 = V(lambda e: e.tensor_scalar(SL[:, i, :], iota, slot, None, ALU.is_equal), a, fr[i])
            a2 = V(lambda e: e.tensor_scalar(BL[:, i, :], iota[:, 0:NB], blk, tokid[:, t:t + 1],
                                             ALU.is_equal, ALU.mult), a, fr[i])
            m = PE(lambda e: e.matmul(b.ap[:, 0:NB], SL[:, i, :], BL[:, i, :], start=(n_ == 0), stop=(n_ == 15)),
                   a1, a2, b.free)
            fr[i] = m
            n_ += 1
    t_idx = V(lambda e: e.tensor_copy(idx, b.ap[:, 0:NB]), m)
    b.free = [t_idx]
    barrier()

    XG = alloc(3, 1024)
    xb = [Yc[:, 2 + i, :].rearrange("p (k t) -> p k t", k=8) for i in range(2)]
    yo = [Yc[:, 4 + i, :] for i in range(3)]
    hd = [Yc[:, 0, 256 * i:256 * i + 256] for i in range(2)]
    hT = [Yc[:, 0, 512 + 256 * i:768 + 256 * i].rearrange("p (f t) -> p f t", f=2) for i in range(2)]
    sg = [Yc[:, 1, 256 * i:256 * i + 256] for i in range(2)]
    dring = Ring([Slot(OT[:, 2 * i:2 * i + 2, :], chan(f"d_n{i}")) for i in range(4)])
    SP(None, t_eo, hn_store)
    sp = SP.eng

    def expert_id(n, row):
        if sp is None:
            return None
        return sp.value_load(eoi[0:1, 16 * row + n:16 * row + n + 1], min_val=0, max_val=31 if row == 0 else 1)
    gat = [None] * NB
    bfree = {"xg": [None] * 3, "xb": [None] * 2, "hd": [None] * 2, "hT": [None] * 2, "sg": [None] * 2,
             "yo": [None] * 3}
    gch = [chan(f"d_g{i}") for i in range(3)]
    ych = [chan(f"d_y{i}") for i in range(3)]
    ystore = []
    blk_ = {}

    def gather(n):
        i = n % 3
        gat[n] = G.dma(gch[i], lambda e: e.indirect_dma_start(
            XG[:, i, :], None, HN, bass.IndirectOffsetOnAxis(ap=idx[:, n:n + 1].bitcast(mybir.dt.uint32), axis=0)),
            t_idx, hn_store, bfree["xg"][i])

    def weights(n):
        s, d = wring.take(), dring.take()
        gu = s.ap.rearrange("p (k n) -> p k n", k=8)
        dn = d.ap.rearrange("p a b -> p (a b)").rearrange("p (k n) -> p k n", k=8)
        if n < 32:
            tg_ = SP.dma(s.chan, lambda e: e.dma_start(gu, I["w_gu"][n]), s.free)
            td_ = SP.dma(d.chan, lambda e: e.dma_start(dn, I["w_dn"][n]), d.free)
        else:
            v = expert_id(n - 32, 0)
            tg_ = SP.dma(s.chan, lambda e: e.dma_start(
                gu, I["w_gu"][bass.ds(v, 1)].rearrange("o p k n -> (o p) k n")), s.free)
            td_ = SP.dma(d.chan, lambda e: e.dma_start(
                dn, I["w_dn"][bass.ds(v, 1)].rearrange("o p k n -> (o p) k n")), d.free)
        blk_[n] = (s, d, gu, d.ap.rearrange("p f n -> p (f n)").rearrange("p (f n) -> p f n", f=2), tg_, td_)

    def up(n):
        s, d, gu, dn, tg_, td_ = blk_[n]
        x_, i = xb[n % 2], n % 2
        src = XG[:, n % 3, :]
        outs = []
        for half in range(2):
            b = rb.take()
            tr = PE(transposes([(b.ap[:, j * 128:(j + 1) * 128], src[:, (half * 4 + j) * 128:(half * 4 + j + 1) * 128])
                                for j in range(4)], ident), gat[n], b.free)
            o = []
            for j in range(4):
                k = half * 4 + j
                s_ = b.ap[:, j * 128:(j + 1) * 128]
                if half == 0:
                    o = A(lambda e: e.activation(x_[:, k, :], s_, ACT.Identity, bias=MOD[:, 24 + k, 0:1],
                                                 scale=AF[:, k:k + 1]), tr, bfree["xb"][i])
                else:
                    o = V(lambda e: e.tensor_scalar(x_[:, k, :], s_, AF[:, k:k + 1], MOD[:, 24 + k, 0:1],
                                                    ALU.mult, ALU.add), tr, bfree["xb"][i])
            b.free = [o]
            outs.append(o)
        bfree["xg"][n % 3] = tr
        b = rb.take()
        m = PE(mm_group(b.ap, [(x_[:, k, :], gu[:, k, :]) for k in range(8)]), outs, tg_, b.free)
        s.free = [m]
        bfree["xb"][i] = m
        a = recip_sig(sg[i], b.ap[:, 0:256], m, bfree["sg"][i])
        a = V(lambda e: e.tensor_tensor(sg[i], b.ap[:, 0:256], sg[i], ALU.mult), a)
        a = V(lambda e: e.tensor_tensor(hd[i], b.ap[:, 256:512], sg[i], ALU.mult), a, bfree["hd"][i])
        bfree["sg"][i] = a
        b.free = [a]
        blk_[n] += (a,)

    def down(n):
        s, d, gu, dn, tg_, td_, th = blk_[n]
        i = n % 2
        b = rb.take()
        tr = PE(transposes([(b.ap[:, f * 128:(f + 1) * 128], hd[i][:, f * 128:(f + 1) * 128]) for f in range(2)],
                           ident), th, b.free)
        bfree["hd"][i] = tr
        o = A(lambda e: e.activation(hT[i], b.ap[:, 0:256].rearrange("p (f t) -> p f t", f=2), ACT.Copy),
              tr, bfree["hT"][i])
        b.free = [o]
        y_ = yo[n % 3]
        outs = []
        for g in range(2):
            b = rb.take()
            gs = slice(g * 512, (g + 1) * 512)
            m = PE(mm_group(b.ap, [(hT[i][:, f, :], dn[:, f, gs]) for f in range(2)]), o, td_, b.free)
            if g == 0:
                c = A(lambda e: e.activation(y_[:, gs], b.ap, ACT.Copy), m, bfree["yo"][n % 3])
            else:
                c = V(lambda e: e.tensor_copy(y_[:, gs], b.ap), m, bfree["yo"][n % 3])
            b.free = [c]
            outs.append(c)
        d.free = [m]
        bfree["hT"][i] = m
        st_ = G.dma(ych[n % 3], lambda e: e.dma_start(YB[n * 128:(n + 1) * 128, :], y_), outs)
        bfree["yo"][n % 3] = st_
        ystore.append(st_)
    gather(0)
    gather(1)
    for n in range(NB + 1):
        if n < NB:
            weights(n)
            up(n)
        if n:
            down(n - 1)
        if n + 2 < NB:
            gather(n + 2)
    barrier()
    Y2 = XG
    gg_ = []
    zch = [chan(f"d_z{i}") for i in range(8)]
    for t in range(NL_T):
        gg_.append(G.dma(zch[t], lambda e: e.indirect_dma_start(
            Yc[:, t, :], None, YB, bass.IndirectOffsetOnAxis(ap=desti[:, 0, t:t + 1].bitcast(mybir.dt.uint32), axis=0)),
            ystore[-3:]))
    fr = [None] * 3
    for t in range(NL_T):
        i = t % 3
        l2 = G.dma(gch[i], lambda e: e.indirect_dma_start(
            Y2[:, i, :], None, YB, bass.IndirectOffsetOnAxis(ap=desti[:, 1, t:t + 1].bitcast(mybir.dt.uint32), axis=0)),
            ystore[-3:], fr[i])
        a = V(lambda e: e.tensor_scalar(Yc[:, t, :], Yc[:, t, :], w12[:, 0, t:t + 1], None, ALU.mult), gg_[t])
        fr[i] = V(lambda e: e.scalar_tensor_tensor(Yc[:, t, :], Y2[:, i, :], w12[:, 1, t:t + 1], Yc[:, t, :],
                                                   ALU.mult, ALU.add), a, l2)
    barrier()
    at[0] = ret_work
    gtr = alloc(1024)
    nfr = alloc(1024)
    sq = alloc(1024)
    ss = alloc(NL_T)
    bar = [q.last() for q in (PE, V, A, G)]
    t_nf = load(nfr, I["norm_final"].partition_broadcast(128), bar)
    tgr = row_broadcast(gtr, MOD[:, 40:48, 0], 8)
    ssl = []
    for t in range(NL_T):
        a = V(lambda e: e.tensor_tensor(Yc[:, t, :], Yc[:, t, :], gtr, ALU.mult), tgr)
        a = G(lambda e: e.tensor_tensor(Yc[:, t, :], Yc[:, t, :], XO[:, t, :], ALU.add), a)
        ssl = [A(lambda e: e.activation(sq, Yc[:, t, :], ACT.Square, accum_out=ss[:, t:t + 1]), a, ssl)]
    r = rstd_of(ss, ss, 1.0 / 1024, ssl)
    fin = []
    for t in range(NL_T):
        a = V(lambda e: e.scalar_tensor_tensor(Yc[:, t, :], Yc[:, t, :], ss[:, t:t + 1], nfr, ALU.mult, ALU.mult),
              r, t_nf)
        fin.append(SP.dma(ch_x[t], lambda e: e.dma_start(out[t * 128:(t + 1) * 128, :], Yc[:, t, :]), a))
    SP(None, fin)


def second_inputs(r, x):
    r["c2"] = np.stack([_cols(x["c_2"][0]), _cols(x["c_ctx_2"])], 2)
    r["w_ada2"] = _groups(x["w_ada_2"][0], [np.arange(i * 512, (i + 1) * 512) for i in range(12)])
    r["b_ada2"] = _cols(x["b_ada_2"][0])
    r["norm_mix"], r["norm_ffn"] = _cols(x["norm_mix_2"][0]), _cols(x["norm_ffn_2"][0])
    r["norm_final"], r["gla_norm"] = x["norm_final_2"], x["gla_norm_2"][0]
    w = x["w_in_2"][0]
    o = np.cumsum([0, 512, 512, 1024, 1024, 16, 16, 512, 512, 1024, 1024, 1024, 1024])
    part = [np.arange(o[i], o[i + 1]) for i in range(12)]
    gq, gk, gv, gg, lf, lb, rq, rk, rv, rg, mg, mr = part
    q, v = [slice(h * 128, (h + 1) * 128) for h in range(4)], [slice(h * 256, (h + 1) * 256) for h in range(4)]
    r["w_gla"] = _groups(w, [np.concatenate([gq[q[h]], gk[q[h]], gv[v[h]]]) for h in range(4)])
    r["w_gg"] = _groups(w, [gg[v[h]] for h in range(4)])
    r["w_ret"] = _groups(w, [np.concatenate([rq[q[h]], rk[q[h]], rv[v[h]]]) for h in range(4)])
    r["w_rg"] = _groups(w, [rg[v[h]] for h in range(4)])
    r["w_lr"] = _groups(w, [np.concatenate([lf, lb])])[0]
    halves = [np.arange(512), np.arange(512, 1024)]
    r["w_bg_m"], r["w_br_m"] = _groups(w, [mg[i] for i in halves]), _groups(w, [mr[i] for i in halves])
    r["w_bg"], r["w_br"] = _groups(x["w_branch_gla_2"][0], halves), _groups(x["w_branch_ret_2"][0], halves)
    r["w_out2"] = _groups(x["w_out_2"][0], halves)
    lr = x["gla_lr_w_2"][0]
    g = np.zeros((4, 32, 2, 128), np.float32)
    for h in range(4):
        for d in range(2):
            g[h, 16 * d:16 * d + 16, d, :] = lr[d][:, q[h]]
    r["gla_lr"] = [g[h] for h in range(4)]
    b = x["gla_lr_b_2"][0].reshape(2, 4, 128)
    r["lr_b"] = b.reshape(8, 128).T
    r["w_router"] = _groups(np.concatenate([x["w_router_group_2"][0], x["w_router_expert_2"][0]], 1), [np.arange(36)])[0]
    r["b_router"] = np.concatenate([x["b_router_group_2"][0], x["b_router_expert_2"][0]])
    r["k_rev"] = np.broadcast_to(np.concatenate([4.0 - np.arange(4), 32.0 - np.arange(32)]).astype(np.float32)[None], (128, 36))
    wg, wu, wd = x["w_expert_gate_2"][0], x["w_expert_up_2"][0], x["w_expert_down_2"][0]
    gu = np.concatenate([wg, wu], 2).reshape(32, 8, 128, 512).transpose(0, 2, 1, 3)
    dn = wd.reshape(32, 2, 128, 1024).transpose(0, 2, 1, 3)
    r["w_gu"] = gu.reshape(32, 128, 8, 512)
    r["w_dn"] = dn.reshape(32, 128, 8, 256)
    return r


def _constants():
    r = {}
    i = np.arange(128)
    r["k_ident"] = np.eye(128, dtype=np.float32)
    sel = np.zeros((4, 4, 128), np.float32)
    for h in range(4):
        sel[h, h] = 1.0
    r["k_sel4"] = sel
    b = np.zeros((4, 128), np.float32)
    for h in range(4):
        b[h, (h % 2) * 64:(h % 2) * 64 + 64] = 1.0
    r["k_bsel"] = b
    s, t = i[:, None], i[None, :]
    neg = np.stack([np.where(s <= t, 0.0, -1e30), np.where(s >= t, 0.0, -1e30)]).astype(np.float32)
    r["k_mneg"] = np.tile(neg, (1, 1, 4))
    rst = np.ones((128, T), np.float32)
    rst[:, ::128] = 0.0
    r["k_rst"] = rst
    tok = np.arange(1024)
    row, col = (tok // 64).astype(np.float32), (tok % 64).astype(np.float32)
    f = (np.float32(10000.0) ** (-np.arange(16, dtype=np.float32) / np.float32(16))).astype(np.float32)
    tab = np.zeros((1024, 128), np.float32)
    for n, p in enumerate((row, col)):
        ang = (p[:, None] * f).astype(np.float32)
        c, sn = np.cos(ang), np.sin(ang)
        tab[:, n * 32:n * 32 + 16] = c
        tab[:, n * 32 + 16:n * 32 + 32] = c
        tab[:, 64 + n * 32:64 + n * 32 + 16] = -sn
        tab[:, 64 + n * 32 + 16:64 + n * 32 + 32] = sn
    r["k_rope1"] = tab.reshape(8, 128, 128).transpose(1, 0, 2)
    f = (np.float32(10000.0) ** (-np.arange(32, dtype=np.float32) / np.float32(32))).astype(np.float32)
    tab = np.zeros((1024, 256), np.float32)
    for n, p in enumerate((row, col)):
        ang = (p[:, None] * f).astype(np.float32)
        c, sn = np.cos(ang), np.sin(ang)
        tab[:, n * 64:n * 64 + 32] = c
        tab[:, n * 64 + 32:n * 64 + 64] = c
        tab[:, 128 + n * 64:128 + n * 64 + 32] = -sn
        tab[:, 128 + n * 64 + 32:128 + n * 64 + 64] = sn
    r["k_rope2"] = tab.reshape(8, 128, 256).transpose(1, 0, 2)
    h = np.arange(4, dtype=np.float64)
    lf, lb = np.log1p(-np.exp2(-5.0 - h)), np.log1p(-np.exp2(-5.5 - h))
    s3, t3 = s[None].astype(np.float64), t[None].astype(np.float64)
    dm = np.where(t3 >= s3, np.exp((t3 - s3) * lf[:, None, None]), np.exp((s3 - t3) * lb[:, None, None]))
    r["k_rdm"] = dm.transpose(1, 0, 2).astype(np.float32)
    qd = np.stack([np.exp((i[None] + 1.0) * lf[:, None]), np.exp((128.0 - i[None]) * lb[:, None])])
    r["k_rqd"] = np.broadcast_to(qd.reshape(1, 2, 4, 128), (128, 2, 4, 128)).astype(np.float32)
    kd = np.stack([np.exp((127.0 - i[:, None]) * lf[None]), np.exp(i[:, None] * lb[None])], 1)
    cd = np.broadcast_to(np.stack([np.exp(128 * lf), np.exp(128 * lb)])[None], (128, 2, 4))
    r["k_rkd"] = np.concatenate([kd.reshape(128, 8), cd.reshape(128, 8)], 1).astype(np.float32)
    m = np.zeros((128, 8, 128), np.float32)
    for n, L in enumerate(LEVELS):
        m[:, n, :] = (s // (2 * L) == t // (2 * L)) & (s // L != t // L)
    m[:, 7, :] = s == t
    r["k_lmask"] = m
    r["k_iota"] = np.broadcast_to(np.arange(128, dtype=np.float32)[None], (128, 128))
    r["k_tri"] = np.where(s < t, 1.0, 0.0)
    r["k_tokid"] = np.arange(1024, dtype=np.float32).reshape(8, 128).T
    return {k: np.ascontiguousarray(v, dtype=np.float32) for k, v in r.items()}


def _groups(w, cols):
    return [np.ascontiguousarray(w[:, c].reshape(8, 128, len(c)).transpose(1, 0, 2)) for c in cols]


def _cols(v):
    return np.ascontiguousarray(v.reshape(-1, 128).T)


def _inputs(x):
    r = dict(_constants())
    x = {k: np.asarray(v) for k, v in x.items()}
    r["x"], r["ctx"], r["ctx2"] = x["x"][0], x["ctx"][0], x["ctx_2"][0]
    r["c"] = np.stack([_cols(x["c"][0]), _cols(x["c_ctx"])], 2)
    r["g_final"] = x["g_final"]
    lists = {n: [] for n in ("w_ada", "b_ada", "g_norm", "w_s", "b_s", "g_q", "g_k", "b_gates", "g_head", "w_out")}
    w_in = [[] for _ in W1]
    o = np.cumsum([0, 256, 256, 256, 512, 128, 128, 512, 256, 256, 256, 256, 256, 16])
    au, av, az, bq, bk, bv, bz, cq, ck, cv, co, cz, cg = [np.arange(o[i], o[i + 1]) for i in range(13)]
    cgp = cg.reshape(4, 4)[[0, 2, 1, 3]].ravel()
    cols = [[av, au], [az, bk, bv], [bq], [bz], [ck, cv], [co, cz], [cq, cgp]]
    cols = [np.concatenate(c) for c in cols]
    sp = [np.arange(i * 512, (i + 1) * 512) for i in range(12)]
    for l in range(2):
        lists["w_ada"].append(_groups(x["w_ada"][l], sp[:6]))
        lists["b_ada"].append(_cols(x["b_ada"][l]))
        lists["g_norm"].append(_cols(x["g_norm"][l]))
        lists["w_s"].append(x["w_s"][l].transpose(2, 0, 1))
        lists["b_s"].append(x["b_s"][l].T)
        lists["g_q"].append(x["g_q"][l])
        lists["g_k"].append(x["g_k"][l])
        lists["b_gates"].append(x["b_gates"][l].reshape(4, 4)[[0, 2, 1, 3]].T)
        lists["g_head"].append(x["g_head"][l])
        lists["w_out"].append(_groups(x["w_out"][l], sp[:2]))
        for g, a in enumerate(_groups(x["w_in"][l], cols)):
            w_in[g].append(a)
    r.update(lists)
    r["w_in"] = w_in
    return second_inputs(r, x)


def _flat(r):
    out = {}
    for k, v in r.items():
        if isinstance(v, list):
            out.update(_flat({f"{k}_{i}": a for i, a in enumerate(v)}))
        else:
            out[k] = np.ascontiguousarray(v)
    return out


def _named(r, nc, prefix=""):
    out = {}
    for k, v in (r.items() if isinstance(r, dict) else enumerate(r)):
        name = f"{prefix}{k}"
        if isinstance(v, (dict, list)):
            out[k] = _named(v, nc, name + "_")
        else:
            v = np.asarray(v)
            out[k] = nc.dram_tensor(name, v.shape, mybir.dt.from_np(v.dtype), kind="ExternalInput").ap()
    return out if isinstance(r, dict) else [out[i] for i in range(len(r))]


def kernel(**inputs):
    import concourse.bacc as _bacc
    from concourse.bass_utils import run_bass_kernel_spmd as _run

    laid = _inputs(inputs)
    nc = _bacc.Bacc("TRN2", target_bir_lowering=False, num_devices=1)
    out = nc.dram_tensor("out_dram", (1024, 1024), F32, kind="ExternalOutput").ap()
    program(nc, _named(laid, nc), out)
    r = _run(nc, [_flat(laid)], core_ids=[0])
    return r.results[0]["out_dram"].reshape(1, 1024, 1024)
```

```python
from contextlib import ExitStack

import numpy as np

import concourse.bass as bass
from concourse import mybir

F32 = mybir.dt.float32
ALU = mybir.AluOpType
ACT = mybir.ActivationFunctionType
AX = mybir.AxisListType.X

NC_T = 2
NL_T = 8
NT = NC_T + NL_T
T = NT * 128
ARENA = 53200
GELU_C = -2.0 * 0.7978845608028654
W1 = [512, 512, 512, 512, 512, 512, 272]
LEVELS = [64, 32, 16, 8, 4, 2, 1]


def flat(tokens):
    for a in tokens:
        if isinstance(a, (list, tuple)):
            yield from flat(a)
        elif a is not None:
            yield a


class Op:

    def __init__(self, queue, index, sem, value):
        self.queue, self.index, self.sem, self.value = queue, index, sem, value


class Queue:

    def __init__(self, sem, awaited, eng):
        self.sem, self.awaited, self.eng = sem, awaited, eng
        self.n = self.count = 0
        self.seen = {}
        self.tail = None

    def _wait(self, after):
        for a in flat(after):
            if a.index is not None:
                a.queue.awaited.add(a.index)
            if self.eng is not None and self.seen.get(id(a.sem), 0) < a.value:
                self.eng.wait_ge(a.sem, a.value)
                self.seen[id(a.sem)] = a.value

    def __call__(self, fn, *after):
        self._wait(after)
        if fn is None:
            return None
        self.n += 1
        hit = self.n in self.awaited
        self.count += hit
        if self.eng is not None:
            ins = fn(self.eng)
            if hit:
                ins.then_inc(self.sem, 1)
        self.tail = Op(self, self.n, self.sem, self.count)
        return self.tail

    def dma(self, chan, fn, *after):
        self._wait(after)
        chan.count += 16
        if self.eng is not None:
            fn(self.eng).then_inc(chan.sem, 16)
        return Op(self, None, chan.sem, chan.count)

    def last(self):
        return self.tail


class Chan:
    def __init__(self, sem):
        self.sem, self.count = sem, 0


class Slot:

    def __init__(self, ap, chan=None):
        self.ap, self.free, self.chan = ap, [], chan


class Ring:
    def __init__(self, slots):
        self.slots, self.n = slots, 0

    def take(self):
        s = self.slots[self.n % len(self.slots)]
        self.n += 1
        return s


ENGINES = ("pe", "v", "a", "g", "sp")
CHANNELS = [f"d_m{i}" for i in range(24)] + [f"d_w{i}" for i in range(3)] + [f"d_x{i}" for i in range(NT)] + \
           [f"d_o{i}" for i in range(4)] + [f"d_rope{i}" for i in range(2)] + [f"d_n{i}" for i in range(4)] + \
           [f"d_g{i}" for i in range(3)] + [f"d_y{i}" for i in range(3)] + \
           [f"d_z{i}" for i in range(8)]
NOV = 15
NB = 32 + NOV


def program(nc, I, out):
    with ExitStack() as ctx:
        arena = ctx.enter_context(nc.sbuf_tensor("arena", [128, ARENA], F32))
        psum = ctx.enter_context(nc.psum_tensor("psum", [128, 8, 512], F32))
        sems = {n: ctx.enter_context(nc.semaphore("s_" + n)) for n in list(ENGINES) + CHANNELS}
        X1 = nc.dram_tensor("x1_scratch", [T, 1024], F32, kind="Internal").ap()
        X2 = nc.dram_tensor("x2_scratch", [1024, 1024], F32, kind="Internal").ap()
        HN = nc.dram_tensor("hn_scratch", [1024, 1024], F32, kind="Internal").ap()
        YB = nc.dram_tensor("yb_scratch", [NB * 128, 1024], F32, kind="Internal").ap()
        awaited = {n: set() for n in ENGINES}
        block = ctx.enter_context(nc.Block())

        def run(name, eng):
            describe(I, out, arena, psum, X1, X2, HN, YB, sems,
                     [Queue(sems[n], awaited[n], eng if n == name else None) for n in ENGINES])
        run(None, None)
        block.tensor(lambda e: run("pe", e))
        block.vector(lambda e: run("v", e))


        def scalar(e):
            e.preload_act_table_set("natural_log_exp_and_others")
            run("a", e)
        block.scalar(scalar)
        block.gpsimd(lambda e: run("g", e))
        block.sync(lambda e: run("sp", e))


def describe(I, out, arena, psum, X1, X2, HN, YB, sems, queues):
    PE, V, A, G, SP = queues

    def chan(name):
        return Chan(sems[name])

    at = [0]

    def alloc(*shape):
        n = int(np.prod(shape))
        a = arena[:, at[0]:at[0] + n]
        at[0] += n
        assert at[0] <= ARENA, at[0]
        if len(shape) > 1:
            names = "abcd"[:len(shape)]
            kw = {names[i]: shape[i] for i in range(len(shape))}
            a = a.rearrange("p (" + " ".join(names) + ") -> p " + " ".join(names), **kw)
        return a

    STOP = object()

    def bc(ap, n):
        return ap.unsqueeze(len(ap.shape)).broadcast_to(list(ap.shape) + [n])

    def mid(ap, n):
        p, m = ap.shape
        return ap.unsqueeze(1).broadcast_to([p, n, m])

    banks = [Slot(psum[:, i, :]) for i in range(8)]
    rb = Ring(banks)

    def barrier():
        tails = [q.last() for q in (PE, V, A, G)]
        for q in (PE, V, A, G):
            q(None, tails)
        return tails

    ch_misc = [chan(f"d_m{i}") for i in range(24)]
    misc_last = [None] * 24
    misc_n = [0]

    def load(dst, src, *after):
        i = misc_n[0] % 24
        misc_n[0] += 1
        misc_last[i] = SP.dma(ch_misc[i], lambda e: e.dma_start(dst, src), misc_last[i], *after)
        return misc_last[i]

    ident = alloc(128)
    ones = alloc(128)
    sel4 = alloc(4, 128)
    bsel = alloc(128)
    small = alloc(64)
    t_id = load(ident, I["k_ident"])
    t_sel = load(sel4[0:4], I["k_sel4"])
    t_bsel = load(bsel[0:4], I["k_bsel"])
    t_ones = V(lambda e: e.memset(ones, 1.0))
    wring = Ring([Slot(alloc(4096), chan(f"d_w{i}")) for i in range(3)])

    def wload(src, cols, *after):
        s = wring.take()
        dst = s.ap[:, 0:8 * cols].rearrange("p (k n) -> p k n", k=8)
        tok = SP.dma(s.chan, lambda e: e.dma_start(dst, src), s.free, *after)
        return dst, tok, s

    def paired(units):
        units = list(units)
        before = []
        for n in range(0, len(units) + 2, 2):
            now = units[n:n + 2]
            for g in now:
                next(g, None)
            while before:
                before = [g for g in before if next(g, STOP) is not STOP]
            before = [g for g in now if next(g, STOP) is not STOP]

    def overlapped4(units):
        before = None
        for g in units:
            for u in (g, before, g, before):
                if u is not None:
                    next(u, None)
            before = g
        next(before, None)
        next(before, None)

    def overlapped(units):
        before = None
        for g in units:
            next(g, None)
            if before is not None:
                next(before, None)
            before = g
        next(before, None)

    def rstd_of(ss, dst, scale, *after):
        a = V(lambda e: e.tensor_scalar(dst, ss, scale, 1e-6, ALU.mult, ALU.add), *after)
        a = A(lambda e: e.activation(dst, dst, ACT.Ln), a)
        return A(lambda e: e.activation(dst, dst, ACT.Exp, scale=-0.5), a)

    def mm_group(out_ap, pairs):
        def fn(e):
            n = len(pairs)
            for i, (l, r) in enumerate(pairs):
                ins = e.matmul(out_ap, l, r, start=(i == 0), stop=(i == n - 1))
            return ins
        return fn

    def transposes(outs_ins, idn):
        def fn(e):
            for o, i in outs_ins:
                ins = e.transpose(o, i, idn)
            return ins
        return fn

    def to_feature(src, dst, t, scale, bias, *after):
        toks = []
        for half in range(2):
            b = rb.take()
            tr = PE(transposes([(b.ap[:, j * 128:(j + 1) * 128],
                                 src[:, (half * 4 + j) * 128:(half * 4 + j + 1) * 128]) for j in range(4)],
                               ident), b.free, t_id, *after)
            q = A if half == 0 else V
            for j in range(4):
                k = half * 4 + j
                d = dst[:, k, t * 128:(t + 1) * 128]
                s_ = b.ap[:, j * 128:(j + 1) * 128]
                if scale is None:
                    if q is A:
                        o = A(lambda e, d=d, s_=s_: e.activation(d, s_, ACT.Copy), tr)
                    else:
                        o = V(lambda e, d=d, s_=s_: e.tensor_copy(d, s_), tr)
                elif q is A:
                    o = A(lambda e, d=d, s_=s_, k=k: e.activation(
                        d, s_, ACT.Identity, bias=bias[:, k:k + 1], scale=scale[:, k:k + 1]), tr)
                else:
                    o = V(lambda e, d=d, s_=s_, k=k: e.tensor_scalar(
                        d, s_, scale[:, k:k + 1], bias[:, k:k + 1], ALU.mult, ALU.add), tr)
            b.free = [o]
            toks.append(o)
        return toks

    def sig_den(dst, src, *after):
        a = A(lambda e: e.activation(dst, src, ACT.Exp, scale=-1.0), *after)
        return G(lambda e: e.tensor_scalar(dst, dst, 1.0, None, ALU.add), a)

    def modulation(name_w, ngroups, cvec, t_c, MOD, badd):
        got, row = {}, [None, None]

        def fetch(g):
            got[g] = wload(name_w[g], 512)

        def compute(g, bank, *after):
            w, tw, s = got.pop(g)
            m = PE(mm_group(bank[0:2, :], [(cvec[:, k, :], w[:, k, :]) for k in range(8)]), tw, t_c, *after)
            s.free = [m]
            row[0] = V(lambda e: e.tensor_copy(mrow[0][0:2, :], bank[0:2, :]), m, row[1])
            return row[0]

        def turn(g, bank, *after):
            row[1] = PE(transposes([(bank[:, 2 * j:2 * j + 2], mrow[0][0:2, 128 * j:128 * j + 128]) for j in range(4)],
                                   ident[0:2, 0:2]), t_id, row[0], *after)
            return V(lambda e: e.tensor_tensor(
                MOD[:, 4 * g:4 * g + 4, :], bank[:, 0:8].rearrange("p (j v) -> p j v", v=2),
                bc(badd[:, 4 * g:4 * g + 4], 2), ALU.add), row[1])
        return fetch, compute, turn

    def silu_c(cvec, tmp, src, *after):
        l = load(cvec, src, *after)
        a = A(lambda e: e.activation(tmp, cvec, ACT.Exp, scale=-1.0), l)
        a = V(lambda e: e.tensor_scalar(tmp, tmp, 1.0, None, ALU.add), a)
        a = V(lambda e: e.reciprocal(tmp, tmp), a)
        return V(lambda e: e.tensor_tensor(cvec, cvec, tmp, ALU.mult), a)

    def row_broadcast(dst, cols, n, *after):
        dg = alloc(2, 128)
        free = [None, None]
        last = None
        for j in range(n):
            b = rb.take()
            d = V(lambda e, j=j: e.tensor_scalar(dg[:, j % 2, :], ident, cols[:, j:j + 1], None, ALU.mult),
                  t_id, free[j % 2], *after)
            m = PE(lambda e, j=j, b=b: e.matmul(b.ap[:, 0:128], ones, dg[:, j % 2, :], start=True, stop=True),
                   d, t_ones, b.free)
            free[j % 2] = m
            last = A(lambda e, j=j, b=b: e.activation(dst[:, j * 128:(j + 1) * 128], b.ap[:, 0:128], ACT.Copy), m)
            b.free = [last]
        return last

    def load_rows(X, src_rows, *after):
        return [SP.dma(ch_x[t], lambda e: e.dma_start(X[:, t, :], src_rows[t]), *after) for t in range(NT)]

    def normalise_in(X, xT, lo, scale, bias, t_mod, *after):
        ss = alloc(NT)
        sq = alloc(1024)
        a = None
        for t in range(NT):
            a = A(lambda e, t=t: e.activation(sq, X[:, t, :], ACT.Square, accum_out=ss[:, t:t + 1]), lo[t], after, a)
        r = rstd_of(ss, ss, 1.0 / 1024, a)
        toks = []
        for t in range(NT):
            q = V if t % 2 else G
            m = q(lambda e, t=t: e.tensor_scalar(X[:, t, :], X[:, t, :], ss[:, t:t + 1], None, ALU.mult), r)
            v = 1 if t < NC_T else 0
            toks += to_feature(X[:, t, :], xT, t, scale[:, :, v], bias[:, :, v], m, t_mod)
        return toks

    ch_x = [chan(f"d_x{i}") for i in range(NT)]
    ch_o = [chan(f"d_o{i}") for i in range(4)]

    x1_store = [None] * NT
    x2_store = [None] * NL_T
    mrow = [None]
    MODs = [alloc(24, 2), alloc(24, 2)]
    MOD2 = alloc(48, 2)
    cvec = alloc(2, 8, 2)
    ctmp = alloc(8, 2)
    badd = [alloc(24), alloc(24), alloc(48)]
    gns = alloc(3, 8)
    nf = alloc(8)
    t_gn_ = [load(gns[:, 0, :], I["g_norm"][0]), load(gns[:, 1, :], I["g_norm"][1]), load(gns[:, 2, :], I["norm_mix"])]
    t_nf_ = load(nf, I["norm_ffn"])
    t_ba = [load(badd[0], I["b_ada"][0]), load(badd[1], I["b_ada"][1]), load(badd[2], I["b_ada2"])]
    tc1 = silu_c(cvec[:, 0], ctmp, I["c"])
    tc2 = silu_c(cvec[:, 1], ctmp, I["c2"], tc1)
    mods = [modulation(I["w_ada"][0], 6, cvec[:, 0], [tc1, t_ba[0]], MODs[0], badd[0]),
            modulation(I["w_ada"][1], 6, cvec[:, 0], [tc1, t_ba[1]], MODs[1], badd[1]),
            modulation(I["w_ada2"], 12, cvec[:, 1], [tc2, t_ba[2]], MOD2, badd[2])]
    mod_t = [[], [], []]
    top = at[0]
    rows0 = [I["ctx"][t * 128:(t + 1) * 128, :] for t in range(NC_T)] + \
            [I["x"][t * 128:(t + 1) * 128, :] for t in range(NL_T)]
    DEPTH = 2
    phase = []
    for l in range(DEPTH):
        emit_ctx = l < DEPTH - 1
        t0 = 0 if emit_ctx else NC_T
        at[0] = top
        xnT = alloc(8, T)
        Y = alloc(NT, 1024)
        MOD = MODs[l]
        AM = alloc(8, 2)
        gates_b = alloc(16)
        keep = at[0]
        rows = rows0 if l == 0 else [X1[t * 128:(t + 1) * 128, :] for t in range(NT)]
        x_in = load_rows(Y, rows, phase, x1_store)
        if l == 0:
            mrow[0] = alloc(512)
            for g in range(6):
                mods[0][0](g)
                b, b2 = rb.take(), rb.take()
                b.free = [mods[0][1](g, b.ap, b.free)]
                b2.free = [mods[0][2](g, b2.ap, b2.free)]
                mod_t[0] += b2.free
        tm = V(lambda e: e.tensor_scalar(AM, MOD[:, 8:16, :], 1.0, None, ALU.add), mod_t[l], phase)
        tm = V(lambda e: e.tensor_tensor(AM, AM, bc(gns[:, l, :], 2), ALU.mult), tm, t_gn_)
        tx = normalise_in(Y, xnT, x_in, AM, MOD[:, 0:8, :], tm, phase)
        xnT_ready = tx
        barrier()
        at[0] = keep
        KV = alloc(NT, 256)
        wsT = alloc(4, 128)
        bsT = alloc(4)
        vu = alloc(4, 512)
        zb = alloc(4, 256)
        t1s = alloc(2, 512)
        t2s = alloc(2, 512)
        t3s = alloc(2, 256)
        t4s = alloc(2, 256)
        sts = alloc(2, 16)
        bar = [q.last() for q in (PE, V, A, G)]
        w0, tw0, s0 = wload(I["w_in"][0][l], 512)
        w1, tw1, s1 = wload(I["w_in"][1][l], 512)
        dw = load(wsT, I["w_s"][l], bar)
        db = load(bsT, I["b_s"][l], bar)
        prev_vu = [None] * 4
        last_y = [None] * NT
        kv_t = [None] * NT
        def branch_a(t):
            cols = slice(t * 128, (t + 1) * 128)
            full = t >= t0
            b1 = rb.take()
            c0 = 0 if full else 256
            m1 = PE(mm_group(b1.ap[:, c0:512], [(xnT[:, k, cols], w1[:, k, c0:512]) for k in range(8)]),
                    tw1, xnT_ready, b1.free)
            if not full:
                s1.free = [m1]
                yield
                kv_t[t] = A(lambda e, t=t, b1=b1: e.activation(KV[:, t, :], b1.ap[:, 256:512], ACT.Copy), m1)
                b1.free = [kv_t[t]]
                return
            b0 = rb.take()
            m0 = PE(mm_group(b0.ap, [(xnT[:, k, cols], w0[:, k, :]) for k in range(8)]),
                    tw0, xnT_ready, b0.free)
            s0.free, s1.free = [m0], [m0]
            yield
            kv_t[t] = A(lambda e, t=t, b1=b1: e.activation(KV[:, t, :], b1.ap[:, 256:512], ACT.Copy), m1)
            b1.free = [kv_t[t]]
            x_ = vu[:, t % 4, :]
            z_ = zb[:, t % 4, :]
            zc = A(lambda e, z_=z_, b1=b1: e.activation(z_, b1.ap[:, 0:256], ACT.Copy), m1, prev_vu[t % 4])
            b1.free = [zc]
            xc = A(lambda e, x_=x_, b0=b0: e.activation(x_, b0.ap, ACT.Copy), m0, prev_vu[t % 4])
            b0.free = [xc]
            yield
            t1, t2, t3, t4, st = (z[:, t % 2, :] for z in (t1s, t2s, t3s, t4s, sts))
            a = V(lambda e, x_=x_: e.tensor_tensor(t1, x_, x_, ALU.mult), xc)
            yield
            a = V(lambda e: e.tensor_scalar(t1, t1, 0.044715, 1.0, ALU.mult, ALU.add), a)
            yield
            a = V(lambda e, x_=x_: e.tensor_tensor(t1, t1, x_, ALU.mult), a)
            yield
            a = A(lambda e: e.activation(t2, t1, ACT.Exp, scale=GELU_C), a)
            yield
            a = V(lambda e: e.tensor_scalar(t2, t2, 1.0, None, ALU.add), a)
            yield
            a = V(lambda e: e.reciprocal(t2, t2), a)
            yield
            g_ = V(lambda e, x_=x_: e.tensor_tensor(x_, t2, x_, ALU.mult), a)
            yield
            v4 = x_[:, 0:256].rearrange("p (g d) -> p g d", g=4)
            q4 = t3.rearrange("p (g d) -> p g d", g=4)
            a = V(lambda e, v4=v4: e.tensor_reduce(st[:, 0:4], v4, AX, ALU.add), g_)
            yield
            a = V(lambda e: e.tensor_scalar(st[:, 0:4], st[:, 0:4], 1.0 / 64, None, ALU.mult), a)
            yield
            vc = V(lambda e, v4=v4: e.tensor_tensor(v4, v4, bc(st[:, 0:4], 64), ALU.subtract), a)
            yield
            a = V(lambda e, v4=v4: e.tensor_tensor(q4, v4, v4, ALU.mult), vc)
            yield
            a = V(lambda e: e.tensor_reduce(st[:, 4:8], q4, AX, ALU.add), a)
            yield
            a = rstd_of(st[:, 4:8], st[:, 4:8], 1.0 / 64, a)
            yield
            a = V(lambda e, v4=v4: e.tensor_tensor(v4, v4, bc(st[:, 4:8], 64), ALU.mult), a)
            yield
            b2 = rb.take()

            def fn(e, b2=b2, x_=x_):
                for g in range(4):
                    ins = e.matmul(b2.ap[:, g * 64:(g + 1) * 64], wsT[:, g, :], x_[:, g * 64:(g + 1) * 64],
                                   start=True, stop=True)
                return ins
            ms = PE(fn, a, dw, b2.free)
            zd = sig_den(t4, z_, zc, last_y[t - 2] if t > 1 else None)
            yield
            a = V(lambda e: e.reciprocal(t4, t4), zd)
            yield
            a = V(lambda e, z_=z_: e.tensor_tensor(t4, t4, z_, ALU.mult), a)
            yield
            a1 = V(lambda e, x_=x_: e.tensor_tensor(t4, t4, x_[:, 256:512], ALU.mult), a, g_)
            yield
            a = V(lambda e, b2=b2: e.tensor_tensor(q4, b2.ap[:, 0:256].rearrange("p (g d) -> p g d", g=4),
                                                   bc(bsT, 64), ALU.add), ms, db)
            yield
            b2.free = [a]
            last_y[t] = V(lambda e, t=t: e.tensor_tensor(Y[:, t, 0:256], t3, t4, ALU.mult), a, a1)
            prev_vu[t % 4] = [last_y[t], ms]
        paired(branch_a(t) for t in range(NT))
        barrier()
        at[0] = keep
        KV = alloc(NT, 256)
        kT = alloc(2, T)
        qT = alloc(4, T)
        mark = at[0]
        rope = alloc(NL_T, 128)
        gqk = alloc(2, 64)
        qs = alloc(4, 512)
        t1s = alloc(2, 512)
        t2s = alloc(2, 512)
        kds = alloc(2, 2, 128)
        sts = alloc(2, 16)
        bar = [q.last() for q in (PE, V, A, G)]
        w, tw, s_ = wload(I["w_in"][2][l], 512)
        dr = load(rope, I["k_rope1"], bar)
        dg = [load(gqk[:, 0, :], I["g_q"][l].partition_broadcast(128), bar),
              load(gqk[:, 1, :], I["g_k"][l].partition_broadcast(128), bar)]

        def headnorm_rope(x_, n, gi, t, *after):
            t1, t2, st = (z[:, t % 2, :] for z in (t1s, t2s, sts))
            hn_ = hn[t % 2]
            x3 = x_.rearrange("p (h d) -> p h d", h=n)
            y_ = t1[:, 0:64 * n]
            y3 = y_.rearrange("p (h d) -> p h d", h=n)
            a = G(lambda e: e.tensor_tensor(y_, x_, x_, ALU.mult), hn_[0], *after)
            yield
            a = V(lambda e: e.tensor_reduce(st[:, 0:n], y3, AX, ALU.add), a)
            yield
            a = rstd_of(st[:, 0:n], st[:, 0:n], 1.0 / 64, a)
            yield
            a = V(lambda e: e.tensor_tensor(x3, x3, bc(st[:, 0:n], 64), ALU.mult), a)
            yield
            a = V(lambda e: e.tensor_tensor(x3, x3, mid(gqk[:, gi, :], n), ALU.mult), a, dg)
            yield
            if t < NC_T:
                hn_[0] = a
                return a
            tab = rope[:, t - NC_T, :]
            z_ = t2[:, 0:64 * n]
            z3 = z_.rearrange("p (h d) -> p h d", h=n)
            b_ = V(lambda e: e.tensor_tensor(y3, x3, mid(tab[:, 0:64], n), ALU.mult), a, dr)
            last = []
            x5 = x_.rearrange("p (h r s f) -> p h r s f", h=n, r=2, s=2)
            z5 = z_.rearrange("p (h r s f) -> p h r s f", h=n, r=2, s=2)
            s5 = tab[:, 64:128].rearrange("p (r s f) -> p r s f", r=2, s=2)
            for r in range(2):
                for s in range(2):
                    last.append(G(lambda e, r=r, s=s: e.tensor_tensor(
                        z5[:, :, r, s, :], x5[:, :, r, 1 - s, :], mid(s5[:, r, s, :], n), ALU.mult), a, dr))
            yield
            hn_[0] = V(lambda e: e.tensor_tensor(x_, y_, z_, ALU.add), b_, last)
            yield
            return hn_[0]

        hn = [[None], [None]]

        prev = [None] * 4
        pk = [None, None]
        def branch_b(t):
            cols = slice(t * 128, (t + 1) * 128)
            if t >= t0:
                b = rb.take()
                m = PE(mm_group(b.ap, [(xnT[:, k, cols], w[:, k, :]) for k in range(8)]), tw, b.free)
                s_.free = [m]
            yield
            if t >= t0:
                q_ = qs[:, t % 4, :]
                c = A(lambda e, q_=q_, b=b: e.activation(q_, b.ap, ACT.Copy), m, prev[t % 4])
                b.free = [c]
            yield
            kd = kds[:, t % 2]
            a = yield from headnorm_rope(KV[:, t, 0:128], 2, 1, t)
            k3 = KV[:, t, 0:128].rearrange("p (g d) -> p g d", g=2)
            kd4 = kd.rearrange("p g (r d) -> p g r d", r=2)
            a = [V(lambda e, k3=k3, r=r: e.tensor_copy(kd4[:, :, r, :], k3), a, pk[t % 2]) for r in range(2)]
            yield
            b = rb.take()
            tr = PE(transposes([(b.ap[:, g * 128:(g + 1) * 128], kd[:, g, :]) for g in range(2)], ident), a, b.free)
            pk[t % 2] = tr
            o = A(lambda e, b=b, cols=cols: e.activation(
                kT[:, :, cols], b.ap[:, 0:256].rearrange("p (g t) -> p g t", g=2), ACT.Copy), tr)
            b.free = [o]
            if t < t0:
                return
            a = yield from headnorm_rope(q_, 8, 0, t, c)
            b = rb.take()
            tr = PE(transposes([(b.ap[:, j * 128:(j + 1) * 128], q_[:, j * 128:(j + 1) * 128]) for j in range(4)],
                               ident), a, b.free)
            prev[t % 4] = tr
            o = A(lambda e, b=b, cols=cols: e.activation(
                qT[:, :, cols], b.ap.rearrange("p (g t) -> p g t", g=4), ACT.Copy), tr)
            b.free = [o]
        paired(branch_b(t) for t in range(NT))
        w3, tw3, s3 = wload(I["w_in"][3][l], 512)
        w5, tw5, s5_ = wload(I["w_in"][5][l], 512)
        barrier()
        t1, t2 = t1s[:, 0, :], t2s[:, 0, :]
        pt = None
        for t in range(t0, NT):
            cols = slice(t * 128, (t + 1) * 128)
            b = rb.take()
            m = PE(mm_group(b.ap, [(xnT[:, k, cols], w3[:, k, :]) for k in range(8)]), tw3, b.free)
            s3.free = [m]
            a = A(lambda e, b=b: e.activation(t1, b.ap, ACT.Exp, scale=-1.0), m, pt)
            a = V(lambda e: e.tensor_scalar(t1, t1, 1.0, None, ALU.add), a)
            a = V(lambda e: e.reciprocal(t1, t1), a)
            a = V(lambda e, b=b, t=t: e.tensor_tensor(Y[:, t, 256:768], b.ap, t1, ALU.mult), a)
            b.free = [a]
            b = rb.take()
            m = PE(mm_group(b.ap, [(xnT[:, k, cols], w5[:, k, :]) for k in range(8)]), tw5, b.free)
            s5_.free = [m]
            a2 = A(lambda e, b=b: e.activation(t2, b.ap, ACT.Exp, scale=-1.0), m, pt)
            a2 = V(lambda e: e.tensor_scalar(t2, t2, 1.0, None, ALU.add), a2)
            a2 = V(lambda e: e.tensor_tensor(t2[:, 0:256], t2[:, 0:256], t2[:, 256:512], ALU.mult), a2)
            a2 = V(lambda e: e.reciprocal(t2[:, 0:256], t2[:, 0:256]), a2)
            a2 = V(lambda e, b=b, t=t: e.tensor_tensor(Y[:, t, 768:1024], b.ap[:, 256:512], t2[:, 0:256],
                                                       ALU.mult), a2)
            b.free = [a2]
            pt = [a, a2]
        barrier()
        at[0] = mark
        Pm = alloc(2, T)
        PT = alloc(2, T)
        st = alloc(4, 4)
        sets = [psum[:, 0:3, :].rearrange("p b n -> p (b n)"), psum[:, 3:6, :].rearrange("p b n -> p (b n)")]
        set_free = [[b for s in banks[0:3] for b in s.free], [b for s in banks[3:6] for b in s.free]]
        pv_free = [banks[6].free, banks[7].free]
        P_free = [None, None]
        PT_free = [None, None]
        units = [(t, h) for t in range(t0, NT) for h in range(8)]
        state = {}

        def att_scores(u):
            t, h = units[u]
            n = (NC_T if t < NC_T else NT) * 128
            i = u % 2
            base = 64 * (h % 2)
            g = h // 4
            S = sets[i]

            def fn(e):
                for c in range(0, n, 512):
                    w_ = min(512, n - c)
                    ins = e.matmul(S[:, c:c + w_], qT[base:base + 64, h // 2, t * 128:(t + 1) * 128],
                                   kT[base:base + 64, g, c:c + w_], start=True, stop=True)
                return ins
            m = PE(fn, set_free[i])
            mx = st[:, u % 4, 0:1]
            a = V(lambda e: e.tensor_reduce(mx, S[:, 0:n], AX, ALU.max), m, state.get(u - 4))
            a = V(lambda e: e.tensor_scalar(mx, mx, -0.125, None, ALU.mult), a)
            state["m", u] = a

        def att_exp(u):
            t, h = units[u]
            n = (NC_T if t < NC_T else NT) * 128
            i = u % 2
            S = sets[i]
            mx = st[:, u % 4, 0:1]
            state["e", u] = A(lambda e: e.activation(Pm[:, i, 0:n], S[:, 0:n], ACT.Exp, bias=mx, scale=0.125,
                                                     accum_out=st[:, u % 4, 1:2]),
                              state["m", u], P_free[i])

        def att_turn(u):
            t, h = units[u]
            nt = NC_T if t < NC_T else NT
            i = u % 2
            S = sets[i]
            outs = []
            for c in range(0, nt, 4):
                n = min(4, nt - c)
                tr = PE(transposes([(S[:, (c + j) * 128:(c + j + 1) * 128], Pm[:, i, (c + j) * 128:(c + j + 1) * 128])
                                    for j in range(n)], ident), state["e", u])
                d = PT[:, i, c * 128:(c + n) * 128]
                s_ = S[:, c * 128:(c + n) * 128]
                if c == 0:
                    o = V(lambda e, d=d, s_=s_: e.tensor_copy(d, s_), tr, PT_free[i])
                else:
                    o = A(lambda e, d=d, s_=s_: e.activation(d, s_, ACT.Copy), tr, PT_free[i])
                outs.append(o)
            P_free[i] = [tr]
            set_free[i] = outs
            state["t", u] = outs

        def att_values(u):
            t, h = units[u]
            nt = NC_T if t < NC_T else NT
            i = u % 2
            g = h // 4
            outs = state["t", u]
            O = psum[:, 6 + i, 0:64]

            def fn(e):
                for c in range(nt):
                    ins = e.matmul(O, PT[:, i, c * 128:(c + 1) * 128], KV[:, c, 128 + 64 * g:192 + 64 * g],
                                   start=(c == 0), stop=(c == nt - 1))
                return ins
            m = PE(fn, outs, pv_free[i])
            PT_free[i] = [m]
            a = V(lambda e: e.reciprocal(st[:, u % 4, 2:3], st[:, u % 4, 1:2]), state["e", u])
            yv = Y[:, t, 256 + 64 * h:320 + 64 * h]
            a = V(lambda e: e.scalar_tensor_tensor(yv, O, st[:, u % 4, 2:3], yv, ALU.mult, ALU.mult), a, m)
            pv_free[i] = [a]
            state[u] = a

        mrow[0] = alloc(512)
        nxt, ng = mods[l + 1], 6 if l == 0 else 12
        for u in range(len(units) + 2):
            if u < len(units):
                att_scores(u)
            if 0 < u <= len(units):
                att_turn(u - 1)
            if u < len(units):
                att_exp(u)
            if u > 1:
                att_values(u - 2)
            step = 10 if l == 0 else 5
            if u >= 3 and u % step == 3 and u // step < ng:
                nxt[0](u // step)
            if u > step and u % step == 1 and u // step - 1 < ng:
                i = (u + 1) % 2
                pv_free[i] = [nxt[1](u // step - 1, psum[:, 6 + i, :], pv_free[i])]
            if u >= 3 + step and u % step == 3 and u // step - 1 < ng:
                i = (u + 1) % 2
                pv_free[i] = [nxt[2](u // step - 1, psum[:, 6 + i, :], pv_free[i])]
                mod_t[l + 1] += pv_free[i]
        barrier()
        for b in banks:
            b.free = []
        at[0] = keep
        kc = alloc(NT, 256)
        va = alloc(NT, 4, 65)
        qkT = alloc(4, T)
        graw = alloc(2, 288)
        LIF = alloc(4, T)
        bar = [q.last() for q in (PE, V, A, G)]
        gb4 = gates_b[0:4, 0:4]
        w4, tw4, s4 = wload(I["w_in"][4][l], 512)
        w6, tw6, s6 = wload(I["w_in"][6][l], 272)
        dgb = load(gb4, I["b_gates"][l], bar)
        on = V(lambda e: e.memset(va[:, :, :, 64:65], 1.0))
        prev = [None, None]
        for t in range(NT):
            cols = slice(t * 128, (t + 1) * 128)
            b = rb.take()
            m = PE(mm_group(b.ap, [(xnT[:, k, cols], w4[:, k, :]) for k in range(8)]), tw4, b.free)
            s4.free = [m]
            a1 = A(lambda e, b=b, t=t: e.activation(kc[:, t, :], b.ap[:, 0:256], ACT.Copy, scale=0.125), m)
            a2 = V(lambda e, b=b, t=t: e.tensor_copy(
                va[:, t, :, 0:64], b.ap[:, 256:512].rearrange("p (h d) -> p h d", h=4)), m, a1)
            b.free = [a2]
            b = rb.take()
            m = PE(mm_group(b.ap[:, 0:272], [(xnT[:, k, cols], w6[:, k, :]) for k in range(8)]), tw6, b.free)
            s6.free = [m]
            a3 = A(lambda e, b=b, t=t: e.activation(graw[:, t % 2, 0:272], b.ap[:, 0:272], ACT.Copy), m, prev[t % 2])
            b.free = [a3]
            b = rb.take()
            tr = PE(transposes(
                [(b.ap[:, j * 128:(j + 1) * 128], graw[:, t % 2, j * 128:(j + 1) * 128]) for j in range(2)] +
                [(b.ap[:, (2 + j) * 128:(3 + j) * 128], kc[:, t, j * 128:(j + 1) * 128]) for j in range(2)],
                ident), a1, a3, b.free)
            o = V(lambda e, b=b, cols=cols: e.tensor_copy(qkT[:, :, cols], b.ap.rearrange("p (g t) -> p g t", g=4)), tr)
            b.free = [o]
            b = rb.take()
            tr = PE(transposes([(b.ap[0:4, j * 128:(j + 1) * 128], graw[:, t % 2, 256 + 4 * j:260 + 4 * j])
                                for j in range(4)], ident), b.free)
            prev[t % 2] = tr
            o = A(lambda e, b=b, cols=cols: e.activation(
                LIF[0:4, :, cols], b.ap[0:4, :].rearrange("p (g t) -> p g t", g=4), ACT.Copy), tr)
            b.free = [o]
        barrier()
        at[0] = top
        B_ = alloc(T)
        M_ = alloc(T)
        Wd = alloc(T)
        NM = alloc(T)
        stack = alloc(T)
        rst = alloc(T)
        HF = alloc(NT, 256)
        assert at[0] <= top + 8 * T
        at[0] = keep + NT * 256 + NT * 260 + 4 * T + 2 * 288 + 4 * T
        colq1 = alloc(NT, 128)
        colq = colq1.unsqueeze(1).broadcast_to([128, 2, NT, 128])
        mneg = alloc(2, 512)
        gh = stack[:, 1024:1280]
        C0 = alloc(2, 130)
        kw = alloc(2, 256)
        NMx = B_[:, 0:1024].rearrange("p (a b) -> p a b", a=2)
        dec1 = B_[:, 1024:1024 + 2 * NT].rearrange("p (c j) -> p c j", j=2)
        dec = dec1.unsqueeze(1).broadcast_to([128, 2, NT, 2])
        st = B_[:, 1100:1132].rearrange("p (a b) -> p a b", a=2)
        Dm = stack[:, 0:1024].rearrange("p (a b) -> p a b", a=2)
        nd = graw.rearrange("p a b -> p (a b)")[:, 0:520].rearrange("p (a b) -> p a b", a=2)
        bar = [q.last() for q in (PE, V, A, G)]
        t_m = [load(mneg[:, 0, :], I["k_mneg"][0], bar), load(mneg[:, 1, :], I["k_mneg"][1], bar)]
        t_rst = load(rst[0:4, :], I["k_rst"][0:4, :], bar)
        ends = []
        for j in (2, 3, 0, 1):
            a = V(lambda e, j=j: e.tensor_scalar(LIF[0:4, j, :], LIF[0:4, j, :], gb4[:, j:j + 1], None, ALU.add), dgb)
            if j >= 2:
                x_ = LIF[0:4, j, :]
                y_ = (B_ if j == 2 else M_)[0:4, :]
                a1 = A(lambda e: e.activation(y_, x_, ACT.Abs), a)
                a1 = A(lambda e: e.activation(y_, y_, ACT.Exp, scale=-1.0), a1)
                a1 = A(lambda e: e.activation(y_, y_, ACT.Ln, bias=1.0), a1)
                ends.append((x_, y_, a1))
        for x_, y_, a1 in ends:
            a = V(lambda e: e.tensor_scalar(x_, x_, 0.0, None, ALU.min), a1)
            a = V(lambda e: e.tensor_tensor(x_, x_, y_, ALU.subtract), a, a1)
        barrier()
        zs = V(lambda e: e.memset(stack, 0.0))
        hprev = [None] * NT
        for d in range(2):
            LI, LF = LIF[0:4, d, :], LIF[0:4, 2 + d, :]
            seg = [(0, NC_T * 128), (NC_T * 128, T)]

            def view(ap, a_, b_, d=d):
                v = ap[:, a_:b_]
                return v[:, ::-1] if d else v
            init = 0.0
            tok = [t_rst]
            for a_, b_ in seg:
                tok.append(V(lambda e, a_=a_, b_=b_: e.tensor_tensor_scan(
                    view(B_[0:4, :], a_, b_), rst[0:4, a_:b_], view(LF, a_, b_), 0.0, ALU.mult, ALU.add), t_rst))
                tok.append(V(lambda e, a_=a_, b_=b_, init=init: e.tensor_tensor_scan(
                    view(M_[0:4, :], a_, b_), view(LF, a_, b_), view(LI, a_, b_), init, ALU.add, ALU.max), tok))
                init = M_[0:4, a_:a_ + 1] if d else M_[0:4, b_ - 1:b_]
            a = V(lambda e: e.tensor_tensor(Wd[0:4, :], LI, B_[0:4, :], ALU.subtract), tok)
            a1 = V(lambda e: e.tensor_tensor(NM[0:4, :], B_[0:4, :], M_[0:4, :], ALU.subtract), a)
            order = list(range(NT)) if d == 0 else list(range(NC_T))[::-1] + list(range(NC_T, NT))[::-1]
            pr = None
            a1 = [a1, zs]
            for c in order:
                cs = slice(c * 128, (c + 1) * 128)
                end = c * 128 if d else c * 128 + 127
                if pr is None:
                    a1.append(V(lambda e, cs=cs: e.tensor_copy(stack[0:4, cs], NM[0:4, cs]), a1))
                else:
                    pe_ = pr * 128 if d else pr * 128 + 127
                    a1.append(V(lambda e, cs=cs, pe_=pe_: e.tensor_scalar(
                        stack[0:4, cs], NM[0:4, cs], M_[0:4, pe_:pe_ + 1], None, ALU.add), a1))
                a1.append(V(lambda e, cs=cs, end=end: e.tensor_scalar(
                    stack[64:68, cs], Wd[0:4, cs], NM[0:4, end:end + 1], None, ALU.add), a1))
                pr = c
            a1.append(V(lambda e: e.tensor_scalar(stack[32:36, :], M_[0:4, :], -1.0, None, ALU.mult), a1))
            ends = stack[0:4, :].rearrange("p (c t) -> p c t", c=NT)[:, :, 0 if d else 127]
            dx = NMx[0:4, 0, 0:NT * 4].rearrange("p (c h) -> p c h", c=NT)
            a = V(lambda e: e.tensor_tensor(dx, bc(ends, 4), mid(ident[0:4, 0:4], NT), ALU.mult), a1)
            b = rb.take()

            def fn(e, b=b):
                bb = b.ap[:, 0:2 * NT].rearrange("p (c j) -> p c j", j=2)
                x4 = dx.rearrange("p c (j i) -> p c j i", i=2)
                e.matmul(bb, bsel[0:4, :], x4[:, :, :, 0], start=True, stop=False)
                return e.matmul(bb, bsel[0:4, :], x4[:, :, :, 1], start=False, stop=True)
            m = PE(fn, a, t_bsel, b.free)
            t_dec = A(lambda e, b=b, d=d: e.activation(dec[:, d, :, :], b.ap[:, 0:2 * NT].rearrange(
                "p (c j) -> p c j", j=2), ACT.Exp), m)
            b.free = [t_dec]
            cq = []
            for c0 in range(0, NT, 4):
                n = min(4, NT - c0)
                b = rb.take()
                tr = PE(transposes([(b.ap[:, j * 128:(j + 1) * 128], stack[:, (c0 + j) * 128:(c0 + j + 1) * 128])
                                    for j in range(n)], ident), a1, b.free)
                o = A(lambda e, b=b, c0=c0, n=n, d=d: e.activation(
                    colq[:, d, c0:c0 + n, :], b.ap[:, 0:n * 128].rearrange("p (c t) -> p c t", c=n), ACT.Exp), tr)
                b.free = [o]
                cq.append(o)
            t_gh = load(gh, I["g_head"][l].partition_broadcast(128), cq) if d else None
            zc = V(lambda e: e.memset(C0, 0.0))
            cst = [zc]
            fD = [cq, cq]
            fkw = [None, None]
            fnd = [None, None]
            fx = [a, a]
            fst = [None, None]
            m_dec = m
            rc, held = Ring(banks[0:6]), banks[6:8]

            def chunk(n_, c):
                i = n_ % 2
                cs = slice(c * 128, (c + 1) * 128)
                if emit_ctx or c >= NC_T:
                    nx = NMx[0:4, i, :].rearrange("p (h t) -> p h t", h=4)
                    a = V(lambda e, nx=nx, cs=cs: e.tensor_tensor(nx, mid(NM[0:4, cs], 4), sel4[0:4], ALU.mult),
                          fx[i], t_sel, m_dec)
                    b = rc.take()

                    def fn(e, b=b, cs=cs, i=i):
                        e.matmul(b.ap, Wd[0:4, cs], sel4[0:4].rearrange("p h t -> p (h t)"), start=True, stop=False)
                        return e.matmul(b.ap, ones[0:4, 0:128], NMx[0:4, i, :], start=False, stop=True)
                    mA = PE(fn, a, b.free)
                    fx[i] = mA
                    a = V(lambda e, b=b, i=i, d=d: e.tensor_tensor(Dm[:, i, :], b.ap, mneg[:, d, :], ALU.min),
                          mA, t_m, fD[i])
                    b.free = [a]
                    a = A(lambda e, i=i: e.activation(Dm[:, i, :], Dm[:, i, :], ACT.Exp), a)
                    bs = [rc.take(), rc.take()]
                    prods = []
                    for r in range(2):
                        p, b = 64 * r, bs[r]

                        def fn(e):
                            for j in range(2):
                                ins = e.matmul(b.ap[:, j * 128:(j + 1) * 128], qkT[p:p + 64, 2 + j, cs],
                                               qkT[p:p + 64, j, cs], start=True, stop=True)
                            return ins
                        mS = PE(fn, b.free)
                        D4 = Dm[:, i, :].rearrange("p (j r t) -> p j r t", j=2, r=2)[:, :, r, :]
                        prods.append(V(lambda e: e.tensor_tensor(
                            D4, b.ap[:, 0:256].rearrange("p (j t) -> p j t", j=2), D4, ALU.mult), mS, a))
                        b.free = [prods[-1]]
                    a = prods
                    b = held[i]

                    def fn(e, b=b, i=i, c=c):
                        for h in range(4):
                            ins = e.matmul(b.ap[:, h * 65:h * 65 + 65], Dm[:, i, h * 128:(h + 1) * 128],
                                           va[:, c, h, :], start=True, stop=True)
                        return ins
                    mO = PE(fn, a, on, b.free)
                    fD[i] = mO
                yield
                C3 = C0[:, i, :].rearrange("p (j n) -> p j n", j=2)
                Cn = C0[:, 1 - i, :].rearrange("p (j n) -> p j n", j=2)
                cur = list(cst)
                reads = []
                if emit_ctx or c >= NC_T:
                    n3 = nd[:, i, :].rearrange("p (h n) -> p h n", h=4)
                    n4 = nd[:, i, :].rearrange("p (j r n) -> p j r n", j=2, r=2)
                    s_ = st[:, i, :]
                    prods = []
                    for r in range(2):
                        p, b2 = 64 * r, rc.take()

                        def fn(e):
                            for j in range(2):
                                ins = e.matmul(b2.ap[:, j * 65:j * 65 + 65], qkT[p:p + 64, j, cs],
                                               C3[p:p + 64, j, :], start=True, stop=True)
                            return ins
                        mI = PE(fn, cur, b2.free)
                        reads.append(mI)
                        g2 = colq[:, d, c, 0:4].rearrange("p (j r) -> p j r", r=2)[:, :, r]
                        prods.append(V(lambda e: e.tensor_tensor(
                            n4[:, :, r, :], b2.ap[:, 0:130].rearrange("p (j n) -> p j n", j=2), bc(g2, 65),
                            ALU.mult), mI, cq, fnd[i]))
                        b2.free = [prods[-1]]
                    combine = prods
                else:
                    combine = None
                if n_ < len(order) - 1:
                    k3 = kc[:, c, :].rearrange("p (h n) -> p h n", h=4)
                    kw3 = kw[:, i, :].rearrange("p (h n) -> p h n", h=4)
                    a = G(lambda e, k3=k3, kw3=kw3, d=d, c=c: e.tensor_tensor(kw3, k3, bc(colq[:, d, c, 64:68], 64), ALU.mult),
                          cq, fkw[i])
                    bu = rc.take()

                    def fn(e, b=bu, kw3=kw3, c=c):
                        for h in range(4):
                            p = 64 * (h % 2)
                            j = h // 2
                            ins = e.matmul(b.ap[p:p + 64, j * 65:j * 65 + 65], kw3[:, h, :], va[:, c, h, :],
                                           start=True, stop=True)
                        return ins
                    mC = PE(fn, a, on, bu.free)
                    fkw[i] = mC
                    dd = dec[:, d, c, :]
                    a = V(lambda e, Cn=Cn, C3=C3, dd=dd: e.tensor_tensor(Cn, C3, bc(dd, 65), ALU.mult), cur, t_dec, fst[i])
                    a = V(lambda e, Cn=Cn, b=bu: e.tensor_tensor(
                        Cn, b.ap[:, 0:130].rearrange("p (j n) -> p j n", j=2), Cn, ALU.add), a, mC)
                    bu.free = [a]
                    fst[1 - i] = reads
                    cst[:] = [a]
                yield
                if combine:
                    a, b = combine, held[i]
                    a = V(lambda e, b=b, i=i: e.tensor_tensor(nd[:, i, :], b.ap[:, 0:260], nd[:, i, :], ALU.add), a, mO)
                    b.free = [a]
                    a = V(lambda e, n3=n3, s_=s_: e.tensor_scalar(s_[:, 0:4], n3[:, :, 64], -1.0, None, ALU.mult), a)
                    a = V(lambda e, n3=n3, s_=s_: e.tensor_tensor(s_[:, 0:4], s_[:, 0:4], n3[:, :, 64], ALU.max), a)
                    a = V(lambda e, s_=s_, d=d, c=c: e.tensor_tensor(s_[:, 0:4], s_[:, 0:4], colq[:, d, c, 32:36], ALU.max), a)
                    a = V(lambda e, s_=s_: e.reciprocal(s_[:, 0:4], s_[:, 0:4]), a)
                    H3 = HF[:, c, :].rearrange("p (h n) -> p h n", h=4)
                    if d == 0:
                        a = V(lambda e, H3=H3, n3=n3, s_=s_: e.tensor_tensor(H3, n3[:, :, 0:64], bc(s_[:, 0:4], 64), ALU.mult), a)
                        hprev[c] = a
                    else:
                        a = V(lambda e, n3=n3, s_=s_: e.tensor_tensor(n3[:, :, 0:64], n3[:, :, 0:64], bc(s_[:, 0:4], 64), ALU.mult), a)
                        a = V(lambda e, H3=H3, n3=n3: e.tensor_tensor(H3, n3[:, :, 0:64], H3, ALU.add), a, hprev[c])
                        yield
                        a = V(lambda e, H3=H3, n3=n3: e.tensor_tensor(n3[:, :, 0:64], H3, H3, ALU.mult), a)
                        a = V(lambda e, n3=n3, s_=s_: e.tensor_reduce(s_[:, 4:8], n3[:, :, 0:64], AX, ALU.add), a)
                        a = rstd_of(s_[:, 4:8], s_[:, 4:8], 1.0 / 64, a)
                        a = V(lambda e, H3=H3, s_=s_: e.tensor_tensor(H3, H3, bc(s_[:, 4:8], 64), ALU.mult), a)
                        a = G(lambda e, c=c: e.tensor_tensor(HF[:, c, :], HF[:, c, :], gh, ALU.mult), a, t_gh)
                        a = G(lambda e, c=c: e.tensor_tensor(Y[:, c, 768:1024], HF[:, c, :], Y[:, c, 768:1024], ALU.mult), a)
                    fnd[i] = a
            overlapped4(chunk(n_, c) for n_, c in enumerate(order))
            barrier()
        at[0] = top
        yT = alloc(8, T)
        at[0] = keep
        gtr = alloc(2, 1024)
        xr = alloc(2, 1024)
        xo = alloc(2, 1024)
        sq = alloc(1024)
        ss = alloc(4)
        gf = alloc(1024)
        bar = [q.last() for q in (PE, V, A, G)]
        last_layer = l == DEPTH - 1
        wo = [wload(I["w_out"][l][g], 512) for g in range(2)]
        t_gf = load(gf, I["g_final"].partition_broadcast(128), bar) if last_layer else None
        tg_ = [row_broadcast(gtr[:, v, :], MOD[:, 16:24, v], 8) for v in range(2)]
        for t in range(t0, NT):
            tt = to_feature(Y[:, t, :], yT, t, None, None)
        fr = [None, None]
        fo = [None, None]
        new_store = []
        for t in range(t0, NT):
            i = t % 2
            cols = slice(t * 128, (t + 1) * 128)
            lx = SP.dma(ch_x[i], lambda e, t=t, i=i: e.dma_start(xr[:, i, :], rows[t]), bar, fr[i])
            v = 1 if t < NC_T else 0
            toks = []
            for g in range(2):
                w, tw, s_ = wo[g]
                b = rb.take()
                m = PE(mm_group(b.ap, [(yT[:, k, cols], w[:, k, :]) for k in range(8)]), tw, b.free, tt)
                s_.free = [m]
                gs = slice(g * 512, (g + 1) * 512)
                a = V(lambda e, b=b, i=i, gs=gs, v=v: e.tensor_tensor(xo[:, i, gs], b.ap, gtr[:, v, gs], ALU.mult),
                      m, tg_, fo[i])
                b.free = [a]
                toks.append(V(lambda e, i=i, gs=gs: e.tensor_tensor(xo[:, i, gs], xo[:, i, gs], xr[:, i, gs], ALU.add),
                              a, lx))
            fr[i] = toks
            if not last_layer:
                st_ = SP.dma(ch_o[i], lambda e, t=t, i=i: e.dma_start(X1[t * 128:(t + 1) * 128, :], xo[:, i, :]), toks)
                x1_store[t] = st_
            else:
                a = A(lambda e, i=i: e.activation(sq, xo[:, i, :], ACT.Square, accum_out=ss[:, i:i + 1]), toks)
                a = rstd_of(ss[:, i:i + 1], ss[:, i:i + 1], 1.0 / 1024, a)
                a = V(lambda e, i=i: e.scalar_tensor_tensor(xo[:, i, :], xo[:, i, :], ss[:, i:i + 1], gf,
                                                            ALU.mult, ALU.mult), a, t_gf)
                st_ = SP.dma(ch_o[i], lambda e, t=t, i=i: e.dma_start(
                    X2[(t - NC_T) * 128:(t - NC_T + 1) * 128, :], xo[:, i, :]), a)
                x2_store[t - NC_T] = st_
            fo[i] = st_
            new_store.append(st_)
        phase = barrier() + [x for x in fo if x is not None]


    def recip_sig(dst, src, *after):
        a = A(lambda e: e.activation(dst, src, ACT.Exp, scale=-1.0), *after)
        a = V(lambda e: e.tensor_scalar(dst, dst, 1.0, None, ALU.add), a)
        return V(lambda e: e.reciprocal(dst, dst), a)

    at[0] = top
    MOD = MOD2
    AM = alloc(8, 2)
    AF = alloc(8)
    lmask = alloc(8, 128)
    xnT = alloc(8, T)
    OT = alloc(8, 1024)
    work = at[0]
    Yc = alloc(8, 1024)
    ret_work = at[0]
    at[0] = work
    X = alloc(NT, 1024)
    tlm = load(lmask, I["k_lmask"], phase)
    tm = V(lambda e: e.tensor_scalar(AM, MOD[:, 8:16, :], 1.0, None, ALU.add), mod_t[2], phase)
    tm = V(lambda e: e.tensor_tensor(AM, AM, bc(gns[:, 2, :], 2), ALU.mult), tm, t_gn_)
    ta = V(lambda e: e.tensor_scalar(AF, MOD[:, 32:40, 0], 1.0, None, ALU.add), tm)
    ta = V(lambda e: e.tensor_tensor(AF, AF, nf, ALU.mult), ta, t_nf_)
    rows = [I["ctx2"][t * 128:(t + 1) * 128, :] for t in range(NC_T)] + \
           [X2[t * 128:(t + 1) * 128, :] for t in range(NL_T)]
    normalise_in(X, xnT, load_rows(X, rows, phase, x2_store), AM, MOD[:, 0:8, :], tm, phase)
    barrier()

    at[0] = work
    Vt = alloc(NT, 256)
    LRT = alloc(T)
    WLR = alloc(2, 128)
    qT = alloc(NL_T * 128)
    kT = alloc(T)
    bf = alloc(T)
    bb = alloc(T)
    E = alloc(T)
    KDT = alloc(NT, 128)
    Sb = alloc(NT, 256)
    Sf = alloc(2, 256)
    QF = alloc(2, 512)
    QK = alloc(2, 2, 512)
    acc = alloc(2, 512)
    tm_ = alloc(2, 256)
    gg = alloc(2, 256)
    gnr = alloc(256)
    bz = alloc(8)
    dec = alloc(2, NT)
    one = ones
    st = alloc(8)
    bar = [q.last() for q in (PE, V, A, G)]
    wl, twl, sl = wload(I["w_lr"], 32)
    t_bz = load(bz, I["lr_b"], bar)
    t_gn = load(gnr, I["gla_norm"].partition_broadcast(128), bar)
    t_one = t_ones
    for t in range(NT):
        cols = slice(t * 128, (t + 1) * 128)
        i = t % 2
        b = rb.take()
        m = PE(mm_group(b.ap[:, 0:32], [(xnT[:, k, cols], wl[:, k, :]) for k in range(8)]), twl, b.free)
        sl.free = [m]
        c = A(lambda e: e.activation(tm_[:, i, 0:32], b.ap[:, 0:32], ACT.Copy), m, A.last(), PE.last())
        b.free = [c]
        b = rb.take()
        tr = PE(transposes([(b.ap[0:32, 0:128], tm_[:, i, 0:32])], ident), c, b.free)
        o = A(lambda e: e.activation(LRT[0:32, cols], b.ap[0:32, 0:128], ACT.Copy), tr)
        b.free = [o]
    for h in range(4):
        barrier()
        w, tw, s_ = wload(I["w_gla"][h], 512)
        wg, twg, sg_ = wload(I["w_gg"][h], 256)
        t_wl = load(WLR[0:32], I["gla_lr"][h], [q.last() for q in (PE, V, A, G)])
        tg = None
        for d, b_ in ((0, bf), (1, bb)):
            zs = []
            for c0 in range(0, T, 512):
                n = min(512, T - c0)
                b = rb.take()
                m = PE(lambda e: e.matmul(b.ap[:, 0:n], WLR[0:32, d, :], LRT[0:32, c0:c0 + n],
                                          start=True, stop=True), t_wl, b.free)
                o = A(lambda e: e.activation(b_[:, c0:c0 + n], b.ap[:, 0:n], ACT.Identity,
                                             bias=bz[:, 4 * d + h:4 * d + h + 1]), m, t_bz)
                b.free = [o]
                zs.append(o)
            a = A(lambda e: e.activation(E, b_, ACT.Abs), zs, tg)
            a = A(lambda e: e.activation(E, E, ACT.Exp, scale=-1.0), a)
            a = A(lambda e: e.activation(E, E, ACT.Ln, bias=1.0), a)
            a1 = V(lambda e: e.tensor_scalar(b_, b_, 0.0, 0.0625, ALU.min, ALU.mult), a)
            tg = V(lambda e: e.scalar_tensor_tensor(E, E, -0.0625, b_, ALU.mult, ALU.add), a1)
            sc = []
            for c in range(NT):
                v_ = b_[:, c * 128:(c + 1) * 128]
                e_ = E[:, c * 128:(c + 1) * 128]
                if d:
                    v_, e_ = v_[:, ::-1], e_[:, ::-1]
                sc.append(V(lambda e: e.tensor_tensor_scan(v_, one, e_, 0.0, ALU.mult, ALU.add), tg, t_one))
            tg = sc
        tgate = tg
        qk_t = []
        prev = [None, None]

        def gla_in(t):
            cols = slice(t * 128, (t + 1) * 128)
            i = t % 2
            lat = t >= NC_T
            c0 = 0 if lat else 128
            b = rb.take()
            m = PE(mm_group(b.ap[:, c0:512], [(xnT[:, k, cols], w[:, k, c0:512]) for k in range(8)]), tw, b.free)
            s_.free = [m]
            a1 = A(lambda e: e.activation(Vt[:, t, :], b.ap[:, 256:512], ACT.Copy), m)
            a2 = [A(lambda e: e.activation(tm_[:, i, 128:256], b.ap[:, 128:256], ACT.Copy), m, prev[i])]
            if lat:
                a2.append(A(lambda e: e.activation(tm_[:, i, 0:128], b.ap[:, 0:128], ACT.Copy,
                                                   scale=float(128 ** -0.5)), m, prev[i]))
            b.free = [a1, a2]
            yield
            b = rb.take()
            tr = PE(transposes([(b.ap[:, c0:c0 + 128], tm_[:, i, c0:c0 + 128])] +
                               ([(b.ap[:, 128:256], tm_[:, i, 128:256])] if lat else []), ident), a2, b.free)
            prev[i] = tr
            o = [V(lambda e: e.tensor_copy(kT[:, cols], b.ap[:, 128:256]), tr)]
            if lat:
                qc = slice((t - NC_T) * 128, (t - NC_T + 1) * 128)
                o.append(V(lambda e: e.tensor_copy(qT[:, qc], b.ap[:, 0:128]), tr))
            b.free = o
            qk_t.extend(o)
        overlapped(gla_in(t) for t in range(NT))
        def decayed_keys(d, b_, *after):
            e3 = E.rearrange("p (c t) -> p c t", c=NT)
            b3 = b_.rearrange("p (c t) -> p c t", c=NT)
            end = b3[:, :, 0] if d else b3[:, :, 127]
            a0 = A(lambda e: e.activation(dec[:, d, :], end, ACT.Exp), *after)
            a = V(lambda e: e.tensor_tensor(e3, bc(end, 128), b3, ALU.subtract), *after)
            a = A(lambda e: e.activation(E, E, ACT.Exp), a)
            a = V(lambda e: e.tensor_tensor(E, E, kT, ALU.mult), a)
            outs = [a0]
            for c0 in range(0, NT, 4):
                n = min(4, NT - c0)
                b = rb.take()
                tr = PE(transposes([(b.ap[:, j * 128:(j + 1) * 128], e3[:, c0 + j, :]) for j in range(n)], ident),
                        a, b.free)
                o = A(lambda e: e.activation(KDT[:, c0:c0 + n, :], b.ap[:, 0:n * 128].rearrange(
                    "p (c t) -> p c t", c=n), ACT.Copy), tr, *after)
                b.free = [o]
                outs.append(o)
            return outs

        def next_state(dst, src, d, c, *after):
            b = rb.take()
            m = PE(lambda e: e.matmul(b.ap[:, 0:256], KDT[:, c, :], Vt[:, c, :], start=True, stop=True), b.free, *after)
            a = V(lambda e: e.scalar_tensor_tensor(dst, src, dec[:, d, c:c + 1], b.ap[:, 0:256],
                                                   ALU.mult, ALU.add), m, *after)
            b.free = [a]
            return a
        barrier()
        kd = decayed_keys(1, bb)
        order = list(range(NC_T))[::-1] + list(range(NC_T, NT))[::-1]
        a = V(lambda e: e.memset(Sb[:, order[0], :], 0.0))
        for n_ in range(NT - 1):
            a = next_state(Sb[:, order[n_ + 1], :], Sb[:, order[n_], :], 1, order[n_], kd, a)
        barrier()
        kd = decayed_keys(0, bf)
        a = V(lambda e: e.memset(Sf[:, 0, :], 0.0))
        for c in range(NC_T):
            a = next_state(Sf[:, (c + 1) % 2, :], Sf[:, c % 2, :], 0, c, kd, a)
        barrier()
        sft = [a]
        rb.slots = banks[0:6]
        gate_m = {}
        for half in range(2):
            ls = NC_T * 128 + half * 512
            qs_ = half * 512
            bfh, bbh = bf[:, ls:ls + 512], bb[:, ls:ls + 512]
            qh, kh = qT[:, qs_:qs_ + 512], kT[:, ls:ls + 512]
            ac = acc[:, half, :]
            ac3 = ac.rearrange("p (c t) -> p c t", c=4)

            def scores(qq, kk, *after):
                b = rb.take()

                def fn(e):
                    for c in range(4):
                        ins = e.matmul(b.ap[:, c * 128:(c + 1) * 128], kk[:, c * 128:(c + 1) * 128],
                                       qq[:, c * 128:(c + 1) * 128], start=True, stop=True)
                    return ins
                return b, PE(fn, b.free, *after)
            b, m = scores(qh, kh)
            a = V(lambda e: e.tensor_tensor(ac3, b.ap.rearrange("p (c t) -> p c t", c=4),
                                            lmask[:, 7, :].unsqueeze(1).broadcast_to([128, 4, 128]), ALU.mult), m, tlm)
            b.free = [a]
            last_acc = a
            a1 = A(lambda e: e.activation(QF[:, 0, :], bfh, ACT.Exp), PE.last())
            a1 = G(lambda e: e.tensor_tensor(QF[:, 0, :], QF[:, 0, :], qh, ALU.mult), a1)
            a2 = A(lambda e: e.activation(QF[:, 1, :], bbh, ACT.Exp), PE.last())
            a2 = G(lambda e: e.tensor_tensor(QF[:, 1, :], QF[:, 1, :], qh, ALU.mult), a2)
            q1, q2 = a1, a2
            fq = [None, None]

            def differences(n_, L):
                nb = 512 // (2 * L)
                i = n_ % 2
                f4 = bfh.rearrange("p (n s l) -> p n s l", s=2, l=L)
                b4 = bbh.rearrange("p (n s l) -> p n s l", s=2, l=L)
                aq = QK[:, i, 0, :]
                ak = QK[:, i, 1, :]
                q4 = aq.rearrange("p (n s l) -> p n s l", s=2, l=L)
                k4 = ak.rearrange("p (n s l) -> p n s l", s=2, l=L)
                rf = f4[:, :, 0, L - 1:L].broadcast_to([128, nb, L])
                rb_ = b4[:, :, 1, 0:1].broadcast_to([128, nb, L])
                o1 = V(lambda e: e.tensor_tensor(q4[:, :, 1, :], f4[:, :, 1, :], rf, ALU.subtract), fq[i])
                o2 = G(lambda e: e.tensor_tensor(q4[:, :, 0, :], b4[:, :, 0, :], rb_, ALU.subtract), fq[i])
                o3 = V(lambda e: e.tensor_tensor(k4[:, :, 0, :], rf, f4[:, :, 0, :], ALU.subtract), fq[i])
                o4 = G(lambda e: e.tensor_tensor(k4[:, :, 1, :], rb_, b4[:, :, 1, :], ALU.subtract), fq[i])
                return aq, ak, A(lambda e: e.activation(QK[:, i, :, :], QK[:, i, :, :], ACT.Exp), o1, o2, o3, o4)
            ahead = differences(0, LEVELS[0])
            for n_, L in enumerate(LEVELS):
                i = n_ % 2
                aq, ak, a = ahead
                if n_ + 1 < len(LEVELS):
                    ahead = differences(n_ + 1, LEVELS[n_ + 1])
                o1 = G(lambda e: e.tensor_tensor(aq, aq, qh, ALU.mult), a)
                o2 = V(lambda e: e.tensor_tensor(ak, ak, kh, ALU.mult), a)
                b, m = scores(aq, ak, o1, o2)
                if n_ < 4:
                    gx_ = slice((NC_T + half * 4 + n_) * 128, (NC_T + half * 4 + n_ + 1) * 128)
                    hb = banks[6 + n_ // 2]
                    gate_m[n_] = PE(mm_group(hb.ap[:, (n_ % 2) * 256:(n_ % 2) * 256 + 256],
                                             [(xnT[:, k, gx_], wg[:, k, :]) for k in range(8)]), twg, hb.free)
                    if n_ % 2:
                        hb.free = []
                        sg_.free = [gate_m[n_]]
                fq[i] = m
                a = V(lambda e: e.copy_predicated(
                    ac3, lmask[:, n_, :].bitcast(mybir.dt.int32).unsqueeze(1).broadcast_to([128, 4, 128]),
                    b.ap.rearrange("p (c t) -> p c t", c=4)), m, last_acc)
                b.free = [a]
                last_acc = a
            prev = [None, None]

            def gla_out(cc):
                c = NC_T + half * 4 + cc
                i = c % 2
                cs = slice(cc * 128, (cc + 1) * 128)
                ts = slice((c - NC_T) * 128, (c - NC_T + 1) * 128)
                xs = slice(c * 128, (c + 1) * 128)
                cur = Sf[:, c % 2, :]
                yield
                b = rb.take()

                def fn(e):
                    e.matmul(b.ap[:, 0:256], ac[:, cs], Vt[:, c, :], start=True, stop=False)
                    e.matmul(b.ap[:, 0:256], QF[:, 0, cs], cur, start=False, stop=False)
                    return e.matmul(b.ap[:, 0:256], QF[:, 1, cs], Sb[:, c, :], start=False, stop=True)
                mo = PE(fn, last_acc, q1, q2, sft, b.free)
                if c < NT - 1:
                    sft[0] = next_state(Sf[:, (c + 1) % 2, :], cur, 0, c, kd, sft, mo)
                hb = banks[6 + cc // 2]
                gp = hb.ap[:, (cc % 2) * 256:(cc % 2) * 256 + 256]
                g_ = gg[:, i, :]
                a = recip_sig(g_, gp, gate_m[cc | 1], prev[i])
                ag = V(lambda e: e.tensor_tensor(g_, gp, g_, ALU.mult), a)
                hb.free = hb.free + [ag]
                ag = G(lambda e: e.tensor_tensor(g_, g_, gnr, ALU.mult), ag, t_gn)
                yield
                s1 = st[:, i:i + 1]
                a = A(lambda e: e.activation(tm_[:, i, :], b.ap[:, 0:256], ACT.Square, accum_out=s1), mo, prev[i])
                a = rstd_of(s1, s1, 1.0 / 256, a)
                a = V(lambda e: e.scalar_tensor_tensor(tm_[:, i, :], b.ap[:, 0:256], s1, g_, ALU.mult, ALU.mult), a, ag)
                b.free = [a]
                yield
                b = rb.take()
                tr = PE(transposes([(b.ap[:, j * 128:(j + 1) * 128], tm_[:, i, j * 128:(j + 1) * 128])
                                    for j in range(2)], ident), a, b.free)
                o = A(lambda e: e.activation(OT[:, 2 * h:2 * h + 2, ts], b.ap[:, 0:256].rearrange(
                    "p (j t) -> p j t", j=2), ACT.Copy), tr)
                b.free = [o]
                prev[i] = [tr, o]
            overlapped4(gla_out(cc) for cc in range(4))

        rb.slots = banks

    def merge(name, first):
        barrier()
        at[0] = ret_work
        sg2 = alloc(2, 512)
        fr = [None, None]
        for g in range(2):
            wb, twb, sb_ = wload(I[name][g], 512)
            wm, twm, sm_ = wload(I[name + "_m"][g], 512)
            for t in range(NL_T):
                i = t % 2
                b1, b2 = rb.take(), rb.take()
                m2 = PE(mm_group(b2.ap, [(xnT[:, k, (NC_T + t) * 128:(NC_T + t + 1) * 128], wm[:, k, :])
                                         for k in range(8)]), twm, b2.free)
                m1 = PE(mm_group(b1.ap, [(OT[:, k, t * 128:(t + 1) * 128], wb[:, k, :]) for k in range(8)]),
                        twb, b1.free)
                sb_.free, sm_.free = [m1], [m2]
                a = recip_sig(sg2[:, i, :], b2.ap, m2, fr[i])
                b2.free = [a]
                y_ = Yc[:, t, g * 512:(g + 1) * 512]
                if first:
                    a = V(lambda e: e.tensor_tensor(y_, b1.ap, sg2[:, i, :], ALU.mult), a, m1)
                    b1.free = [a]
                else:
                    a = V(lambda e: e.tensor_tensor(sg2[:, i, :], b1.ap, sg2[:, i, :], ALU.mult), a, m1)
                    b1.free = [a]
                    a = G(lambda e: e.tensor_tensor(y_, y_, sg2[:, i, :], ALU.add), a)
                fr[i] = a
        barrier()

    merge("w_bg", True)

    at[0] = ret_work
    Vt = alloc(NT, 256)
    KD = alloc(NT, 2, 128)
    qT = alloc(NL_T * 128)
    kT = alloc(T)
    rope = alloc(2, 256)
    rdm = alloc(128)
    rqd = alloc(2, 128)
    rkd = small[:, 0:16]
    Sb = alloc(NL_T, 256)
    Sf = alloc(2, 256)
    lm = lmask.rearrange("p a b -> p (a b)")
    tm_ = lm[:, 0:512].rearrange("p (a b) -> p a b", a=2)
    tz, ty = lm[:, 512:768], lm[:, 768:1024]
    gg = alloc(2, 256)
    acc = alloc(2, 128)
    QF = rope
    st = small[:, 16:32]
    bar = [q.last() for q in (PE, V, A, G)]
    t_rk = load(rkd, I["k_rkd"], bar)
    rope_ch = [chan(f"d_rope{i}") for i in range(2)]
    for h in range(4):
        barrier()
        bar = [q.last() for q in (PE, V, A, G)]
        w, tw, s_ = wload(I["w_ret"][h], 512)
        wg, twg, sg_ = wload(I["w_rg"][h], 256)
        t_dm = load(rdm, I["k_rdm"][:, h, :], bar)
        t_qd = load(rqd, I["k_rqd"][:, :, h, :], bar)
        prev = [None, None]
        hz = [None]

        def ret_in(t):
            cols = slice(t * 128, (t + 1) * 128)
            i = t % 2
            lat = t >= NC_T
            c0 = 0 if lat else 128
            if lat:
                lr = SP.dma(rope_ch[i], lambda e: e.dma_start(rope[:, i, :], I["k_rope2"][:, t - NC_T, :]), bar, prev[i])
            b = rb.take()
            m = PE(mm_group(b.ap[:, c0:512], [(xnT[:, k, cols], w[:, k, c0:512]) for k in range(8)]), tw, b.free)
            s_.free = [m]
            a2 = [A(lambda e: e.activation(tm_[:, i, 128:256], b.ap[:, 128:256], ACT.Copy,
                                           scale=float(128 ** -0.5)), m, prev[i])]
            if lat:
                a2.append(A(lambda e: e.activation(tm_[:, i, 0:128], b.ap[:, 0:128], ACT.Copy), m, prev[i]))
            a1 = V(lambda e: e.tensor_copy(Vt[:, t, :], b.ap[:, 256:512]), a2)
            b.free = [a1]
            yield
            if lat:
                x3 = tm_[:, i, :].rearrange("p (a d) -> p a d", a=2)
                y3 = ty.rearrange("p (a d) -> p a d", a=2)
                x5 = tm_[:, i, :].rearrange("p (a r s f) -> p a r s f", a=2, r=2, s=2)
                z5 = tz.rearrange("p (a r s f) -> p a r s f", a=2, r=2, s=2)
                s4 = rope[:, i, 128:256].rearrange("p (r s f) -> p r s f", r=2, s=2)
                o = [V(lambda e: e.tensor_tensor(y3, x3, mid(rope[:, i, 0:128], 2), ALU.mult), a2, lr, hz)]
                for s in range(2):
                    tb_ = s4[:, :, s, :].unsqueeze(1).broadcast_to([128, 2, 2, 32])
                    o.append(G(lambda e: e.tensor_tensor(z5[:, :, :, s, :], x5[:, :, :, 1 - s, :], tb_, ALU.mult),
                               a2, lr, hz))
                hz[0] = V(lambda e: e.tensor_tensor(tm_[:, i, :], ty, tz, ALU.add), o)
                a2 = [hz[0]]
            kk = [G(lambda e: e.tensor_scalar(KD[:, t, d, :], tm_[:, i, 128:256], rkd[:, 4 * d + h:4 * d + h + 1],
                                              None, ALU.mult), a2, t_rk) for d in range(2)]
            b = rb.take()
            tr = PE(transposes([(b.ap[:, 128:256], tm_[:, i, 128:256])] +
                               ([(b.ap[:, 0:128], tm_[:, i, 0:128])] if lat else []), ident), a2, b.free)
            prev[i] = [tr, kk]
            o = [A(lambda e: e.activation(kT[:, cols], b.ap[:, 128:256], ACT.Copy), tr)]
            if lat:
                qc = slice((t - NC_T) * 128, (t - NC_T + 1) * 128)
                o.append(A(lambda e: e.activation(qT[:, qc], b.ap[:, 0:128], ACT.Copy), tr))
            b.free = o
        overlapped(ret_in(t) for t in range(NT))

        def next_ret(dst, src, d, c, *after):
            b = rb.take()
            m = PE(lambda e: e.matmul(b.ap[:, 0:256], KD[:, c, d, :], Vt[:, c, :], start=True, stop=True), b.free, *after)
            a = V(lambda e: e.scalar_tensor_tensor(dst, src, rkd[:, 8 + 4 * d + h:9 + 4 * d + h], b.ap[:, 0:256],
                                                   ALU.mult, ALU.add), m, *after)
            b.free = [a]
            return a
        barrier()
        order = list(range(NC_T))[::-1] + list(range(NC_T, NT))[::-1]
        back = [Sf[:, 1 - c, :] if c < NC_T else Sb[:, c - NC_T, :] for c in range(NT)]
        a = V(lambda e: e.memset(back[order[0]], 0.0))
        for n_ in range(NT - 1):
            a = next_ret(back[order[n_ + 1]], back[order[n_]], 1, order[n_], a)
        a = V(lambda e: e.memset(Sf[:, 0, :], 0.0), a)
        for c in range(NC_T):
            a = next_ret(Sf[:, (c + 1) % 2, :], Sf[:, c % 2, :], 0, c, a)
        sft = [a]
        prev = [None, None]

        def ret_out(c):
            i = c % 2
            ts = slice((c - NC_T) * 128, (c - NC_T + 1) * 128)
            xs = slice(c * 128, (c + 1) * 128)
            cur = Sf[:, c % 2, :]
            b = rb.take()
            m = PE(lambda e: e.matmul(b.ap[:, 0:128], kT[:, xs], qT[:, ts], start=True, stop=True), b.free)
            a1 = V(lambda e: e.tensor_tensor(acc[:, i, :], b.ap[:, 0:128], rdm, ALU.mult), m, t_dm, prev[i])
            b.free = [a1]
            q3 = QF[:, i, :].rearrange("p (d t) -> p d t", d=2)
            a2 = G(lambda e: e.tensor_tensor(q3, mid(qT[:, ts], 2), rqd, ALU.mult), t_qd, prev[i])
            yield
            b = rb.take()

            def fn(e):
                e.matmul(b.ap[:, 0:256], acc[:, i, :], Vt[:, c, :], start=True, stop=False)
                e.matmul(b.ap[:, 0:256], QF[:, i, 0:128], cur, start=False, stop=False)
                return e.matmul(b.ap[:, 0:256], QF[:, i, 128:256], Sb[:, c - NC_T, :], start=False, stop=True)
            mo = PE(fn, a1, a2, sft, b.free)
            if c < NT - 1:
                sft[0] = next_ret(Sf[:, (c + 1) % 2, :], cur, 0, c, sft, mo)
            b2 = rb.take()
            m = PE(mm_group(b2.ap[:, 0:256], [(xnT[:, k, xs], wg[:, k, :]) for k in range(8)]), twg, b2.free)
            sg_.free = [m]
            g_ = gg[:, i, :]
            a = recip_sig(g_, b2.ap[:, 0:256], m, prev[i])
            ag = V(lambda e: e.tensor_tensor(g_, b2.ap[:, 0:256], g_, ALU.mult), a)
            b2.free = [ag]
            yield
            s1, s2 = st[:, 4 * i:4 * i + 1], st[:, 4 * i + 1:4 * i + 2]
            o_ = tm_[:, i, :]
            a = A(lambda e: e.activation(o_, b.ap[:, 0:256], ACT.Copy, accum_out=s1), mo, prev[i])
            b.free = [a]
            a = V(lambda e: e.tensor_scalar(s1, s1, -1.0 / 256, None, ALU.mult), a)
            a = V(lambda e: e.tensor_scalar(o_, o_, s1, None, ALU.add), a)
            a = A(lambda e: e.activation(ty, o_, ACT.Square, accum_out=s2), a, hz)
            hz[0] = a
            a = rstd_of(s2, s2, 1.0 / 256, a)
            a = V(lambda e: e.scalar_tensor_tensor(o_, o_, s2, g_, ALU.mult, ALU.mult), a, ag)
            yield
            b = rb.take()
            tr = PE(transposes([(b.ap[:, j * 128:(j + 1) * 128], tm_[:, i, j * 128:(j + 1) * 128])
                                for j in range(2)], ident), a, b.free)
            o = A(lambda e: e.activation(OT[:, 2 * h:2 * h + 2, ts], b.ap[:, 0:256].rearrange(
                "p (j t) -> p j t", j=2), ACT.Copy), tr)
            b.free = [o]
            prev[i] = [tr, o, mo]
        overlapped4(ret_out(c) for c in range(NC_T, NT))

    merge("w_br", False)

    at[0] = ret_work
    gtr = alloc(1024)
    xr = alloc(2, 1024)
    sq = alloc(1024)
    ss = alloc(NL_T)
    XO = xnT.rearrange("p k t -> p (k t)")[:, 0:8192].rearrange("p (t n) -> p t n", t=8)
    bar = [q.last() for q in (PE, V, A, G)]
    wo = [wload(I["w_out2"][g], 512) for g in range(2)]
    tgr = row_broadcast(gtr, MOD[:, 16:24, 0], 8)
    for t in range(NL_T):
        tt = to_feature(Yc[:, t, :], OT, t, None, None)
    fr = [None, None]
    ssl = []
    for t in range(NL_T):
        i = t % 2
        lx = SP.dma(ch_x[i], lambda e: e.dma_start(xr[:, i, :], X2[t * 128:(t + 1) * 128, :]), bar, fr[i])
        toks = []
        for g in range(2):
            w, tw, s_ = wo[g]
            b = rb.take()
            m = PE(mm_group(b.ap, [(OT[:, k, t * 128:(t + 1) * 128], w[:, k, :]) for k in range(8)]), tw, b.free, tt)
            s_.free = [m]
            gs = slice(g * 512, (g + 1) * 512)
            a = V(lambda e: e.tensor_tensor(XO[:, t, gs], b.ap, gtr[:, gs], ALU.mult), m, tgr)
            b.free = [a]
            toks.append(V(lambda e: e.tensor_tensor(XO[:, t, gs], XO[:, t, gs], xr[:, i, gs], ALU.add), a, lx))
        fr[i] = toks
        ssl = [A(lambda e: e.activation(sq, XO[:, t, :], ACT.Square, accum_out=ss[:, t:t + 1]), toks, ssl)]
    r = rstd_of(ss, ss, 1.0 / 1024, ssl)
    barrier()
    tt = []
    hn_store = []
    for t in range(NL_T):
        q = V if t % 2 else G
        m = q(lambda e: e.tensor_scalar(Yc[:, t, :], XO[:, t, :], ss[:, t:t + 1], None, ALU.mult), r)
        hn_store.append(SP.dma(ch_x[2 + t], lambda e: e.dma_start(HN[t * 128:(t + 1) * 128, :], Yc[:, t, :]), m))
        tt += to_feature(Yc[:, t, :], OT, t, AF, MOD[:, 24:32, 0], m)

    barrier()
    at[0] = ret_work
    wr = alloc(8, 36)
    br = alloc(36)
    LG = alloc(8, 36)
    rev = alloc(36)
    Wt = alloc(8, 32)
    em = alloc(8, 32)
    em2 = alloc(8, 32)
    oh1 = alloc(8, 32)
    oh2 = alloc(8, 32)
    s8 = alloc(12, 8)
    go = alloc(8, 4)
    gx = alloc(8, 4)
    bar = [q.last() for q in (PE, V, A, G)]
    t_r = [load(wr, I["w_router"], bar), load(br, I["b_router"].partition_broadcast(128), bar),
           load(rev, I["k_rev"], bar)]
    lg = []
    for t in range(NL_T):
        b = rb.take()
        m = PE(mm_group(b.ap[:, 0:36], [(OT[:, k, t * 128:(t + 1) * 128], wr[:, k, :]) for k in range(8)]), t_r, b.free)
        a = V(lambda e: e.tensor_tensor(LG[:, t, :], b.ap[:, 0:36], br, ALU.add), m)
        b.free = [a]
        lg.append(a)
    t_router = m
    gl = LG[:, :, 0:4]
    el = LG[:, :, 4:36]

    def red(dst, src, op, *after):
        return V(lambda e: e.tensor_reduce(dst, src, AX, op), *after)

    def tt_(dst, x_, y_, op, *after):
        return V(lambda e: e.tensor_tensor(dst, x_, y_, op), *after)

    def pick_first(oh, val, vmax, n, r_, tmp, a):
        a = tt_(oh, val, bc(vmax, n), ALU.is_equal, a)
        a = tt_(oh, oh, mid(r_, 8), ALU.mult, a)
        a = red(tmp, oh, ALU.max, a)
        return tt_(oh, oh, bc(tmp, n), ALU.is_equal, a)
    a = red(s8[:, 0, :], gl, ALU.max, lg)
    g1_ = pick_first(go, gl, s8[:, 0, :], 4, rev[:, 0:4], s8[:, 1, :], a)
    a = tt_(gx, gl, bc(s8[:, 0, :], 4), ALU.subtract, g1_)
    a = A(lambda e: e.activation(gx, gx, ACT.Exp), a)
    a = red(s8[:, 2, :], gx, ALU.add, a)
    gw = V(lambda e: e.reciprocal(s8[:, 3, :], s8[:, 2, :]), a)
    a = V(lambda e: e.tensor_scalar(go, go, -1.0, 1e30, ALU.add, ALU.mult), gw)
    em4 = em.rearrange("p t (g x) -> p (t g) x", g=4)
    el4 = em2.rearrange("p t (g x) -> p (t g) x", g=4)
    a = V(lambda e: e.tensor_copy(em2, el), a)
    a = tt_(em4, el4, bc(go.rearrange("p t g -> p (t g)"), 8), ALU.add, a)
    a = red(s8[:, 4, :], em, ALU.max, a)
    a = pick_first(oh1, em, s8[:, 4, :], 32, rev[:, 4:36], s8[:, 5, :], a)
    a = V(lambda e: e.scalar_tensor_tensor(em2, oh1, -3e30, em, ALU.mult, ALU.add), a)
    a = red(s8[:, 6, :], em2, ALU.max, a)
    a = pick_first(oh2, em2, s8[:, 6, :], 32, rev[:, 4:36], s8[:, 7, :], a)
    a = tt_(s8[:, 8, :], s8[:, 6, :], s8[:, 4, :], ALU.subtract, a)
    a = A(lambda e: e.activation(s8[:, 8, :], s8[:, 8, :], ACT.Exp), a)
    a = V(lambda e: e.tensor_scalar(s8[:, 9, :], s8[:, 8, :], 1.0, None, ALU.add), a)
    a = V(lambda e: e.reciprocal(s8[:, 9, :], s8[:, 9, :]), a)
    a = tt_(s8[:, 9, :], s8[:, 9, :], s8[:, 3, :], ALU.mult, a)
    a = tt_(s8[:, 10, :], s8[:, 9, :], s8[:, 8, :], ALU.mult, a)
    M = alloc(8, 32)
    R = alloc(8, 32)
    C = alloc(32)
    nov = alloc(32)
    ovend = alloc(32)
    ovst = alloc(32)
    zero = alloc(32)
    tri = alloc(128)
    iota = alloc(128)
    tokid = alloc(8)
    tmp = alloc(8, 32)
    pj = alloc(2, 8, 8)
    eo = alloc(NOV, 32)
    eor = alloc(2, 16)
    SL = alloc(2, 128)
    BL = alloc(2, NB)
    ints = alloc(NB + 48).bitcast(mybir.dt.int32)
    idx = ints[:, 0:NB]
    desti = ints[:, NB:NB + 16].rearrange("p (j t) -> p j t", j=2)
    eoi = ints[:, NB + 16:NB + 48]
    t_c = [load(tri, I["k_tri"], bar), load(iota, I["k_iota"], bar), load(tokid, I["k_tokid"], bar)]
    w12 = s8[:, 9:11, :]
    a = tt_(M, oh1, oh2, ALU.add, a)
    b = rb.take()

    def fn(e):
        for t in range(8):
            for u in range(t + 1):
                e.matmul(b.ap[:, t * 32:(t + 1) * 32], tri if u == t else ones, M[:, u, :],
                         start=(u == 0), stop=(u == t))
        for t in range(8):
            ins = e.matmul(b.ap[:, 256:288], ones, M[:, t, :], start=(t == 0), stop=(t == 7))
        return ins
    m = PE(fn, a, t_c, t_ones, b.free)
    a = V(lambda e: e.tensor_copy(R, b.ap[:, 0:256].rearrange("p (t x) -> p t x", t=8)), m)
    a = V(lambda e: e.tensor_copy(C, b.ap[:, 256:288]), a)
    b.free = [a]
    a = V(lambda e: e.memset(zero, 0.0), a)
    a = V(lambda e: e.memset(nov, 0.0), a)
    for k in range(1, 8):
        a = V(lambda e: e.scalar_tensor_tensor(nov, C, 128.0 * k, nov, ALU.is_gt, ALU.add), a)
    a = V(lambda e: e.tensor_tensor_scan(ovend, nov, zero, 0.0, ALU.add, ALU.add), a)
    a = tt_(ovst, ovend, nov, ALU.subtract, a)
    a = tt_(eo[0:1], ovend[0:1, :].unsqueeze(1).broadcast_to([1, NOV, 32]), bc(iota[0:1, 0:NOV], 32), ALU.is_le, a)
    a = red(eor[0:1, 0, 0:NOV], eo[0:1], ALU.add, a)
    a = V(lambda e: e.tensor_scalar(eor[0:1, 1, 0:NOV], eor[0:1, 0, 0:NOV], 31.5, None, ALU.is_lt), a)
    a = V(lambda e: e.tensor_scalar(eor[0:1, 0, 0:NOV], eor[0:1, 0, 0:NOV], 31.0, None, ALU.min), a)
    t_eo = V(lambda e: e.tensor_copy(eoi[0:1, 0:32].rearrange("p (a b) -> p a b", a=2)[:, :, 0:NOV],
                                     eor[0:1, :, 0:NOV]), a)
    a = t_eo
    dst_t = []
    for j, oh in enumerate((oh1, oh2)):
        r_, e_, o_, f_, g_, blk, slot, dest = [pj[:, j, n, :] for n in range(8)]
        for dst, by in ((r_, R), (e_, mid(iota[:, 0:32], 8)), (o_, mid(ovst, 8))):
            a = tt_(tmp, oh, by, ALU.mult, a)
            a = red(dst, tmp, ALU.add, a)
        a = V(lambda e: e.tensor_scalar(g_, r_, 128.0, None, ALU.is_ge), a)
        a = V(lambda e: e.tensor_copy(f_, g_), a)
        for k in range(2, 8):
            a = V(lambda e: e.scalar_tensor_tensor(f_, r_, 128.0 * k, f_, ALU.is_ge, ALU.add), a)
        a = tt_(blk, o_, e_, ALU.subtract, a)
        a = V(lambda e: e.scalar_tensor_tensor(blk, blk, 31.0, g_, ALU.add, ALU.mult), a)
        a = tt_(blk, blk, e_, ALU.add, a)
        a = tt_(blk, blk, f_, ALU.add, a)
        a = V(lambda e: e.scalar_tensor_tensor(slot, f_, -128.0, r_, ALU.mult, ALU.add), a)
        a = V(lambda e: e.scalar_tensor_tensor(dest, blk, 128.0, slot, ALU.mult, ALU.add), a)
        a = V(lambda e: e.tensor_copy(desti[:, j, :], dest), a)
        dst_t.append(a)
    b = rb.take()
    fr = [None, None]
    n_ = 0
    for t in range(8):
        for j in range(2):
            i = n_ % 2
            slot, blk = pj[:, j, 6, t:t + 1], pj[:, j, 5, t:t + 1]
            a1 = V(lambda e: e.tensor_scalar(SL[:, i, :], iota, slot, None, ALU.is_equal), a, fr[i])
            a2 = V(lambda e: e.tensor_scalar(BL[:, i, :], iota[:, 0:NB], blk, tokid[:, t:t + 1],
                                             ALU.is_equal, ALU.mult), a, fr[i])
            m = PE(lambda e: e.matmul(b.ap[:, 0:NB], SL[:, i, :], BL[:, i, :], start=(n_ == 0), stop=(n_ == 15)),
                   a1, a2, b.free)
            fr[i] = m
            n_ += 1
    t_idx = V(lambda e: e.tensor_copy(idx, b.ap[:, 0:NB]), m)
    b.free = [t_idx]
    barrier()

    XG = alloc(3, 1024)
    xb = [Yc[:, 2 + i, :].rearrange("p (k t) -> p k t", k=8) for i in range(2)]
    yo = [Yc[:, 4 + i, :] for i in range(3)]
    hd = [Yc[:, 0, 256 * i:256 * i + 256] for i in range(2)]
    hT = [Yc[:, 0, 512 + 256 * i:768 + 256 * i].rearrange("p (f t) -> p f t", f=2) for i in range(2)]
    sg = [Yc[:, 1, 256 * i:256 * i + 256] for i in range(2)]
    dring = Ring([Slot(OT[:, 2 * i:2 * i + 2, :], chan(f"d_n{i}")) for i in range(4)])
    for s_ in dring.slots:
        s_.free = [t_router]
    sp = SP.eng

    def expert_id(n, row):
        if sp is None:
            return None
        return sp.value_load(eoi[0:1, 16 * row + n:16 * row + n + 1], min_val=0, max_val=31 if row == 0 else 1)
    gat = [None] * NB
    bfree = {"xg": [None] * 3, "xb": [None] * 2, "hd": [None] * 2, "hT": [None] * 2, "sg": [None] * 2,
             "yo": [None] * 3}
    gch = [chan(f"d_g{i}") for i in range(3)]
    ych = [chan(f"d_y{i}") for i in range(3)]
    ystore = []
    blk_ = {}

    def gather(n):
        i = n % 3
        gat[n] = G.dma(gch[i], lambda e: e.indirect_dma_start(
            XG[:, i, :], None, HN, bass.IndirectOffsetOnAxis(ap=idx[:, n:n + 1].bitcast(mybir.dt.uint32), axis=0)),
            t_idx, hn_store, bfree["xg"][i])

    def weights(n):
        s, d = wring.take(), dring.take()
        gu = s.ap.rearrange("p (k n) -> p k n", k=8)
        dn = d.ap.rearrange("p a b -> p (a b)").rearrange("p (k n) -> p k n", k=8)
        if n < 32:
            tg_ = SP.dma(s.chan, lambda e: e.dma_start(gu, I["w_gu"][n]), s.free)
            td_ = SP.dma(d.chan, lambda e: e.dma_start(dn, I["w_dn"][n]), d.free)
        else:
            SP(None, t_eo)
            v = expert_id(n - 32, 0)
            tg_ = SP.dma(s.chan, lambda e: e.dma_start(
                gu, I["w_gu"][bass.ds(v, 1)].rearrange("o p k n -> (o p) k n")), s.free)
            td_ = SP.dma(d.chan, lambda e: e.dma_start(
                dn, I["w_dn"][bass.ds(v, 1)].rearrange("o p k n -> (o p) k n")), d.free)
        blk_[n] = (s, d, gu, d.ap.rearrange("p f n -> p (f n)").rearrange("p (f n) -> p f n", f=2), tg_, td_)

    turned = {}

    def turn(n):
        x_, i = xb[n % 2], n % 2
        src = XG[:, n % 3, :]
        outs = []
        for half in range(2):
            b = rb.take()
            tr = PE(transposes([(b.ap[:, j * 128:(j + 1) * 128], src[:, (half * 4 + j) * 128:(half * 4 + j + 1) * 128])
                                for j in range(4)], ident), gat[n], b.free)
            o = []
            for j in range(4):
                k = half * 4 + j
                s_ = b.ap[:, j * 128:(j + 1) * 128]
                if half == 0:
                    o = A(lambda e: e.activation(x_[:, k, :], s_, ACT.Identity, bias=MOD[:, 24 + k, 0:1],
                                                 scale=AF[:, k:k + 1]), tr, bfree["xb"][i])
                else:
                    o = V(lambda e: e.tensor_scalar(x_[:, k, :], s_, AF[:, k:k + 1], MOD[:, 24 + k, 0:1],
                                                    ALU.mult, ALU.add), tr, bfree["xb"][i])
            b.free = [o]
            outs.append(o)
        bfree["xg"][n % 3] = tr
        turned[n] = outs

    def up(n):
        s, d, gu, dn, tg_, td_ = blk_[n]
        x_, i = xb[n % 2], n % 2
        b = rb.take()
        m = PE(mm_group(b.ap, [(x_[:, k, :], gu[:, k, :]) for k in range(8)]), turned.pop(n), tg_, b.free)
        s.free = [m]
        bfree["xb"][i] = m
        a = recip_sig(sg[i], b.ap[:, 0:256], m, bfree["sg"][i])
        a = V(lambda e: e.tensor_tensor(sg[i], b.ap[:, 0:256], sg[i], ALU.mult), a)
        a = V(lambda e: e.tensor_tensor(hd[i], b.ap[:, 256:512], sg[i], ALU.mult), a, bfree["hd"][i])
        bfree["sg"][i] = a
        b.free = [a]
        blk_[n] += (a,)

    def down(n):
        s, d, gu, dn, tg_, td_, th = blk_[n]
        i = n % 2
        b = rb.take()
        tr = PE(transposes([(b.ap[:, f * 128:(f + 1) * 128], hd[i][:, f * 128:(f + 1) * 128]) for f in range(2)],
                           ident), th, b.free)
        bfree["hd"][i] = tr
        o = A(lambda e: e.activation(hT[i], b.ap[:, 0:256].rearrange("p (f t) -> p f t", f=2), ACT.Copy),
              tr, bfree["hT"][i])
        b.free = [o]
        y_ = yo[n % 3]
        outs = []
        for g in range(2):
            b = rb.take()
            gs = slice(g * 512, (g + 1) * 512)
            m = PE(mm_group(b.ap, [(hT[i][:, f, :], dn[:, f, gs]) for f in range(2)]), o, td_, b.free)
            if g == 0:
                c = A(lambda e: e.activation(y_[:, gs], b.ap, ACT.Copy), m, bfree["yo"][n % 3])
            else:
                c = V(lambda e: e.tensor_copy(y_[:, gs], b.ap), m, bfree["yo"][n % 3])
            b.free = [c]
            outs.append(c)
        d.free = [m]
        bfree["hT"][i] = m
        st_ = G.dma(ych[n % 3], lambda e: e.dma_start(YB[n * 128:(n + 1) * 128, :], y_), outs)
        bfree["yo"][n % 3] = st_
        ystore.append(st_)
    gather(0)
    gather(1)
    turn(0)
    for n in range(NB + 1):
        if n + 2 < NB:
            gather(n + 2)
        if n < NB:
            weights(n)
        if n + 1 < NB:
            turn(n + 1)
        if n < NB:
            up(n)
        if n:
            down(n - 1)
    barrier()
    Y2 = XG
    gg_ = []
    zch = [chan(f"d_z{i}") for i in range(8)]
    for t in range(NL_T):
        gg_.append(G.dma(zch[t], lambda e: e.indirect_dma_start(
            Yc[:, t, :], None, YB, bass.IndirectOffsetOnAxis(ap=desti[:, 0, t:t + 1].bitcast(mybir.dt.uint32), axis=0)),
            ystore[-3:]))
    fr = [None] * 3
    for t in range(NL_T):
        i = t % 3
        l2 = G.dma(gch[i], lambda e: e.indirect_dma_start(
            Y2[:, i, :], None, YB, bass.IndirectOffsetOnAxis(ap=desti[:, 1, t:t + 1].bitcast(mybir.dt.uint32), axis=0)),
            ystore[-3:], fr[i])
        a = V(lambda e: e.tensor_scalar(Yc[:, t, :], Yc[:, t, :], w12[:, 0, t:t + 1], None, ALU.mult), gg_[t])
        fr[i] = V(lambda e: e.scalar_tensor_tensor(Yc[:, t, :], Y2[:, i, :], w12[:, 1, t:t + 1], Yc[:, t, :],
                                                   ALU.mult, ALU.add), a, l2)
    barrier()
    at[0] = ret_work
    gtr = alloc(1024)
    nfr = alloc(1024)
    sq = alloc(1024)
    ss = alloc(NL_T)
    bar = [q.last() for q in (PE, V, A, G)]
    t_nf = load(nfr, I["norm_final"].partition_broadcast(128), bar)
    tgr = row_broadcast(gtr, MOD[:, 40:48, 0], 8)
    ssl = []
    for t in range(NL_T):
        a = V(lambda e: e.tensor_tensor(Yc[:, t, :], Yc[:, t, :], gtr, ALU.mult), tgr)
        a = G(lambda e: e.tensor_tensor(Yc[:, t, :], Yc[:, t, :], XO[:, t, :], ALU.add), a)
        ssl = [A(lambda e: e.activation(sq, Yc[:, t, :], ACT.Square, accum_out=ss[:, t:t + 1]), a, ssl)]
    r = rstd_of(ss, ss, 1.0 / 1024, ssl)
    fin = []
    for t in range(NL_T):
        a = V(lambda e: e.scalar_tensor_tensor(Yc[:, t, :], Yc[:, t, :], ss[:, t:t + 1], nfr, ALU.mult, ALU.mult),
              r, t_nf)
        fin.append(SP.dma(ch_x[t], lambda e: e.dma_start(out[t * 128:(t + 1) * 128, :], Yc[:, t, :]), a))
    SP(None, fin)


def second_inputs(r, x):
    r["c2"] = np.stack([_cols(x["c_2"][0]), _cols(x["c_ctx_2"])], 2)
    r["w_ada2"] = _groups(x["w_ada_2"][0], [np.arange(i * 512, (i + 1) * 512) for i in range(12)])
    r["b_ada2"] = _cols(x["b_ada_2"][0])
    r["norm_mix"], r["norm_ffn"] = _cols(x["norm_mix_2"][0]), _cols(x["norm_ffn_2"][0])
    r["norm_final"], r["gla_norm"] = x["norm_final_2"], x["gla_norm_2"][0]
    w = x["w_in_2"][0]
    o = np.cumsum([0, 512, 512, 1024, 1024, 16, 16, 512, 512, 1024, 1024, 1024, 1024])
    part = [np.arange(o[i], o[i + 1]) for i in range(12)]
    gq, gk, gv, gg, lf, lb, rq, rk, rv, rg, mg, mr = part
    q, v = [slice(h * 128, (h + 1) * 128) for h in range(4)], [slice(h * 256, (h + 1) * 256) for h in range(4)]
    r["w_gla"] = _groups(w, [np.concatenate([gq[q[h]], gk[q[h]], gv[v[h]]]) for h in range(4)])
    r["w_gg"] = _groups(w, [gg[v[h]] for h in range(4)])
    r["w_ret"] = _groups(w, [np.concatenate([rq[q[h]], rk[q[h]], rv[v[h]]]) for h in range(4)])
    r["w_rg"] = _groups(w, [rg[v[h]] for h in range(4)])
    r["w_lr"] = _groups(w, [np.concatenate([lf, lb])])[0]
    halves = [np.arange(512), np.arange(512, 1024)]
    r["w_bg_m"], r["w_br_m"] = _groups(w, [mg[i] for i in halves]), _groups(w, [mr[i] for i in halves])
    r["w_bg"], r["w_br"] = _groups(x["w_branch_gla_2"][0], halves), _groups(x["w_branch_ret_2"][0], halves)
    r["w_out2"] = _groups(x["w_out_2"][0], halves)
    lr = x["gla_lr_w_2"][0]
    g = np.zeros((4, 32, 2, 128), np.float32)
    for h in range(4):
        for d in range(2):
            g[h, 16 * d:16 * d + 16, d, :] = lr[d][:, q[h]]
    r["gla_lr"] = [g[h] for h in range(4)]
    b = x["gla_lr_b_2"][0].reshape(2, 4, 128)
    r["lr_b"] = b.reshape(8, 128).T
    r["w_router"] = _groups(np.concatenate([x["w_router_group_2"][0], x["w_router_expert_2"][0]], 1), [np.arange(36)])[0]
    r["b_router"] = np.concatenate([x["b_router_group_2"][0], x["b_router_expert_2"][0]])
    r["k_rev"] = np.broadcast_to(np.concatenate([4.0 - np.arange(4), 32.0 - np.arange(32)]).astype(np.float32)[None], (128, 36))
    wg, wu, wd = x["w_expert_gate_2"][0], x["w_expert_up_2"][0], x["w_expert_down_2"][0]
    gu = np.concatenate([wg, wu], 2).reshape(32, 8, 128, 512).transpose(0, 2, 1, 3)
    dn = wd.reshape(32, 2, 128, 1024).transpose(0, 2, 1, 3)
    r["w_gu"] = gu.reshape(32, 128, 8, 512)
    r["w_dn"] = dn.reshape(32, 128, 8, 256)
    return r


def _constants():
    r = {}
    i = np.arange(128)
    r["k_ident"] = np.eye(128, dtype=np.float32)
    sel = np.zeros((4, 4, 128), np.float32)
    for h in range(4):
        sel[h, h] = 1.0
    r["k_sel4"] = sel
    b = np.zeros((4, 128), np.float32)
    for h in range(4):
        b[h, (h % 2) * 64:(h % 2) * 64 + 64] = 1.0
    r["k_bsel"] = b
    s, t = i[:, None], i[None, :]
    neg = np.stack([np.where(s <= t, 0.0, -1e30), np.where(s >= t, 0.0, -1e30)]).astype(np.float32)
    r["k_mneg"] = np.tile(neg, (1, 1, 4))
    rst = np.ones((128, T), np.float32)
    rst[:, ::128] = 0.0
    r["k_rst"] = rst
    tok = np.arange(1024)
    row, col = (tok // 64).astype(np.float32), (tok % 64).astype(np.float32)
    f = (np.float32(10000.0) ** (-np.arange(16, dtype=np.float32) / np.float32(16))).astype(np.float32)
    tab = np.zeros((1024, 128), np.float32)
    for n, p in enumerate((row, col)):
        ang = (p[:, None] * f).astype(np.float32)
        c, sn = np.cos(ang), np.sin(ang)
        tab[:, n * 32:n * 32 + 16] = c
        tab[:, n * 32 + 16:n * 32 + 32] = c
        tab[:, 64 + n * 32:64 + n * 32 + 16] = -sn
        tab[:, 64 + n * 32 + 16:64 + n * 32 + 32] = sn
    r["k_rope1"] = tab.reshape(8, 128, 128).transpose(1, 0, 2)
    f = (np.float32(10000.0) ** (-np.arange(32, dtype=np.float32) / np.float32(32))).astype(np.float32)
    tab = np.zeros((1024, 256), np.float32)
    for n, p in enumerate((row, col)):
        ang = (p[:, None] * f).astype(np.float32)
        c, sn = np.cos(ang), np.sin(ang)
        tab[:, n * 64:n * 64 + 32] = c
        tab[:, n * 64 + 32:n * 64 + 64] = c
        tab[:, 128 + n * 64:128 + n * 64 + 32] = -sn
        tab[:, 128 + n * 64 + 32:128 + n * 64 + 64] = sn
    r["k_rope2"] = tab.reshape(8, 128, 256).transpose(1, 0, 2)
    h = np.arange(4, dtype=np.float64)
    lf, lb = np.log1p(-np.exp2(-5.0 - h)), np.log1p(-np.exp2(-5.5 - h))
    s3, t3 = s[None].astype(np.float64), t[None].astype(np.float64)
    dm = np.where(t3 >= s3, np.exp((t3 - s3) * lf[:, None, None]), np.exp((s3 - t3) * lb[:, None, None]))
    r["k_rdm"] = dm.transpose(1, 0, 2).astype(np.float32)
    qd = np.stack([np.exp((i[None] + 1.0) * lf[:, None]), np.exp((128.0 - i[None]) * lb[:, None])])
    r["k_rqd"] = np.broadcast_to(qd.reshape(1, 2, 4, 128), (128, 2, 4, 128)).astype(np.float32)
    kd = np.stack([np.exp((127.0 - i[:, None]) * lf[None]), np.exp(i[:, None] * lb[None])], 1)
    cd = np.broadcast_to(np.stack([np.exp(128 * lf), np.exp(128 * lb)])[None], (128, 2, 4))
    r["k_rkd"] = np.concatenate([kd.reshape(128, 8), cd.reshape(128, 8)], 1).astype(np.float32)
    m = np.zeros((128, 8, 128), np.float32)
    for n, L in enumerate(LEVELS):
        m[:, n, :] = (s // (2 * L) == t // (2 * L)) & (s // L != t // L)
    m[:, 7, :] = s == t
    r["k_lmask"] = m
    r["k_iota"] = np.broadcast_to(np.arange(128, dtype=np.float32)[None], (128, 128))
    r["k_tri"] = np.where(s < t, 1.0, 0.0)
    r["k_tokid"] = np.arange(1024, dtype=np.float32).reshape(8, 128).T
    return {k: np.ascontiguousarray(v, dtype=np.float32) for k, v in r.items()}


def _groups(w, cols):
    return [np.ascontiguousarray(w[:, c].reshape(8, 128, len(c)).transpose(1, 0, 2)) for c in cols]


def _cols(v):
    return np.ascontiguousarray(v.reshape(-1, 128).T)


def _inputs(x):
    r = dict(_constants())
    x = {k: np.asarray(v) for k, v in x.items()}
    r["x"], r["ctx"], r["ctx2"] = x["x"][0], x["ctx"][0], x["ctx_2"][0]
    r["c"] = np.stack([_cols(x["c"][0]), _cols(x["c_ctx"])], 2)
    r["g_final"] = x["g_final"]
    lists = {n: [] for n in ("w_ada", "b_ada", "g_norm", "w_s", "b_s", "g_q", "g_k", "b_gates", "g_head", "w_out")}
    w_in = [[] for _ in W1]
    o = np.cumsum([0, 256, 256, 256, 512, 128, 128, 512, 256, 256, 256, 256, 256, 16])
    au, av, az, bq, bk, bv, bz, cq, ck, cv, co, cz, cg = [np.arange(o[i], o[i + 1]) for i in range(13)]
    cgp = cg.reshape(4, 4)[[0, 2, 1, 3]].ravel()
    cols = [[av, au], [az, bk, bv], [bq], [bz], [ck, cv], [co, cz], [cq, cgp]]
    cols = [np.concatenate(c) for c in cols]
    sp = [np.arange(i * 512, (i + 1) * 512) for i in range(12)]
    for l in range(2):
        lists["w_ada"].append(_groups(x["w_ada"][l], sp[:6]))
        lists["b_ada"].append(_cols(x["b_ada"][l]))
        lists["g_norm"].append(_cols(x["g_norm"][l]))
        lists["w_s"].append(x["w_s"][l].transpose(2, 0, 1))
        lists["b_s"].append(x["b_s"][l].T)
        lists["g_q"].append(x["g_q"][l])
        lists["g_k"].append(x["g_k"][l])
        lists["b_gates"].append(x["b_gates"][l].reshape(4, 4)[[0, 2, 1, 3]].T)
        lists["g_head"].append(x["g_head"][l])
        lists["w_out"].append(_groups(x["w_out"][l], sp[:2]))
        for g, a in enumerate(_groups(x["w_in"][l], cols)):
            w_in[g].append(a)
    r.update(lists)
    r["w_in"] = w_in
    return second_inputs(r, x)


def _flat(r):
    out = {}
    for k, v in r.items():
        if isinstance(v, list):
            out.update(_flat({f"{k}_{i}": a for i, a in enumerate(v)}))
        else:
            out[k] = np.ascontiguousarray(v)
    return out


def _named(r, nc, prefix=""):
    out = {}
    for k, v in (r.items() if isinstance(r, dict) else enumerate(r)):
        name = f"{prefix}{k}"
        if isinstance(v, (dict, list)):
            out[k] = _named(v, nc, name + "_")
        else:
            v = np.asarray(v)
            out[k] = nc.dram_tensor(name, v.shape, mybir.dt.from_np(v.dtype), kind="ExternalInput").ap()
    return out if isinstance(r, dict) else [out[i] for i in range(len(r))]


def kernel(**inputs):
    import concourse.bacc as _bacc
    from concourse.bass_utils import run_bass_kernel_spmd as _run

    laid = _inputs(inputs)
    nc = _bacc.Bacc("TRN2", target_bir_lowering=False, num_devices=1)
    out = nc.dram_tensor("out_dram", (1024, 1024), F32, kind="ExternalOutput").ap()
    program(nc, _named(laid, nc), out)
    r = _run(nc, [_flat(laid)], core_ids=[0])
    return r.results[0]["out_dram"].reshape(1, 1024, 1024)
```
